# Optimizing a Trainium2 kernel written in Bass

```python
import jax, jax.numpy as jnp
from jax import lax
import numpy as np

D_MODEL = 2048
BATCH = 1
SEQ = 256
DEPTH = 1
DEC_BATCH = 8
DEC_SEQ = 8
PAST_LEN = 2048
PAGE_SIZE = 128

HEAD_DIM = 128
POOL_WINDOWS = (2, 4, 8, 16)
N_POOL_GROUPS = len(POOL_WINDOWS)
POOL_WIDTH = D_MODEL // 4
POOL_GROUP_DIM = POOL_WIDTH // N_POOL_GROUPS
POOL_HIST = max(POOL_WINDOWS) - 1
CONV_WIDTH = 3 * D_MODEL // 8
N_CONV_HEADS = CONV_WIDTH // HEAD_DIM
SHORT_CONV = 3
SGU_WIDTH = 3 * D_MODEL // 8
N_SGU_HEADS = SGU_WIDTH // HEAD_DIM
SGU_HEAD_DIM = HEAD_DIM
CHUNK = 128
MIX_WIDTH = POOL_WIDTH + CONV_WIDTH + SGU_WIDTH
IN_WIDTH = POOL_WIDTH + 3 * CONV_WIDTH + 2 * SGU_WIDTH
D_FF = 11 * D_MODEL // 4
FFN_CONV = 3
EPS = 1e-6

kernel_name = "hybrid_pool_shortconv_chunkgmlp_decoder_step"

def rmsnorm(x, g):
    xf = x.astype(jnp.float32)
    y = xf * lax.rsqrt(jnp.mean(xf * xf, axis=-1, keepdims=True) + EPS)
    return (y * g.astype(jnp.float32)).astype(x.dtype)

def causal_conv(z, prev, w):
    k = w.shape[0]
    t = z.shape[1]
    zz = jnp.concatenate([prev, z], axis=1)
    y = sum(w[i] * zz[:, i:i + t] for i in range(k))
    return y, zz[:, -(k - 1):]

def pool_mixer(xa, prev, start, pool_w, pool_scale):
    b, t, p = xa.shape
    zz = jnp.concatenate([prev, xa], axis=1)
    cs = jnp.concatenate([jnp.zeros((b, 1, p), jnp.float32),
                          jnp.cumsum(zz.astype(jnp.float32), axis=1)], axis=1)
    pos = start + jnp.arange(t)
    lo = POOL_HIST + 1
    outs = []
    for g, w in enumerate(POOL_WINDOWS):
        sl = slice(g * POOL_GROUP_DIM, (g + 1) * POOL_GROUP_DIM)
        s = cs[:, lo:lo + t, sl] - cs[:, lo - w:lo - w + t, sl]
        cnt = jnp.minimum(w, pos + 1).astype(jnp.float32)
        outs.append(s / cnt[None, :, None])
    pooled = jnp.stack(outs, axis=2)
    pooled = pooled - xa.astype(jnp.float32).reshape(b, t, N_POOL_GROUPS, POOL_GROUP_DIM)
    y = jnp.einsum('btgc,gcd->btgd', pooled.astype(xa.dtype), pool_w).reshape(b, t, p)
    return y * pool_scale, zz[:, -POOL_HIST:]

def short_conv_mixer(h, bg, cg, prev, conv_w):
    y, new = causal_conv(cg * h, prev, conv_w)
    return bg * y, new

def sgu_mixer(u, v, sgu_norm, sgu_w, sgu_b):
    b, t, s = v.shape
    v = rmsnorm(v, sgu_norm)
    n_chunks = -(-t // CHUNK)
    pad = n_chunks * CHUNK - t
    vp = jnp.pad(v, ((0, 0), (0, pad), (0, 0))).reshape(b, n_chunks, CHUNK, N_SGU_HEADS, SGU_HEAD_DIM)
    mask = jnp.tril(jnp.ones((CHUNK, CHUNK), dtype=bool))
    ws = jnp.where(mask[None], sgu_w, jnp.zeros_like(sgu_w))
    g = jnp.einsum('hqs,bnshd->bnqhd', ws, vp) + sgu_b.T[None, None, :, :, None]
    g = g.reshape(b, n_chunks * CHUNK, s)[:, :t]
    return u * g, v

def conv_ffn(x, prev, up, cw, cb, down):
    a = x @ up
    gate, val = jnp.split(a, 2, axis=-1)
    gc, new = causal_conv(gate, prev, cw)
    h = jax.nn.gelu(gc + cb, approximate=True) * val
    return h @ down, new

def block(x, pool_prev, conv_prev, ffn_prev, start, g_mix_pre, g_mix_post, g_ffn_pre, g_ffn_post,
          w_in, pool_w, pool_scale, conv_w, sgu_norm, sgu_w, sgu_b, w_out,
          ffn_up, ffn_conv_w, ffn_conv_b, ffn_down):
    h = rmsnorm(x, g_mix_pre)
    p = h @ w_in
    o1 = POOL_WIDTH
    o2 = o1 + CONV_WIDTH
    o3 = o2 + CONV_WIDTH
    o4 = o3 + CONV_WIDTH
    o5 = o4 + SGU_WIDTH
    ya, new_pool = pool_mixer(p[..., :o1], pool_prev, start, pool_w, pool_scale)
    yb, new_conv = short_conv_mixer(p[..., o1:o2], p[..., o2:o3], p[..., o3:o4], conv_prev, conv_w)
    yc, v_rows = sgu_mixer(p[..., o4:o5], p[..., o5:], sgu_norm, sgu_w, sgu_b)
    mix = jnp.concatenate([ya, yb, yc], axis=-1) @ w_out
    x = x + rmsnorm(mix, g_mix_post)
    f, new_ffn = conv_ffn(rmsnorm(x, g_ffn_pre), ffn_prev, ffn_up, ffn_conv_w, ffn_conv_b, ffn_down)
    x = x + rmsnorm(f, g_ffn_post)
    return x, new_pool, new_conv, new_ffn, v_rows

def setup_inputs(seed: int = 0) -> dict:
    key = jax.random.key(seed)
    ks = jax.random.split(key, 24)
    f32 = jnp.float32
    nrm = lambda k, shape, scale: (jax.random.normal(k, shape, f32) * scale)
    gain = lambda k, shape: 1.0 + 0.05 * jax.random.normal(k, shape, f32)
    return {
        "x_prompt": nrm(ks[0], (BATCH, SEQ, D_MODEL), 1.0),
        "x_sample": nrm(ks[1], (DEC_BATCH, DEC_SEQ, D_MODEL), 1.0),
        "state_pool": nrm(ks[2], (DEPTH, DEC_BATCH, POOL_HIST, POOL_WIDTH), 1.0),
        "state_conv": nrm(ks[3], (DEPTH, DEC_BATCH, SHORT_CONV - 1, CONV_WIDTH), 1.0),
        "state_ffn": nrm(ks[4], (DEPTH, DEC_BATCH, FFN_CONV - 1, D_FF), 1.0),
        "g_mix_pre": gain(ks[5], (DEPTH, D_MODEL)),
        "g_mix_post": gain(ks[6], (DEPTH, D_MODEL)),
        "g_ffn_pre": gain(ks[7], (DEPTH, D_MODEL)),
        "g_ffn_post": gain(ks[8], (DEPTH, D_MODEL)),
        "w_in": nrm(ks[9], (DEPTH, D_MODEL, IN_WIDTH), D_MODEL ** -0.5),
        "pool_w": nrm(ks[10], (DEPTH, N_POOL_GROUPS, POOL_GROUP_DIM, POOL_GROUP_DIM), POOL_GROUP_DIM ** -0.5),
        "pool_scale": gain(ks[11], (DEPTH, POOL_WIDTH)),
        "conv_w": nrm(ks[12], (DEPTH, SHORT_CONV, CONV_WIDTH), SHORT_CONV ** -0.5),
        "sgu_norm": gain(ks[13], (DEPTH, SGU_WIDTH)),
        "sgu_w": nrm(ks[14], (DEPTH, N_SGU_HEADS, CHUNK, CHUNK), CHUNK ** -0.5),
        "sgu_b": gain(ks[15], (DEPTH, N_SGU_HEADS, CHUNK)),
        "w_out": nrm(ks[16], (DEPTH, MIX_WIDTH, D_MODEL), MIX_WIDTH ** -0.5),
        "ffn_up": nrm(ks[17], (DEPTH, D_MODEL, 2 * D_FF), D_MODEL ** -0.5),
        "ffn_conv_w": nrm(ks[18], (DEPTH, FFN_CONV, D_FF), FFN_CONV ** -0.5),
        "ffn_conv_b": nrm(ks[19], (DEPTH, D_FF), 0.02),
        "ffn_down": nrm(ks[20], (DEPTH, D_FF, D_MODEL), D_FF ** -0.5),
    }

def reference(x_prompt, x_sample, state_pool, state_conv, state_ffn,
              g_mix_pre, g_mix_post, g_ffn_pre, g_ffn_post, w_in, pool_w, pool_scale,
              conv_w, sgu_norm, sgu_w, sgu_b, w_out, ffn_up, ffn_conv_w, ffn_conv_b, ffn_down):
    bp = x_prompt.shape[0]
    dt = x_prompt.dtype
    zero_pool = jnp.zeros((bp, POOL_HIST, POOL_WIDTH), dt)
    zero_conv = jnp.zeros((bp, SHORT_CONV - 1, CONV_WIDTH), dt)
    zero_ffn = jnp.zeros((bp, FFN_CONV - 1, D_FF), dt)
    hp = x_prompt
    hs = x_sample
    pool_p, pool_s, conv_p, conv_s, ffn_p, ffn_s, v_s = [], [], [], [], [], [], []
    for l in range(DEPTH):
        w = (g_mix_pre[l], g_mix_post[l], g_ffn_pre[l], g_ffn_post[l], w_in[l], pool_w[l], pool_scale[l],
             conv_w[l], sgu_norm[l], sgu_w[l], sgu_b[l], w_out[l], ffn_up[l], ffn_conv_w[l],
             ffn_conv_b[l], ffn_down[l])
        hp, np_, nc_, nf_, _ = block(hp, zero_pool, zero_conv, zero_ffn, 0, *w)
        hs, ns_, ncs_, nfs_, vs_ = block(hs, state_pool[l], state_conv[l], state_ffn[l], PAST_LEN, *w)
        pool_p.append(np_)
        conv_p.append(nc_)
        ffn_p.append(nf_)
        pool_s.append(ns_)
        conv_s.append(ncs_)
        ffn_s.append(nfs_)
        v_s.append(vs_)
    return (hp, hs, jnp.stack(pool_p), jnp.stack(pool_s), jnp.stack(conv_p), jnp.stack(conv_s),
            jnp.stack(ffn_p), jnp.stack(ffn_s), jnp.stack(v_s))


_drawn_inputs = setup_inputs


def setup_inputs(seed=0):
    import zlib

    import numpy as np

    out = dict(_drawn_inputs(seed))
    spreads = {}
    factors = {'pool_scale': 3.035, 'ffn_conv_b': 4.976, 'sgu_b': 2.771}
    for name, (base, spread) in spreads.items():
        noise = np.random.default_rng([zlib.crc32(name.encode()), seed]).standard_normal(out[name].shape)
        drawn = base * np.exp(spread * noise) if base else spread * noise
        out[name] = __import__('jax').numpy.asarray(drawn.astype(out[name].dtype))
    for name, factor in factors.items():
        out[name] = (out[name] * factor).astype(out[name].dtype)
    return out
```

```python
from contextlib import ExitStack

import concourse.bass as bass
from concourse import mybir

F32 = mybir.dt.float32
F32R = mybir.dt.float32r
ACT = mybir.ActivationFunctionType
ALU = mybir.AluOpType

P = 128
EPS = 1e-6
WINDOWS = (2, 4, 8, 16)


def hybrid_layer(nc, x_prompt, x_sample, state_pool, state_conv, state_ffn, g_mix_pre, g_mix_post,
                 g_ffn_pre, g_ffn_post, w_in, pool_w, pool_scale, conv_w, sgu_norm, sgu_w, sgu_b,
                 w_out, ffn_up, ffn_conv_w, ffn_conv_b, ffn_down,
                 y_prompt, y_sample, new_pool_prompt, new_pool_sample, new_conv_prompt,
                 new_conv_sample, new_ffn_prompt, new_ffn_sample, new_chunk_v):
    SEQ, D = x_prompt.shape[1:]
    NB, TB = x_sample.shape[:2]
    TS = NB * TB
    T = SEQ + TS
    KD = D // P
    NPOOL = len(WINDOWS)
    NCONV = conv_w.shape[2] // P
    NSGU = sgu_norm.shape[1] // P
    NF = ffn_conv_b.shape[1] // P
    PH = state_pool.shape[2]
    CH = state_conv.shape[2]
    GROUPS = 4
    NG = NF // GROUPS
    TT = [(0, P), (P, P), (2 * P, TS)]
    assert SEQ == 2 * P and D == 16 * P and TS == 64 and NG * GROUPS == NF and NF % 2 == 0

    POOL0, H0 = 0, NPOOL
    BG0 = H0 + NCONV
    CG0 = BG0 + NCONV
    U0 = CG0 + NCONV
    M_CONV, M_SGU = NPOOL, NPOOL + NCONV
    READY = [0, M_SGU, M_SGU + 1, M_SGU + 2, 1, M_SGU + 3, M_SGU + 4, M_SGU + 5, 2, 3] + \
            [M_CONV + j for j in range(NCONV)]

    C_V = NSGU
    C_POOL = 2 * NSGU
    C_CONV = C_POOL + NPOOL
    C_OUT = C_CONV + 3 * NCONV
    C_FFN = C_OUT + KD
    PER_GROUP = 2 * NG + KD
    CHUNKS = C_FFN + GROUPS * PER_GROUP

    LP = PH + SEQ
    WP = PH + TB
    ZP = LP + NB * WP
    LC = CH + SEQ
    WC = CH + TB
    ZC = LC + NB * WC
    YC = ZC - CH

    CHUNK_B, TILE_B = KD * P * 4, T * 4
    at = {}
    top = [(nc.sbuf_base + 31) // 32 * 32]

    def region(name, size):
        at[name] = top[0]
        top[0] += (size + 31) // 32 * 32

    for name, size in (("raw", 4 * CHUNK_B), ("w_hi", 2 * CHUNK_B), ("w_lo", 2 * CHUNK_B),
                       ("xT", KD * TILE_B), ("a_hi", KD * TILE_B), ("a_lo", KD * TILE_B),
                       ("m_hi", KD * TILE_B), ("m_lo", KD * TILE_B), ("f", KD * TILE_B),
                       ("ident", 512), ("ones", 512), ("vec", 4 * 268), ("r_x", TILE_B),
                       ("r_v", TILE_B), ("acc", TILE_B), ("sq", TILE_B), ("eps", 32),
                       ("ffn_hist", 4 * NF * NB * CH), ("ffn_tail_s", 4 * NF * NB * CH),
                       ("ffn_tail_p", 4 * NF * CH), ("ws", 4 * NSGU * P), ("bd", 4 * NSGU * TS),
                       ("pool_w", 4 * NPOOL * P), ("pool_hist", 4 * NPOOL * NB * PH),
                       ("conv_hist", 4 * NCONV * NB * CH), ("pool_tail_p", 4 * NPOOL * PH),
                       ("pool_tail_s", 4 * NPOOL * TS), ("conv_tail_p", 4 * NCONV * CH),
                       ("conv_tail_s", 4 * NCONV * NB * CH), ("icnt", 4 * NPOOL * 16)):
        region(name, size)
    assert top[0] <= nc.sbuf_usable_end, top[0]

    def sb(name, shape, dt=F32, where=None, plus=0):
        return nc.alloc_sbuf_tensor_at(name, shape, dt, offset=at[where or name] + plus)

    raw = sb("raw", [P, 4 * KD * P])
    w_hi = sb("w_hi", [P, 2 * KD * P], F32R)
    w_lo = sb("w_lo", [P, 2 * KD * P], F32R)
    xT = sb("xT", [P, KD * T])
    a_hi = sb("a_hi", [P, KD * T], F32R)
    a_lo = sb("a_lo", [P, KD * T], F32R)
    m_hi = sb("m_hi", [P, KD * T], F32R)
    m_lo = sb("m_lo", [P, KD * T], F32R)
    f = sb("f", [P, KD * T])
    ident = sb("ident", [P, P])
    ones = sb("ones", [P, P])
    vec = sb("vec", [P, 268])
    r_x = sb("r_x", [P, T])
    r_v = sb("r_v", [P, T])
    acc = sb("acc", [P, T])
    sq = sb("sq", [P, T])
    eps = sb("eps", [P, 1])
    ffn_hist = sb("ffn_hist", [P, NF * NB * CH])
    ffn_tail_s = sb("ffn_tail_s", [P, NF * NB * CH])
    ffn_tail_p = sb("ffn_tail_p", [P, NF * CH])
    ws = sb("ws", [P, NSGU, P])
    bd = sb("bd", [TS, NSGU, NB, TB])
    pool_w_sb = sb("pool_w", [P, NPOOL, P])
    pool_hist = sb("pool_hist", [P, NPOOL, NB, PH])
    conv_hist = sb("conv_hist", [P, NCONV * NB * CH])
    pool_tail_p = sb("pool_tail_p", [P, NPOOL * PH])
    pool_tail_s = sb("pool_tail_s", [P, NPOOL * TS])
    conv_tail_p = sb("conv_tail_p", [P, NCONV * CH])
    conv_tail_s = sb("conv_tail_s", [P, NCONV * NB * CH])
    icnt = sb("icnt", [P, NPOOL, 16])
    sel = sb("sel", [TB, TS], where="conv_tail_s")

    x_tok = sb("x_tok", [P, 3, D], where="m_hi")
    sgu_raw = sb("sgu_raw", [P, NSGU, P], where="m_lo", plus=11264)
    ffn_raw = sb("ffn_raw", [P, 6, P], where="m_lo", plus=11264 + 3072)
    vec_raw = sb("vec_raw", [P, 3, P], where="f", plus=12 * TILE_B)
    pool_raw = sb("pool_raw", [NB * PH, NPOOL, P], where="f", plus=12 * TILE_B + 1536)
    conv_raw = sb("conv_raw", [NCONV * NB * CH, P], where="f", plus=12 * TILE_B + 3584)
    zz = sb("zz", [P, ZP], where="m_hi", plus=4 * TILE_B)
    win = [sb(f"win{i}", [P, ZP], where="m_hi", plus=4 * TILE_B + (i + 1) * 1824) for i in range(2)]
    v_tok = sb("v_tok", [P, 2, 2 * P], where="m_hi", plus=4 * TILE_B + 3 * 1824)
    sgu_bias = sb("sgu_bias", [P, NSGU, P], where="m_lo", plus=4 * TILE_B)
    vs_tok = sb("vs_tok", [TS, NSGU * P], where="m_lo", plus=8192)
    pooled = sb("pooled", [P, T], where="m_lo", plus=9 * TILE_B)
    hs = sb("hs", [P, T], where="f", plus=12 * TILE_B)
    zc = sb("zc", [P, ZC], where="f", plus=13 * TILE_B)
    yc = sb("yc", [P, ZC], where="f", plus=13 * TILE_B + 1376)
    uT, vT = f, f
    state_out = sb("state_out", [P, 5, P], where="ws")
    zf = sb("zf", [P, ZC], where="m_hi", plus=NG * TILE_B)
    yf = sb("yf", [P, ZC], where="m_hi", plus=NG * TILE_B + 1376)
    gel = sb("gel", [P, T], where="m_lo", plus=NG * TILE_B)
    val = sb("val", [P, T], where="m_lo", plus=(NG + 1) * TILE_B)
    y_tok = sb("y_tok", [P, 3, D], where="a_hi")
    ffn_out = sb("ffn_out", [P, 7, P], where="a_lo", plus=8192)

    with ExitStack() as ctx:
        def sem(name):
            return ctx.enter_context(nc.semaphore(name))

        mm = [ctx.enter_context(nc.psum_tensor(f"mm{i}", [P, 512], F32)) for i in range(2)]
        tb = [ctx.enter_context(nc.psum_tensor(f"tb{i}", [P, 512], F32)) for i in range(6)]
        mp = [m[:, 0:SEQ] for m in mm]
        ms = [m[:, SEQ:T].rearrange("p (b t) -> p b t", b=NB) for m in mm]

        landed = [sem(f"landed{i}") for i in range(2)]
        w_hi_done = sem("w_hi_done")
        w_lo_done = sem("w_lo_done")
        used = sem("used")
        drained = [sem(f"drained{i}") for i in range(2)]
        x_in = sem("x_in")
        staged = sem("staged")
        consts = sem("consts")
        vecs_t = sem("vecs_t")
        vecs_done = sem("vecs_done")
        tril_done = sem("tril_done")
        corner_mm = sem("corner_mm")
        sel_done = sem("sel_done")
        corner_done = sem("corner_done")
        bd_done = sem("bd_done")
        pads_done = sem("pads_done")
        x_turned = sem("x_turned")
        a_hi_done = sem("a_hi_done")
        x_copied = sem("x_copied")
        a_lo_done = sem("a_lo_done")
        summed = sem("summed")
        total = sem("total")
        rooted = sem("rooted")
        r_done = sem("r_done")
        v_evac = sem("v_evac")
        v_normed = sem("v_normed")
        v_turned = sem("v_turned")
        v_tok_done = sem("v_tok_done")
        sgu_mm = sem("sgu_mm")
        dstep = sem("dstep")
        mix_ready = sem("mix_ready")
        m_hi_done = sem("m_hi_done")
        m_lo_done = sem("m_lo_done")
        zz_free = sem("zz_free")
        pooled_done = sem("pooled_done")
        pool_mm = sem("pool_mm")
        zc_free = sem("zc_free")
        states_t = sem("states_t")
        states_done = sem("states_done")
        out_squared = sem("out_squared")
        f_scaled = sem("f_scaled")
        x1_done = sem("x1_done")
        f_zeroed = sem("f_zeroed")
        zf_filled = sem("zf_filled")
        zf_free = sem("zf_free")
        conv_done = sem("conv_done")
        gelu_done = sem("gelu_done")
        h_ready = sem("h_ready")
        h_hi_done = sem("h_hi_done")
        h_lo_done = sem("h_lo_done")
        f_gained = sem("f_gained")
        ffn_t = sem("ffn_t")
        ffn_t_done = sem("ffn_t_done")
        y_ready = sem("y_ready")
        y_turned = sem("y_turned")
        y_done = [sem("y_done_a"), sem("y_done_v")]
        v_stored = sem("v_stored")
        stored = sem("stored")

        SUMMED = [1, 2, 2 + KD, 2 + 2 * KD, 2 + 3 * KD]

        def tile(t, k, n=1):
            return t[:, k * T:(k + n) * T] if type(k) is int else t[:, bass.ds(k * T, n * T)]

        def col(k):
            return vec[:, k:k + 1] if type(k) is int else vec[:, bass.ds(k, 1)]

        def samples(t, start, width, lo, hi):
            return t[:, start:start + NB * width].rearrange("p (b w) -> p b w", b=NB)[:, :, lo:hi]

        V_MIX_PRE, V_MIX_POST, V_FFN_PRE, V_FFN_POST = 0, KD, 2 * KD, 3 * KD
        V_CONV = 4 * KD
        V_SGU = V_CONV + 3 * NCONV
        V_POOL = V_SGU + NSGU
        V_FCONV = V_POOL + NPOOL
        V_FBIAS = V_FCONV + 3 * NF
        N_VEC0 = V_FCONV
        N_VEC1 = 2 * NF

        def stage(q):
            rows = 0
            for v in (g_mix_pre, g_mix_post, g_ffn_pre, g_ffn_post, conv_w, sgu_norm, pool_scale):
                n = v.shape[-1] // P * (3 if v is conv_w else 1)
                src = v[0].rearrange("i (j c) -> (i j) c", c=P) if v is conv_w else \
                    v[0].rearrange("(j c) -> j c", c=P)
                yield q.dma_start(vec_raw[rows:rows + n, 0, :], src)
                rows += n
            fc = ffn_conv_w[0].rearrange("i (j c) -> (i j) c", c=P)
            yield q.dma_start(vec_raw[0:2 * NF, 1, :], fc[0:2 * NF, :])
            yield q.dma_start(vec_raw[0:NF, 2, :], fc[2 * NF:3 * NF, :])
            yield q.dma_start(vec_raw[NF:2 * NF, 2, :], ffn_conv_b[0].rearrange("(j c) -> j c", c=P))
            yield q.dma_start(pool_raw[:, :, :], state_pool[0].rearrange("b r (g c) -> (b r) g c", c=P))
            sc = state_conv[0].rearrange("b r (j c) -> (b r) j c", c=P)
            for j in range(NCONV):
                yield q.dma_start(conv_raw[16 * j:16 * j + 16, :], sc[:, j, :])
            yield q.dma_start(sgu_raw[:, :, :], sgu_w[0].rearrange("h q s -> q h s"))
            yield q.dma_start(pool_w_sb[:, :, :], pool_w[0].rearrange("g c d -> c g d"))
            yield q.dma_start(sgu_bias[:, :, :],
                              sgu_b.rearrange("a h q -> a (h q)").to_broadcast([P, NSGU * P]))
            sf = state_ffn[0].rearrange("b r (j c) -> (b r) j c", c=P)
            for j in range(NF):
                yield q.dma_start(ffn_raw[16 * (j % 8):16 * (j % 8) + 16, j // 8, :], sf[:, j, :])

        N_STAGED = 7 + 3 + 1 + NCONV + 3 + NF

        block = ctx.enter_context(nc.Block())

        @block.sync
        def _(sp):
            up = ffn_up[0].rearrange("(k p) n -> p k n", p=P)
            win_v = w_in[0].rearrange("(k p) n -> p k n", p=P)
            wout_v = w_out[0].rearrange("(k p) n -> p k n", p=P)
            down = ffn_down[0].rearrange("(k p) n -> p k n", p=P)

            def cols(view, b):
                return view[:, :, b * P:(b + 1) * P] if type(b) is int else view[:, :, bass.ds(b * P, P)]

            def load(q, e, src, blocks=KD):
                if type(q) is not int or q >= 1:
                    sp.wait_ge(w_hi_done, 4 * q + 2 * e - 3)
                off = (q % 2) * (2 * KD * P) + e * KD * P
                dst = raw[:, off:off + blocks * P] if type(q) is int else \
                    raw[:, bass.ds(off, blocks * P)]
                sp.dma_start(dst.rearrange("p (k c) -> p k c", c=P), src).then_inc(landed[e], 16)

            load(0, 0, cols(win_v, U0))
            xp = x_prompt[0].rearrange("(t p) d -> p t d", p=P)
            for t in range(2):
                sp.dma_start(x_tok[:, t, :], xp[:, t, :]).then_inc(x_in, 16)
            sp.dma_start(x_tok[0:TS, 2, :], x_sample.rearrange("b t d -> (b t) d")).then_inc(x_in, 16)
            load(0, 1, cols(win_v, U0 + 1))
            for e in range(2):
                load(1, e, cols(win_v, U0 + 2 + e))
            with sp.Fori(2, NSGU) as q:
                for e in range(2):
                    load(q, e, cols(win_v, U0 + 2 * q + e))
            for g in range(NPOOL):
                c = C_POOL + g
                load(c // 2, c % 2, cols(win_v, POOL0 + g))
            with sp.Fori(0, NCONV // 2) as i:
                for n in range(6):
                    load(C_CONV // 2 + 3 * i + n // 2, n % 2,
                         cols(win_v, (H0, CG0, BG0)[n % 3] + 2 * i + n // 3))
            with sp.Fori(0, KD // 2) as i:
                for e in range(2):
                    load(C_OUT // 2 + i, e, cols(wout_v, 2 * i + e))
            with sp.Fori(0, GROUPS) as g:
                with sp.Fori(0, NG) as i:
                    q = C_FFN // 2 + g * (PER_GROUP // 2) + i
                    load(q, 0, cols(up, g * NG + i))
                    load(q, 1, cols(up, NF + g * NG + i))
                with sp.Fori(0, KD // 2) as i:
                    q = C_FFN // 2 + g * (PER_GROUP // 2) + NG + i
                    for e in range(2):
                        load(q, e, down[:, bass.ds(g * NG, NG), bass.ds((2 * i + e) * P, P)], NG)

            y_stored = sem("y_stored")
            n = 0
            for k4 in range(KD // 4):
                cs = slice(k4 * 512, (k4 + 1) * 512)
                for i, (t0, nt) in enumerate(TT):
                    sp.wait_ge(y_done[n % 2], n // 2 + 1)
                    dst = y_prompt[0, t0:t0 + P, cs] if i < 2 else \
                        y_sample.rearrange("b t d -> (b t) d")[:, cs]
                    sp.dma_start(dst, y_tok[0:nt, i, cs]).then_inc(y_stored, 16)
                    n += 1
            sp.wait_ge(y_stored, 16 * n)

        @block.tensor
        def _(pe):
            def chunk(q, e, hi, lo, order, ready=None):
                pe.wait_ge(w_lo_done, 4 * q + 2 * e + 2)
                if type(q) is not int or q >= 1:
                    pe.wait_ge(drained[e], q)
                out = mm[e][:, 0:T]
                for n, k in enumerate(order):
                    if ready and ready(n) is not None:
                        pe.wait_ge(*ready(n))
                    s = slice((e * KD + k) * P, (e * KD + k + 1) * P)
                    pe.matmul(out, w_hi[:, s], tile(hi, k), start=(n == 0), stop=False)
                    pe.matmul(out, w_hi[:, s], tile(lo, k), start=False, stop=False)
                    last = pe.matmul(out, w_lo[:, s], tile(hi, k), start=False,
                                     stop=(n == len(order) - 1))
                last.then_inc(used, 1)

            def pair(q, hi, lo, order, ready=None):
                for e in range(2):
                    chunk(q, e, hi, lo, order, ready)

            def token_sums(n):
                pe.wait_ge(summed, SUMMED[n])
                if n:
                    pe.wait_ge(rooted, n)
                pe.matmul(tb[5][:, 0:T], ones[:, :], acc[:, :], start=True, stop=True).then_inc(total, 1)

            pe.wait_ge(consts, 1)
            pe.wait_ge(staged, 16 * N_STAGED)
            for i, (n, o) in enumerate(((N_VEC0, 0), (N_VEC1, N_VEC0), (N_VEC1, N_VEC0 + N_VEC1))):
                pe.transpose(tb[0][:, o:o + n], vec_raw[0:n, i, :], ident[0:n, 0:n])
            n = NB * PH
            for g in range(NPOOL):
                pe.transpose(tb[1][:, g * n:(g + 1) * n], pool_raw[:, g, :], ident[0:n, 0:n])
            n = NCONV * NB * CH
            pe.transpose(tb[2][:, 0:n], conv_raw[:, :], ident[0:n, 0:n])
            for j in range(NSGU):
                pe.transpose(tb[3 + j // 4][:, (j % 4) * P:(j % 4 + 1) * P], sgu_raw[:, j, :], ident[:, :])
            for j in range(6):
                n = P if j < 5 else 64
                o = tb[5][:, j * P:j * P + n] if j < 4 else tb[4][:, 256 + (j - 4) * P:256 + (j - 4) * P + n]
                last = pe.transpose(o, ffn_raw[0:n, j, :], ident[0:n, 0:n])
            last.then_inc(vecs_t, 1)

            pe.wait_ge(x_in, 48)
            pe.wait_ge(vecs_done, 1)
            for k in range(KD):
                if k >= 6:
                    pe.wait_ge(x_copied, k - 5)
                for i, (t0, n) in enumerate(TT):
                    last = pe.transpose(tb[k % 6][:, t0:t0 + n], x_tok[0:n, i, k * P:(k + 1) * P],
                                        ident[0:n, 0:n])
                last.then_inc(x_turned, 1)

            order = range(KD)
            chunk(0, 0, a_hi, a_lo, order, lambda n: (a_lo_done, n + 1))
            pe.wait_ge(tril_done, 1)
            pe.wait_ge(sel_done, 1)
            pe.matmul(tb[0][0:TS, 0:NSGU * TB], sel[:, :], ws[0:TB, :, 0:TB],
                      start=True, stop=True).then_inc(corner_mm, 1)
            chunk(0, 1, a_hi, a_lo, order)
            with pe.Fori(1, NSGU // 2) as q:
                pair(q, a_hi, a_lo, order)
            token_sums(0)
            with pe.Fori(C_V // 2, C_POOL // 2) as q:
                pair(q, a_hi, a_lo, order)

            def pool_map(g):
                pe.wait_ge(pooled_done, g + 1)
                if g:
                    pe.wait_ge(m_lo_done, READY.index(g - 1) + 1)
                pe.matmul(tb[4][:, 0:T], pool_w_sb[:, g, :], pooled[:, :], start=True,
                          stop=True).then_inc(pool_mm, 1)

            def turn_v(j):
                if j >= 2:
                    pe.wait_ge(v_tok_done, j - 1)
                for i, (t0, n) in enumerate(TT):
                    last = pe.transpose(tb[j % 2][0:n, i * P:(i + 1) * P],
                                        f[:, (NSGU + j) * T + t0:(NSGU + j) * T + t0 + n], ident[:, :])
                last.then_inc(v_turned, 1)

            def gate_v(j):
                pe.wait_ge(v_tok_done, j + 1)
                if j >= 2:
                    pe.wait_ge(mix_ready, j - 1)
                out = tb[2 + j % 2]
                for i in range(2):
                    pe.matmul(out[:, i * P:(i + 1) * P], v_tok[:, j % 2, i * P:(i + 1) * P],
                              ws[:, j, :], start=True, stop=True)
                pe.matmul(out[:, SEQ:T], vs_tok[:, j * P:(j + 1) * P],
                          bd[:, j, :, :].rearrange("s b q -> s (b q)"), start=True,
                          stop=True).then_inc(sgu_mm, 1)

            def gates(j0):
                turn_v(j0)
                turn_v(j0 + 1)
                gate_v(j0)
                turn_v(j0 + 2)
                gate_v(j0 + 1)
                gate_v(j0 + 2)

            chunk(C_POOL // 2, 0, a_hi, a_lo, order)
            token_sums(1)
            chunk(C_POOL // 2, 1, a_hi, a_lo, order)
            pool_map(0)
            chunk(C_POOL // 2 + 1, 0, a_hi, a_lo, order)
            pe.wait_ge(v_normed, NSGU)
            pe.wait_ge(bd_done, 1)
            gates(0)
            pool_map(1)
            chunk(C_POOL // 2 + 1, 1, a_hi, a_lo, order)
            gates(3)
            pool_map(2)
            chunk(C_CONV // 2, 0, a_hi, a_lo, order)
            pool_map(3)
            chunk(C_CONV // 2, 1, a_hi, a_lo, order)
            with pe.Fori(C_CONV // 2 + 1, C_OUT // 2) as q:
                pair(q, a_hi, a_lo, order)

            chunk(C_OUT // 2, 0, m_hi, m_lo, READY, lambda n: (m_lo_done, n + 1))
            pe.wait_ge(zz_free, NPOOL)
            pe.wait_ge(zc_free, NCONV + 1)
            pe.transpose(tb[0][0:NPOOL * PH, 0:P], pool_tail_p[:, :], ident[:, :])
            for i in range(2):
                pe.transpose(tb[0][:, (i + 1) * P:(i + 2) * P], pool_tail_s[:, i * P:(i + 1) * P], ident[:, :])
            pe.transpose(tb[0][0:NCONV * CH, 3 * P:4 * P], conv_tail_p[:, :], ident[:, :])
            pe.transpose(tb[1][0:NCONV * NB * CH, 0:P], conv_tail_s[:, :], ident[:, :]).then_inc(states_t, 1)
            chunk(C_OUT // 2, 1, m_hi, m_lo, READY)
            with pe.Fori(C_OUT // 2 + 1, C_FFN // 2) as q:
                pair(q, m_hi, m_lo, READY)
            token_sums(2)

            def up_pairs(g, i0):
                with pe.Fori(i0, NG) as i:
                    pair(C_FFN // 2 + g * (PER_GROUP // 2) + i, a_hi, a_lo, order)

            def down_pairs(g):
                def ready(n):
                    return {0: (h_lo_done, g * NG + NG - 1), NG - 1: (h_lo_done, g * NG + NG)}.get(n)
                with pe.Fori(0, KD // 2) as i:
                    pair(C_FFN // 2 + g * (PER_GROUP // 2) + NG + i, m_hi, m_lo, range(NG), ready)

            chunk(C_FFN // 2, 0, a_hi, a_lo, order, lambda n: (a_lo_done, KD + n + 1))
            token_sums(3)
            chunk(C_FFN // 2, 1, a_hi, a_lo, order)
            up_pairs(0, 1)
            down_pairs(0)
            with pe.Fori(1, GROUPS) as g:
                up_pairs(g, 0)
                down_pairs(g)

            pe.wait_ge(zf_free, NF + 1)
            pe.wait_ge(states_done, 1)
            pe.transpose(tb[0][0:NF * CH, 0:P], ffn_tail_p[:, :], ident[:, :])
            for j in range(6):
                n = P if j < 5 else 64
                last = pe.transpose(tb[(j + 1) // 4][0:n, (j + 1) % 4 * P:(j + 1) % 4 * P + P],
                                    ffn_tail_s[:, j * P:j * P + n], ident[:, :])
            last.then_inc(ffn_t, 1)
            token_sums(4)
            pe.wait_ge(ffn_t_done, 2)
            n = 0
            for k4 in range(KD // 4):
                pe.wait_ge(y_ready, 2 * k4 + 2)
                for i, (t0, nt) in enumerate(TT):
                    if n >= 5:
                        m = n - 5
                        pe.wait_ge(y_done[m % 2], m // 2 + 1)
                    for k in range(4):
                        o = (4 * k4 + k) * T + t0
                        last = pe.transpose(tb[n % 5][0:nt, k * P:(k + 1) * P], xT[:, o:o + nt], ident[:, :])
                    last.then_inc(y_turned, 1)
                    n += 1

        @block.scalar
        def _(act):
            for d in stage(act):
                d.then_inc(staged, 16)

            def split_hi(q, e):
                act.wait_ge(landed[e], 16 * q + 16)
                if type(q) is not int or q >= 1:
                    act.wait_ge(used, 2 * q + e - 1)
                off = (q % 2) * (2 * KD * P) + e * KD * P
                half = KD * P // 2
                for h in range(2):
                    o = off + h * half
                    src = raw[:, o:o + half] if type(q) is int else raw[:, bass.ds(o, half)]
                    d = e * KD * P + h * half
                    act.activation(w_hi[:, d:d + half], src, ACT.Copy).then_inc(w_hi_done, 1)

            def root(n, width):
                act.wait_ge(total, n + 1)
                dst = r_v if n in (1, 3) else r_x
                if n == 2:
                    act.wait_ge(m_lo_done, KD)
                act.activation(dst[:, :], tb[5][:, 0:T], ACT.Sqrt, bias=eps[:, :],
                               scale=1.0 / width).then_inc(rooted, 1)

            split_hi(0, 0)
            act.wait_ge(vecs_done, 1)
            for k in range(KD):
                act.wait_ge(x_copied, k + 1)
                act.activation(tile(a_hi, k), tile(xT, k), ACT.Copy,
                               scale=col(V_MIX_PRE + k)).then_inc(a_hi_done, 1)
            split_hi(0, 1)

            def keep_u(c, j, e):
                act.wait_ge(used, c + 1)
                act.activation(tile(uT, j), mm[e][:, 0:T], ACT.Copy).then_inc(drained[e], 1)

            for c in range(2):
                keep_u(c, c, c)
                split_hi(1, c)
            with act.Fori(1, NSGU // 2) as q:
                for e in range(2):
                    keep_u(2 * q + e, 2 * q + e, e)
                    split_hi(q + 1, e)
            root(0, D)
            with act.Fori(C_V // 2, C_POOL // 2) as q:
                for e in range(2):
                    split_hi(q + 1, e)

            def pool_hi(g):
                act.wait_ge(pool_mm, g + 1)
                act.activation(tile(m_hi, g), tb[4][:, 0:T], ACT.Copy,
                               scale=col(V_POOL + g)).then_inc(m_hi_done, 1)

            def take_v(j):
                act.wait_ge(v_turned, j + 1)
                if j >= 2:
                    act.wait_ge(sgu_mm, j - 1)
                act.activation(v_tok[:, j % 2, :], tb[j % 2][:, 0:SEQ], ACT.Copy)
                act.activation(vs_tok[:, j * P:(j + 1) * P], tb[j % 2][0:TS, SEQ:SEQ + P],
                               ACT.Copy).then_inc(v_tok_done, 1)

            def sgu_hi(j):
                act.wait_ge(mix_ready, j + 1)
                act.activation(tile(m_hi, M_SGU + j), tile(vT, NSGU + j), ACT.Copy).then_inc(m_hi_done, 1)

            def gates(j0):
                take_v(j0)
                take_v(j0 + 1)
                sgu_hi(j0)
                take_v(j0 + 2)
                sgu_hi(j0 + 1)
                sgu_hi(j0 + 2)

            q0 = C_POOL // 2
            split_hi(q0 + 1, 0)
            root(1, NSGU * P)
            split_hi(q0 + 1, 1)
            pool_hi(0)
            split_hi(q0 + 2, 0)
            gates(0)
            pool_hi(1)
            split_hi(q0 + 2, 1)
            gates(3)
            pool_hi(2)
            pool_hi(3)
            with act.Fori(0, NCONV // 2) as i:
                for n in range(6):
                    if n % 3 == 2:
                        act.wait_ge(mix_ready, NSGU + 2 * i + n // 3 + 1)
                        act.activation(tile(m_hi, M_CONV + 2 * i + n // 3), hs[:, :],
                                       ACT.Copy).then_inc(m_hi_done, 1)
                    split_hi(C_CONV // 2 + 3 * i + (n + 2) // 2, n % 2)

            def take_out(c, m, e, first=False):
                act.wait_ge(used, c + 1)
                act.activation(tile(f, m), mm[e][:, 0:T], ACT.Copy, scale=col(V_MIX_POST + m))
                act.wait_ge(summed, SUMMED[1] + m)
                act.activation(sq[:, :], mm[e][:, 0:T], ACT.Square).then_inc(drained[e], 1)

            act.wait_ge(zz_free, NPOOL)
            act.wait_ge(zc_free, NCONV + 1)
            for e in range(2):
                take_out(C_OUT + e, e, e)
                split_hi(C_OUT // 2 + 1, e)
                if e == 0:
                    act.wait_ge(states_t, 1)
                    act.activation(state_out[0:60, 0, :], tb[0][0:60, 0:P], ACT.Copy)
                    act.activation(state_out[:, 1:3, :].rearrange("p a c -> p (a c)"),
                                   tb[0][:, P:3 * P], ACT.Copy)
                    act.activation(state_out[0:12, 3, :], tb[0][0:12, 3 * P:4 * P], ACT.Copy)
                    act.activation(state_out[0:96, 4, :], tb[1][0:96, 0:P],
                                   ACT.Copy).then_inc(states_done, 1)
            with act.Fori(1, KD // 2) as i:
                for e in range(2):
                    take_out(C_OUT + 2 * i + e, 2 * i + e, e)
                    split_hi(C_OUT // 2 + i + 1, e)
            root(2, D)
            for k in range(KD):
                act.wait_ge(x1_done, k + 1)
                act.activation(tile(a_hi, k), tile(xT, k), ACT.Copy,
                               scale=col(V_FFN_PRE + k)).then_inc(a_hi_done, 1)
                act.wait_ge(summed, SUMMED[2] + k)
                act.activation(sq[:, :], tile(xT, k), ACT.Square).then_inc(out_squared, 1)
            root(3, D)

            def up_step(g, i, n):
                q = C_FFN // 2 + g * (PER_GROUP // 2) + i
                split_hi(q + 1, 0)
                act.wait_ge(conv_done, n + 1)
                act.activation(gel[:, 0:SEQ], yf[:, 0:SEQ], ACT.Gelu_apprx_tanh, bias=col(V_FBIAS + n))
                act.activation(gel[:, SEQ:T].rearrange("p (b t) -> p b t", b=NB),
                               samples(yf, LC, WC, 0, TB), ACT.Gelu_apprx_tanh,
                               bias=col(V_FBIAS + n)).then_inc(gelu_done, 1)
                act.wait_ge(h_ready, n + 1)
                act.activation(tile(m_hi, i), val[:, :], ACT.Copy).then_inc(h_hi_done, 1)
                split_hi(q + 1, 1)

            def group(g, last):
                with act.Fori(0, NG) as i:
                    up_step(g, i, g * NG + i)
                qd = C_FFN // 2 + g * (PER_GROUP // 2) + NG
                if not last:
                    with act.Fori(0, KD // 2) as i:
                        for e in range(2):
                            split_hi(qd + i + 1, e)
                    return

                def square_out(m, qm, m_parity):
                    act.wait_ge(drained[m_parity], qm + 1)
                    act.wait_ge(summed, SUMMED[3] + m)
                    act.activation(sq[:, :], tile(f, m), ACT.Square).then_inc(f_gained, 1)
                    act.wait_ge(f_gained, 2 * m + 1)
                    act.activation(tile(f, m), tile(f, m), ACT.Copy,
                                   scale=col(V_FFN_POST + m)).then_inc(f_gained, 1)

                with act.Fori(0, KD // 2 - 1) as i:
                    for e in range(2):
                        split_hi(qd + i + 1, e)
                        square_out(2 * i + e, qd + i, e)
                for e in range(2):
                    square_out(KD - 2 + e, qd + KD // 2 - 1, e)

            with act.Fori(0, GROUPS - 1) as g:
                group(g, False)
            group(GROUPS - 1, True)

            act.wait_ge(ffn_t, 1)
            act.activation(ffn_out[:, 0:4, :].rearrange("p a c -> p (a c)")[0:NF * CH, 0:P],
                           tb[0][0:NF * CH, 0:P], ACT.Copy)
            act.activation(ffn_out[:, 1:4, :].rearrange("p a c -> p (a c)"), tb[0][:, P:4 * P],
                           ACT.Copy).then_inc(ffn_t_done, 1)
            act.activation(ffn_out[:, 4:6, :].rearrange("p a c -> p (a c)"), tb[1][:, 0:2 * P], ACT.Copy)
            act.activation(ffn_out[0:64, 6, :], tb[1][0:64, 2 * P:3 * P], ACT.Copy).then_inc(ffn_t_done, 1)
            root(4, D)
            n = 0
            for k4 in range(KD // 4):
                for i, (t0, nt) in enumerate(TT):
                    if n % 2 == 0:
                        act.wait_ge(y_turned, n + 1)
                        act.activation(y_tok[0:nt, i, k4 * 512:(k4 + 1) * 512], tb[n % 5][0:nt, :],
                                       ACT.Copy).then_inc(y_done[0], 1)
                    n += 1

        @block.vector
        def _(dve):
            def split_lo(q, e):
                off = (q % 2) * (2 * KD * P) + e * KD * P
                half = KD * P // 2
                for h in range(2):
                    dve.wait_ge(w_hi_done, 4 * q + 2 * e + h + 1)
                    o = off + h * half
                    src = raw[:, o:o + half] if type(q) is int else raw[:, bass.ds(o, half)]
                    d = slice(e * KD * P + h * half, e * KD * P + (h + 1) * half)
                    dve.tensor_tensor(w_lo[:, d], src, w_hi[:, d].bitcast(F32),
                                      ALU.subtract).then_inc(w_lo_done, 1)

            def invert(n):
                dve.wait_ge(rooted, n + 1)
                dst = r_v if n in (1, 3) else r_x
                dve.reciprocal(dst[:, :], dst[:, :]).then_inc(r_done, 1)
                dve.wait_ge(r_done, n + 1)

            steps = [0]

            def step(ins):
                steps[0] += 1
                ins.then_inc(dstep, 1)
                dve.wait_ge(dstep, steps[0])

            dve.wait_ge(consts, 1)
            dve.tensor_copy(sel[:, :].rearrange("s (b t) -> s b t", b=NB),
                            ident[0:TB, 0:TB].rearrange("s (a t) -> s a t", a=1).to_broadcast([TB, NB, TB])
                            ).then_inc(sel_done, 1)
            dve.wait_ge(vecs_t, 1)
            dve.tensor_copy(vec[:, :], tb[0][:, 0:268])
            dve.tensor_copy(pool_hist[:, :, :, :].rearrange("p g b r -> p (g b r)"), tb[1][:, 0:480])
            dve.tensor_copy(conv_hist[:, :], tb[2][:, 0:96])
            dve.tensor_copy(ws[:, 0:4, :].rearrange("p j q -> p (j q)"), tb[3][:, :])
            dve.tensor_copy(ws[:, 4:6, :].rearrange("p j q -> p (j q)"), tb[4][:, 0:256])
            dve.tensor_copy(ffn_hist[:, 0:512], tb[5][:, :])
            dve.tensor_copy(ffn_hist[:, 512:704], tb[4][:, 256:448]).then_inc(vecs_done, 1)
            dve.wait_ge(vecs_done, 1)
            split_lo(0, 0)
            for k in range(KD + 2):
                if k < KD:
                    dve.wait_ge(x_turned, k + 1)
                    dve.tensor_copy(tile(xT, k), tb[k % 6][:, 0:T]).then_inc(x_copied, 1)
                if k >= 2:
                    dve.wait_ge(a_hi_done, k - 1)
                    dve.scalar_tensor_tensor(out=tile(a_lo, k - 2), in0=tile(xT, k - 2),
                                             scalar=col(V_MIX_PRE + k - 2),
                                             in1=tile(a_hi, k - 2).bitcast(F32), op0=ALU.mult,
                                             op1=ALU.subtract).then_inc(a_lo_done, 1)
            split_lo(0, 1)
            dve.wait_ge(corner_mm, 1)
            dve.tensor_copy(bd[:, :, :, :],
                            tb[0][0:TS, 0:NSGU * TB].rearrange("s (j a q) -> s j a q", j=NSGU, a=1)
                            .to_broadcast([TS, NSGU, NB, TB])).then_inc(corner_done, 1)
            for e in range(2):
                split_lo(1, e)
            with dve.Fori(1, NSGU // 2) as q:
                for e in range(2):
                    split_lo(q + 1, e)
            invert(0)

            with dve.Fori(C_V // 2, C_POOL // 2) as q:
                for e in range(2):
                    dve.wait_ge(used, 2 * q + e + 1)
                    dve.tensor_tensor(tile(vT, 2 * q + e), mm[e][:, 0:T], r_x[:, :],
                                      ALU.mult).then_inc(drained[e], 1)
                    split_lo(q + 1, e)

            def fill_zz(g, c, e):
                dve.wait_ge(used, c + 1)
                if g:
                    dve.wait_ge(zz_free, g)
                dve.tensor_copy(samples(zz, LP, WP, 0, PH), pool_hist[:, g, :, :])
                dve.tensor_tensor(zz[:, PH:LP], mp[e], r_x[:, 0:SEQ], ALU.mult)
                dve.tensor_tensor(samples(zz, LP, WP, PH, WP), ms[e],
                                  r_x[:, SEQ:T].rearrange("p (b t) -> p b t", b=NB),
                                  ALU.mult).then_inc(drained[e], 1)
                dve.wait_ge(drained[e], c // 2 + 1)

            def pool_windows(g):
                w = WINDOWS[g]
                src, d, n = zz, 1, 0
                while d < w:
                    dst = win[n % 2]
                    o = 2 * d - 1
                    step(dve.tensor_tensor(dst[:, o:ZP], src[:, o:ZP], src[:, o - d:ZP - d], ALU.add))
                    src, d, n = dst, 2 * d, n + 1
                if g:
                    dve.wait_ge(pool_mm, g)
                dve.scalar_tensor_tensor(out=pooled[:, 0:SEQ], in0=src[:, PH:LP], scalar=1.0 / w,
                                         in1=zz[:, PH:LP], op0=ALU.mult, op1=ALU.subtract)
                step(dve.scalar_tensor_tensor(
                    out=pooled[:, SEQ:T].rearrange("p (b t) -> p b t", b=NB),
                    in0=samples(src, LP, WP, PH, WP), scalar=1.0 / w,
                    in1=samples(zz, LP, WP, PH, WP), op0=ALU.mult, op1=ALU.subtract))
                step(dve.tensor_tensor(pooled[:, 0:16], src[:, PH:PH + 16], icnt[:, g, :], ALU.mult))
                dve.tensor_tensor(pooled[:, 0:16], pooled[:, 0:16], zz[:, PH:PH + 16],
                                  ALU.subtract).then_inc(pooled_done, 1)
                dve.wait_ge(pooled_done, g + 1)

            def pool_lo(g):
                dve.wait_ge(m_hi_done, READY.index(g) + 1)
                dve.scalar_tensor_tensor(out=tile(m_lo, g), in0=tb[4][:, 0:T], scalar=col(V_POOL + g),
                                         in1=tile(m_hi, g).bitcast(F32), op0=ALU.mult,
                                         op1=ALU.subtract).then_inc(m_lo_done, 1)

            def gate(j):
                dve.wait_ge(sgu_mm, j + 1)
                out = tb[2 + j % 2]
                v0 = (NSGU + j) * T
                bias = sgu_bias[:, j:j + 1, :]
                dve.tensor_tensor(f[:, v0:v0 + SEQ].rearrange("p (n q) -> p n q", n=2),
                                  out[:, 0:SEQ].rearrange("p (n q) -> p n q", n=2),
                                  bias.to_broadcast([P, 2, P]), ALU.add)
                step(dve.tensor_tensor(f[:, v0 + SEQ:v0 + T].rearrange("p (b q) -> p b q", b=NB),
                                       out[:, SEQ:T].rearrange("p (b q) -> p b q", b=NB),
                                       bias[:, :, 0:TB].to_broadcast([P, NB, TB]), ALU.add))
                step(dve.tensor_tensor(tile(f, NSGU + j), tile(f, NSGU + j), tile(uT, j), ALU.mult))
                dve.tensor_tensor(tile(f, NSGU + j), tile(f, NSGU + j), r_x[:, :],
                                  ALU.mult).then_inc(mix_ready, 1)
                dve.wait_ge(m_hi_done, READY.index(M_SGU + j) + 1)
                dve.tensor_tensor(tile(m_lo, M_SGU + j), tile(f, NSGU + j),
                                  tile(m_hi, M_SGU + j).bitcast(F32), ALU.subtract).then_inc(m_lo_done, 1)

            q0 = C_POOL // 2
            dve.wait_ge(pads_done, 1)
            fill_zz(0, C_POOL, 0)
            split_lo(q0 + 1, 0)
            pool_windows(0)
            invert(1)
            for j in range(NSGU):
                dve.scalar_tensor_tensor(out=tile(vT, NSGU + j), in0=tile(vT, NSGU + j),
                                         scalar=col(V_SGU + j), in1=r_v[:, :], op0=ALU.mult,
                                         op1=ALU.mult).then_inc(v_normed, 1)
            fill_zz(1, C_POOL + 1, 1)
            split_lo(q0 + 1, 1)
            pool_windows(1)
            pool_lo(0)
            fill_zz(2, C_POOL + 2, 0)
            split_lo(q0 + 2, 0)
            for j in range(3):
                gate(j)
            pool_windows(2)
            pool_lo(1)
            fill_zz(3, C_POOL + 3, 1)
            split_lo(q0 + 2, 1)
            for j in range(3, NSGU):
                gate(j)
            pool_windows(3)
            pool_lo(2)
            pool_lo(3)

            dve.wait_ge(zz_free, NPOOL)
            dve.wait_ge(v_stored, 16)
            dve.memset(zc[:, 0:CH], 0.0).then_inc(zc_free, 1)
            head_base, PER_HEAD = steps[0], 4
            with dve.Fori(0, NCONV // 2) as i:
                q = C_CONV // 2 + 3 * i
                for h2 in range(2):
                    j = 2 * i + h2
                    made = [head_base + PER_HEAD * h2]

                    def head_step(ins):
                        made[0] += 1
                        ins.then_inc(dstep, 1)
                        dve.wait_ge(dstep, made[0] + 2 * PER_HEAD * i)

                    n = 3 * h2
                    e = n % 2
                    dve.wait_ge(used, 2 * q + n + 1)
                    dve.tensor_tensor(hs[:, :], mm[e][:, 0:T], r_x[:, :], ALU.mult).then_inc(drained[e], 1)
                    dve.wait_ge(drained[e], q + n // 2 + 1)
                    head_step(dve.tensor_tensor(hs[:, :], hs[:, :], r_x[:, :], ALU.mult))
                    split_lo(q + (n + 2) // 2, e)
                    n = 3 * h2 + 1
                    e = n % 2
                    dve.wait_ge(used, 2 * q + n + 1)
                    dve.wait_ge(zc_free, j + 1)
                    dve.tensor_copy(samples(zc, LC, WC, 0, CH),
                                    conv_hist[:, bass.ds(j * (NB * CH), NB * CH)]
                                    .rearrange("p (b r) -> p b r", b=NB))
                    dve.tensor_tensor(zc[:, CH:LC], mp[e], hs[:, 0:SEQ], ALU.mult)
                    dve.tensor_tensor(samples(zc, LC, WC, CH, WC), ms[e],
                                      hs[:, SEQ:T].rearrange("p (b t) -> p b t", b=NB),
                                      ALU.mult).then_inc(drained[e], 1)
                    dve.wait_ge(drained[e], q + n // 2 + 1)
                    head_step(dve.tensor_scalar(yc[:, 0:YC], zc[:, 0:YC], col(V_CONV + j), None, ALU.mult))
                    for t in range(1, 3):
                        head_step(dve.scalar_tensor_tensor(out=yc[:, 0:YC], in0=zc[:, t:t + YC],
                                                           scalar=col(V_CONV + t * NCONV + j),
                                                           in1=yc[:, 0:YC], op0=ALU.mult, op1=ALU.add))
                    split_lo(q + (n + 2) // 2, e)
                    n = 3 * h2 + 2
                    e = n % 2
                    dve.wait_ge(used, 2 * q + n + 1)
                    dve.tensor_tensor(hs[:, :], mm[e][:, 0:T], r_x[:, :], ALU.mult).then_inc(drained[e], 1)
                    dve.wait_ge(drained[e], q + n // 2 + 1)
                    dve.tensor_tensor(hs[:, 0:SEQ], hs[:, 0:SEQ], yc[:, 0:SEQ], ALU.mult)
                    hv = hs[:, SEQ:T].rearrange("p (b t) -> p b t", b=NB)
                    dve.tensor_tensor(hv, hv, samples(yc, LC, WC, 0, TB), ALU.mult).then_inc(mix_ready, 1)
                    dve.wait_ge(m_hi_done, NPOOL + NSGU + j + 1)
                    dve.tensor_tensor(tile(m_lo, M_CONV + j), hs[:, :],
                                      tile(m_hi, M_CONV + j).bitcast(F32),
                                      ALU.subtract).then_inc(m_lo_done, 1)
                    dve.wait_ge(m_lo_done, NPOOL + NSGU + j + 1)
                    split_lo(q + (n + 2) // 2, e)
            steps[0] += PER_HEAD * NCONV

            with dve.Fori(C_OUT // 2, C_FFN // 2) as q:
                for e in range(2):
                    split_lo(q + 1, e)
            invert(2)
            dve.memset(zf[:, 0:CH], 0.0).then_inc(zf_free, 1)

            def scale_out(k):
                dve.tensor_tensor(tile(f, k), tile(f, k), r_x[:, :], ALU.mult).then_inc(f_scaled, 1)

            def x1_lo(k):
                dve.wait_ge(a_hi_done, KD + k + 1)
                dve.scalar_tensor_tensor(out=tile(a_lo, k), in0=tile(xT, k), scalar=col(V_FFN_PRE + k),
                                         in1=tile(a_hi, k).bitcast(F32), op0=ALU.mult,
                                         op1=ALU.subtract).then_inc(a_lo_done, 1)

            AHEAD = 3
            for k in range(KD + AHEAD):
                if k < KD:
                    scale_out(k)
                if k >= AHEAD:
                    x1_lo(k - AHEAD)
            invert(3)

            block_base, PER_BLOCK = steps[0], 2

            def up_step(g, i, n):
                q = C_FFN // 2 + g * (PER_GROUP // 2) + i
                dve.wait_ge(used, 2 * q + 1)
                dve.wait_ge(zf_free, n + 1)
                dve.tensor_copy(samples(zf, LC, WC, 0, CH),
                                ffn_hist[:, bass.ds(n * (NB * CH), NB * CH)]
                                .rearrange("p (b r) -> p b r", b=NB))
                dve.tensor_tensor(zf[:, CH:LC], mp[0], r_v[:, 0:SEQ], ALU.mult)
                dve.tensor_tensor(samples(zf, LC, WC, CH, WC), ms[0],
                                  r_v[:, SEQ:T].rearrange("p (b t) -> p b t", b=NB),
                                  ALU.mult).then_inc(drained[0], 1)
                dve.wait_ge(drained[0], q + 1)
                dve.tensor_scalar(yf[:, 0:YC], zf[:, 0:YC], col(V_FCONV + n), None,
                                  ALU.mult).then_inc(dstep, 1)
                dve.wait_ge(dstep, block_base + PER_BLOCK * n + 1)
                dve.scalar_tensor_tensor(out=yf[:, 0:YC], in0=zf[:, 1:1 + YC], scalar=col(V_FCONV + NF + n),
                                         in1=yf[:, 0:YC], op0=ALU.mult, op1=ALU.add).then_inc(dstep, 1)
                dve.wait_ge(dstep, block_base + PER_BLOCK * n + 2)
                dve.scalar_tensor_tensor(out=yf[:, 0:YC], in0=zf[:, 2:2 + YC],
                                         scalar=col(V_FCONV + 2 * NF + n), in1=yf[:, 0:YC],
                                         op0=ALU.mult, op1=ALU.add).then_inc(conv_done, 1)
                split_lo(q + 1, 0)
                dve.wait_ge(used, 2 * q + 2)
                dve.tensor_tensor(val[:, :], mm[1][:, 0:T], r_v[:, :], ALU.mult).then_inc(drained[1], 1)
                dve.wait_ge(drained[1], q + 1)
                dve.wait_ge(gelu_done, n + 1)
                dve.tensor_tensor(val[:, :], val[:, :], gel[:, :], ALU.mult).then_inc(h_ready, 1)
                dve.wait_ge(h_hi_done, n + 1)
                dve.tensor_tensor(tile(m_lo, i), val[:, :], tile(m_hi, i).bitcast(F32),
                                  ALU.subtract).then_inc(h_lo_done, 1)
                dve.wait_ge(h_lo_done, n + 1)
                split_lo(q + 1, 1)

            def add_down(q, e, m):
                dve.wait_ge(used, 2 * q + e + 1)
                dve.tensor_tensor(tile(f, m), mm[e][:, 0:T], tile(f, m), ALU.add).then_inc(drained[e], 1)

            def group(g, last):
                with dve.Fori(0, NG) as i:
                    up_step(g, i, g * NG + i)
                dve.wait_ge(f_zeroed, 1)
                qd = C_FFN // 2 + g * (PER_GROUP // 2) + NG
                with dve.Fori(0, KD // 2 - last) as i:
                    for e in range(2):
                        add_down(qd + i, e, 2 * i + e)
                        split_lo(qd + i + 1, e)
                if last:
                    for e in range(2):
                        add_down(qd + KD // 2 - 1, e, KD - 2 + e)

            with dve.Fori(0, GROUPS - 1) as g:
                group(g, 0)
            group(GROUPS - 1, 1)

            invert(4)
            for k2 in range(KD // 2):
                dve.tensor_tensor(f[:, 2 * k2 * T:(2 * k2 + 2) * T].rearrange("p (k t) -> p k t", k=2),
                                  f[:, 2 * k2 * T:(2 * k2 + 2) * T].rearrange("p (k t) -> p k t", k=2),
                                  r_x[:, :].rearrange("p (k t) -> p k t", k=1).to_broadcast([P, 2, T]),
                                  ALU.mult).then_inc(f_scaled, 1)
            n = 0
            for k4 in range(KD // 4):
                for i, (t0, nt) in enumerate(TT):
                    if n % 2 == 1:
                        dve.wait_ge(y_turned, n + 1)
                        dve.tensor_copy(y_tok[0:nt, i, k4 * 512:(k4 + 1) * 512],
                                        tb[n % 5][0:nt, :]).then_inc(y_done[1], 1)
                    n += 1

        @block.gpsimd
        def _(pool):
            own = sem("own")
            steps = [0]

            def step(ins):
                steps[0] += 1
                ins.then_inc(own, 1)
                pool.wait_ge(own, steps[0])

            pool.dma_start(new_pool_sample[0, :, 0:PH - TB, :],
                           state_pool[0, :, TB:PH, :]).then_inc(stored, 16)
            n_stored = 1
            step(pool.memset(ident[:, :], 0.0))
            pool.memset(ones[:, :], 1.0)
            pool.memset(eps[:, :], EPS)
            pool.affine_select(out=ident[:, :], in_=ident[:, :], compare_op=ALU.not_equal, fill=1.0,
                               base=0, pattern=[[-1, P]], channel_multiplier=1).then_inc(consts, 1)
            for g, w in enumerate(WINDOWS):
                pool.memset(icnt[:, g, w - 1:16], 1.0 / w)
                for t in range(w - 1):
                    pool.memset(icnt[:, g, t:t + 1], 1.0 / (t + 1))

            pool.wait_ge(vecs_done, 1)
            pool.affine_select(out=ws[:, :, :], in_=ws[:, :, :], compare_op=ALU.is_ge, fill=0.0, base=0,
                               pattern=[[0, NSGU], [1, P]], channel_multiplier=-1).then_inc(tril_done, 1)

            def add_square(src, first, last):
                dst = acc if first else sq
                ins = pool.tensor_tensor(dst[:, :], src, src, ALU.mult)
                step(ins)
                if not first:
                    ins = pool.tensor_tensor(acc[:, :], acc[:, :], sq[:, :], ALU.add)
                    if last:
                        ins.then_inc(summed, 1)
                    else:
                        step(ins)

            for k in range(KD):
                pool.wait_ge(x_copied, k + 1)
                add_square(tile(xT, k), k == 0, k == KD - 1)

            pool.wait_ge(x_turned, KD)
            pool.memset(zz[:, 0:PH], 0.0).then_inc(pads_done, 1)

            pool.wait_ge(corner_done, 1)
            step(pool.affine_select(out=bd[:, :, :, :], in_=bd[:, :, :, :], compare_op=ALU.is_ge, fill=0.0,
                                    base=0, pattern=[[0, NSGU], [-TB, NB], [0, TB]], channel_multiplier=1))
            pool.affine_select(out=bd[:, :, :, :], in_=bd[:, :, :, :], compare_op=ALU.is_ge, fill=0.0,
                               base=TB - 1, pattern=[[0, NSGU], [TB, NB], [0, TB]],
                               channel_multiplier=-1).then_inc(bd_done, 1)

            pool.wait_ge(total, 1)
            for j in range(NSGU):
                c = C_V + j
                pool.wait_ge(drained[c % 2], c // 2 + 1)
                add_square(tile(vT, NSGU + j), j == 0, j == NSGU - 1)

            for g in range(NPOOL):
                c = C_POOL + g
                pool.wait_ge(drained[c % 2], c // 2 + 1)
                pool.tensor_copy(pool_tail_p[:, g * PH:(g + 1) * PH], zz[:, LP - PH:LP])
                pool.tensor_copy(pool_tail_s[:, g * TS:(g + 1) * TS].rearrange("p (b t) -> p b t", b=NB),
                                 samples(zz, LP, WP, PH, WP)).then_inc(zz_free, 1)
                if g == 2:
                    vn = 0
            pool.wait_ge(v_tok_done, NSGU)
            pool.dma_start(new_chunk_v[0].rearrange("b t c -> (b t) c"), vs_tok[:, :]).then_inc(v_stored, 16)

            with pool.Fori(0, NCONV // 2) as i:
                for h2 in range(2):
                    c = 3 * h2 + 1
                    j = 2 * i + h2
                    pool.wait_ge(drained[c % 2], C_CONV // 2 + 3 * i + c // 2 + 1)
                    pool.tensor_copy(conv_tail_p[:, bass.ds(j * CH, CH)], zc[:, LC - CH:LC])
                    pool.tensor_copy(conv_tail_s[:, bass.ds(j * (NB * CH), NB * CH)]
                                     .rearrange("p (b r) -> p b r", b=NB),
                                     samples(zc, LC, WC, WC - CH, WC)).then_inc(zc_free, 1)

            pool.wait_ge(total, 2)
            step(pool.memset(acc[:, :], 0.0))
            with pool.Fori(0, KD // 2) as i:
                for e in range(2):
                    pool.wait_ge(drained[e], C_OUT // 2 + i + 1)
                    pool.tensor_tensor(acc[:, :], acc[:, :], sq[:, :], ALU.add).then_inc(summed, 1)
                    pool.wait_ge(summed, SUMMED[1] + 2 * i + e + 1)

            pool.wait_ge(states_done, 1)
            for g in range(NPOOL):
                cs = slice(g * P, (g + 1) * P)
                pool.dma_start(new_pool_prompt[0, 0, :, cs],
                               state_out[g * PH:(g + 1) * PH, 0, :]).then_inc(stored, 16)
                src = state_out[(g % 2) * TS:(g % 2 + 1) * TS, 1 + g // 2, :]
                pool.dma_start(new_pool_sample[0, :, PH - TB:PH, cs], src).then_inc(stored, 16)
            for j in range(NCONV):
                cs = slice(j * P, (j + 1) * P)
                pool.dma_start(new_conv_prompt[0, 0, :, cs],
                               state_out[j * CH:(j + 1) * CH, 3, :]).then_inc(stored, 16)
                pool.dma_start(new_conv_sample[0, :, :, cs].rearrange("b r c -> (b r) c"),
                               state_out[j * NB * CH:(j + 1) * NB * CH, 4, :]).then_inc(stored, 16)
            n_stored += 2 * NPOOL + 2 * NCONV

            def add_sq(ready, n, done):
                pool.wait_ge(ready, n)
                pool.tensor_tensor(acc[:, :], acc[:, :], sq[:, :], ALU.add).then_inc(summed, 1)
                pool.wait_ge(summed, done)

            pool.wait_ge(total, 3)
            step(pool.memset(acc[:, :], 0.0))
            for k in range(KD + 2):
                if k < KD:
                    pool.wait_ge(f_scaled, k + 1)
                    pool.tensor_tensor(tile(xT, k), tile(xT, k), tile(f, k), ALU.add).then_inc(x1_done, 1)
                if k >= 2:
                    add_sq(out_squared, k - 1, SUMMED[2] + k - 1)
            pool.wait_ge(x1_done, KD)
            pool.memset(f[:, :], 0.0).then_inc(f_zeroed, 1)

            def save_zf(g, i, n):
                pool.wait_ge(drained[0], C_FFN // 2 + g * (PER_GROUP // 2) + i + 1)
                pool.tensor_copy(ffn_tail_p[:, bass.ds(n * CH, CH)], zf[:, LC - CH:LC])
                pool.tensor_copy(ffn_tail_s[:, bass.ds(n * (NB * CH), NB * CH)]
                                 .rearrange("p (b r) -> p b r", b=NB),
                                 samples(zf, LC, WC, WC - CH, WC)).then_inc(zf_free, 1)

            with pool.Fori(0, GROUPS) as g:
                with pool.Fori(0, NG) as i:
                    save_zf(g, i, g * NG + i)

            pool.wait_ge(total, 4)
            step(pool.memset(acc[:, :], 0.0))
            with pool.Fori(0, KD) as m:
                add_sq(f_gained, 2 * m + 1, SUMMED[3] + m + 1)

            pool.wait_ge(f_gained, 2 * KD)
            for k2 in range(KD // 2):
                pool.wait_ge(f_scaled, KD + k2 + 1)
                pool.tensor_tensor(tile(xT, 2 * k2, 2), tile(xT, 2 * k2, 2), tile(f, 2 * k2, 2),
                                   ALU.add).then_inc(y_ready, 1)

            pool.wait_ge(ffn_t_done, 2)
            for j in range(NF):
                cs = slice(j * P, (j + 1) * P)
                pool.dma_start(new_ffn_sample[0, :, :, cs].rearrange("b r c -> (b r) c"),
                               ffn_out[16 * (j % 8):16 * (j % 8) + 16, 1 + j // 8, :]).then_inc(stored, 16)
            n_stored += NF
            for r in range(CH):
                pass
            pool.dma_start(new_ffn_prompt[0, 0].rearrange("r (j c) -> j r c", c=P),
                           ffn_out[0:NF * CH, 0, :]).then_inc(stored, 16)
            n_stored += 1
            pool.wait_ge(stored, 16 * n_stored)


_INS = ['x_prompt', 'x_sample', 'state_pool', 'state_conv', 'state_ffn', 'g_mix_pre', 'g_mix_post',
        'g_ffn_pre', 'g_ffn_post', 'w_in', 'pool_w', 'pool_scale', 'conv_w', 'sgu_norm', 'sgu_w',
        'sgu_b', 'w_out', 'ffn_up', 'ffn_conv_w', 'ffn_conv_b', 'ffn_down']


def kernel(**inputs):
    import numpy as _np
    import concourse.bacc as _bacc
    from concourse import mybir as _mybir
    from concourse.bass_utils import run_bass_kernel_spmd as _run

    nc = _bacc.Bacc("TRN2", target_bir_lowering=False, num_devices=1)
    arrays, args = {}, []
    for name in _INS:
        a = _np.ascontiguousarray(inputs[name])
        arrays[f"in_{name}_dram"] = a
        args.append(nc.dram_tensor(f"in_{name}_dram", a.shape, _mybir.dt.from_np(a.dtype),
                                   kind="ExternalInput").ap())
    n, b, t = (1,) + inputs["x_sample"].shape[:2]
    outs = [inputs["x_prompt"].shape, inputs["x_sample"].shape]
    for name in ("state_pool", "state_conv", "state_ffn"):
        s = inputs[name].shape
        outs += [(s[0], inputs["x_prompt"].shape[0]) + tuple(s[2:]), s]
    outs.append((inputs["sgu_norm"].shape[0], b, t, inputs["sgu_norm"].shape[1]))
    for i, shape in enumerate(outs):
        args.append(nc.dram_tensor(f"out_{i}_dram", tuple(shape), _mybir.dt.float32,
                                   kind="ExternalOutput").ap())
    hybrid_layer(nc, *args)
    r = _run(nc, [arrays], core_ids=[0])
    return tuple(r.results[0][f"out_{i}_dram"] for i in range(len(outs)))
```

```python
from contextlib import ExitStack

import concourse.bass as bass
from concourse import mybir

F32 = mybir.dt.float32
F32R = mybir.dt.float32r
ACT = mybir.ActivationFunctionType
ALU = mybir.AluOpType

P = 128
EPS = 1e-6
WINDOWS = (2, 4, 8, 16)


def hybrid_layer(nc, x_prompt, x_sample, state_pool, state_conv, state_ffn, g_mix_pre, g_mix_post,
                 g_ffn_pre, g_ffn_post, w_in, pool_w, pool_scale, conv_w, sgu_norm, sgu_w, sgu_b,
                 w_out, ffn_up, ffn_conv_w, ffn_conv_b, ffn_down,
                 y_prompt, y_sample, new_pool_prompt, new_pool_sample, new_conv_prompt,
                 new_conv_sample, new_ffn_prompt, new_ffn_sample, new_chunk_v):
    SEQ, D = x_prompt.shape[1:]
    NB, TB = x_sample.shape[:2]
    TS = NB * TB
    T = SEQ + TS
    KD = D // P
    NPOOL = len(WINDOWS)
    NCONV = conv_w.shape[2] // P
    NSGU = sgu_norm.shape[1] // P
    NF = ffn_conv_b.shape[1] // P
    PH = state_pool.shape[2]
    CH = state_conv.shape[2]
    GROUPS = 4
    NG = NF // GROUPS
    TT = [(0, P), (P, P), (2 * P, TS)]
    assert SEQ == 2 * P and D == 16 * P and TS == 64 and NG * GROUPS == NF and NF % 2 == 0

    POOL0, H0 = 0, NPOOL
    BG0 = H0 + NCONV
    CG0 = BG0 + NCONV
    U0 = CG0 + NCONV
    M_CONV, M_SGU = NPOOL, NPOOL + NCONV
    READY = [0, M_SGU, M_SGU + 1, 1, M_SGU + 2, M_SGU + 3, 2, M_SGU + 4, M_SGU + 5, 3] + \
            [M_CONV + j for j in range(NCONV)]

    C_V = NSGU
    C_POOL = 2 * NSGU
    C_CONV = C_POOL + NPOOL
    C_OUT = C_CONV + 3 * NCONV
    C_FFN = C_OUT + KD
    PER_GROUP = 2 * NG + KD
    CHUNKS = C_FFN + GROUPS * PER_GROUP

    LP = PH + SEQ
    WP = PH + TB
    ZP = LP + NB * WP
    LC = CH + SEQ
    WC = CH + TB
    ZC = LC + NB * WC
    YC = ZC - CH

    CHUNK_B, TILE_B = KD * P * 4, T * 4
    at = {}
    top = [(nc.sbuf_base + 31) // 32 * 32]

    def region(name, size):
        at[name] = top[0]
        top[0] += (size + 31) // 32 * 32

    for name, size in (("raw", 4 * CHUNK_B), ("w_hi", 2 * CHUNK_B), ("w_lo", 2 * CHUNK_B),
                       ("xT", KD * TILE_B), ("a_hi", KD * TILE_B), ("a_lo", KD * TILE_B),
                       ("m_hi", KD * TILE_B), ("m_lo", KD * TILE_B), ("f", KD * TILE_B),
                       ("ident", 512), ("ones", 512), ("vec", 4 * 268), ("r_x", TILE_B),
                       ("r_v", TILE_B), ("acc", TILE_B), ("sq", TILE_B), ("cols", 64),
                       ("ffn_hist", 4 * NF * NB * CH), ("ffn_tail_s", 4 * NF * NB * CH),
                       ("ffn_tail_p", 4 * NF * CH), ("ws", 4 * NSGU * P), ("bd", 4 * NSGU * TS),
                       ("pool_w", 4 * NPOOL * P), ("pool_hist", 4 * NPOOL * NB * PH),
                       ("conv_hist", 4 * NCONV * NB * CH), ("pool_tail_p", 4 * NPOOL * PH),
                       ("pool_tail_s", 4 * NPOOL * TS), ("conv_tail_p", 4 * NCONV * CH),
                       ("conv_tail_s", 4 * NCONV * NB * CH), ("icnt", 4 * NPOOL * 16)):
        region(name, size)
    assert top[0] <= nc.sbuf_usable_end, top[0]

    def sb(name, shape, dt=F32, where=None, plus=0):
        return nc.alloc_sbuf_tensor_at(name, shape, dt, offset=at[where or name] + plus)

    raw = sb("raw", [P, 4 * KD * P])
    w_hi = sb("w_hi", [P, 2 * KD * P], F32R)
    w_lo = sb("w_lo", [P, 2 * KD * P], F32R)
    xT = sb("xT", [P, KD * T])
    a_hi = sb("a_hi", [P, KD * T], F32R)
    a_lo = sb("a_lo", [P, KD * T], F32R)
    m_hi = sb("m_hi", [P, KD * T], F32R)
    m_lo = sb("m_lo", [P, KD * T], F32R)
    f = sb("f", [P, KD * T])
    ident = sb("ident", [P, P])
    ones = sb("ones", [P, P])
    vec = sb("vec", [P, 268])
    r_x = sb("r_x", [P, T])
    r_v = sb("r_v", [P, T])
    acc = sb("acc", [P, T])
    sq = sb("sq", [P, T])
    cols = sb("cols", [P, 4, 4])
    diag = sb("diag", [P, 3, P], where="acc")
    ffn_hist = sb("ffn_hist", [P, NF * NB * CH])
    ffn_tail_s = sb("ffn_tail_s", [P, NF * NB * CH])
    ffn_tail_p = sb("ffn_tail_p", [P, NF * CH])
    ws = sb("ws", [P, NSGU, P])
    bd = sb("bd", [TS, NSGU, NB, TB])
    pool_w_sb = sb("pool_w", [P, NPOOL, P])
    pool_hist = sb("pool_hist", [P, NPOOL, NB, PH])
    conv_hist = sb("conv_hist", [P, NCONV * NB * CH])
    pool_tail_p = sb("pool_tail_p", [P, NPOOL * PH])
    pool_tail_s = sb("pool_tail_s", [P, NPOOL * TS])
    conv_tail_p = sb("conv_tail_p", [P, NCONV * CH])
    conv_tail_s = sb("conv_tail_s", [P, NCONV * NB * CH])
    icnt = sb("icnt", [P, NPOOL, 16])
    sel = sb("sel", [TB, TS], where="conv_tail_s")

    x_tok = sb("x_tok", [P, 3, D], where="m_hi")
    sgu_raw = sb("sgu_raw", [P, NSGU, P], where="m_lo", plus=11264)
    ffn_raw = sb("ffn_raw", [P, 6, P], where="m_lo", plus=11264 + 3072)
    vec_raw = sb("vec_raw", [P, 3, P], where="f", plus=12 * TILE_B)
    pool_raw = sb("pool_raw", [NB * PH, NPOOL, P], where="f", plus=12 * TILE_B + 1536)
    conv_raw = sb("conv_raw", [NCONV * NB * CH, P], where="f", plus=12 * TILE_B + 3584)
    zz = sb("zz", [P, ZP], where="m_hi", plus=4 * TILE_B)
    win = [sb(f"win{i}", [P, ZP], where="m_hi", plus=4 * TILE_B + (i + 1) * 1824) for i in range(2)]
    v_tok = sb("v_tok", [P, 2, 2 * P], where="m_hi", plus=4 * TILE_B + 3 * 1824)
    sgu_bias = sb("sgu_bias", [P, NSGU, P], where="m_lo", plus=4 * TILE_B)
    vs_tok = sb("vs_tok", [TS, NSGU * P], where="m_lo", plus=8192)
    pooled = sb("pooled", [P, T], where="m_lo", plus=9 * TILE_B)
    hs = sb("hs", [P, T], where="f", plus=12 * TILE_B)
    zc = sb("zc", [P, ZC], where="f", plus=13 * TILE_B)
    yc = sb("yc", [P, ZC], where="f", plus=13 * TILE_B + 1376)
    uT, vT = f, f
    state_out = sb("state_out", [P, 5, P], where="ws")
    zf = sb("zf", [P, ZC], where="m_hi", plus=NG * TILE_B)
    yf = sb("yf", [P, ZC], where="m_hi", plus=NG * TILE_B + 1376)
    gel = sb("gel", [P, T], where="m_lo", plus=NG * TILE_B)
    val = sb("val", [P, T], where="m_lo", plus=(NG + 1) * TILE_B)
    y_tok = sb("y_tok", [P, 3, D], where="a_hi")
    QD = D // 512
    f_tok = [sb(f"f_tok{n}", [P, 512], where="a_hi" if n < 8 else "m_hi",
                plus=24576 + 2048 * n if n < 8 else NG * TILE_B) for n in range(3 * (QD - 1))]
    ffn_out = sb("ffn_out", [P, 7, P], where="m_hi", plus=NG * TILE_B + 2048)

    with ExitStack() as ctx:
        def sem(name):
            return ctx.enter_context(nc.semaphore(name))

        mm = [ctx.enter_context(nc.psum_tensor(f"mm{i}", [P, 512], F32)) for i in range(2)]
        tb = [ctx.enter_context(nc.psum_tensor(f"tb{i}", [P, 512], F32)) for i in range(6)]
        mp = [m[:, 0:SEQ] for m in mm]
        ms = [m[:, SEQ:T].rearrange("p (b t) -> p b t", b=NB) for m in mm]

        landed = [sem(f"landed{i}") for i in range(2)]
        w_hi_done = sem("w_hi_done")
        w_lo_done = sem("w_lo_done")
        used = sem("used")
        drained = [sem(f"drained{i}") for i in range(2)]
        x_in = [sem(f"x_in{i}") for i in range(3)]
        vecs_in = sem("vecs_in")
        staged = sem("staged")
        consts = sem("consts")
        vecs_t = sem("vecs_t")
        vecs_done = sem("vecs_done")
        hists_t = sem("hists_t")
        hists_done = sem("hists_done")
        tril_done = sem("tril_done")
        corner_mm = sem("corner_mm")
        sel_done = sem("sel_done")
        corner_done = sem("corner_done")
        bd_done = sem("bd_done")
        pads_done = sem("pads_done")
        x_turned = sem("x_turned")
        a_hi_done = sem("a_hi_done")
        x_copied = sem("x_copied")
        a_lo_done = sem("a_lo_done")
        summed = sem("summed")
        total = sem("total")
        meaned = sem("meaned")
        rooted = sem("rooted")
        diag_done = sem("diag_done")
        spread = sem("spread")
        r_done = sem("r_done")
        squared = sem("squared")
        u_scaled = sem("u_scaled")
        v_normed = sem("v_normed")
        v_turned = sem("v_turned")
        v_tok_done = sem("v_tok_done")
        sgu_mm = sem("sgu_mm")
        dstep = sem("dstep")
        mix_ready = sem("mix_ready")
        m_hi_done = sem("m_hi_done")
        m_lo_done = sem("m_lo_done")
        zz_free = sem("zz_free")
        pooled_done = sem("pooled_done")
        pool_mm = sem("pool_mm")
        zc_free = sem("zc_free")
        states_t = sem("states_t")
        states_done = sem("states_done")
        f_scaled = sem("f_scaled")
        x1_done = sem("x1_done")
        f_zeroed = sem("f_zeroed")
        zf_filled = sem("zf_filled")
        zf_free = sem("zf_free")
        conv_done = sem("conv_done")
        gelu_done = sem("gelu_done")
        h_ready = sem("h_ready")
        h_hi_done = sem("h_hi_done")
        h_lo_done = sem("h_lo_done")
        f_gained = sem("f_gained")
        turned = sem("turned")
        taken = sem("taken")
        y_done = sem("y_done")
        v_stored = sem("v_stored")
        hist_stored = sem("hist_stored")
        stored = sem("stored")

        SUMMED = [1, 2, 2 + KD, 3 + KD, 3 + 2 * KD]

        UNITS = sorted([(m, "x", m // 3, m % 3) for m in range(3 * (KD // 4))] +
                       [(4 * k4 + 5 + i, "f", k4, i) for k4 in range(KD // 4 - 1) for i in range(3)] +
                       [(12, "state", n, 0) for n in range(2)])
        UNITS += [(KD, "f", KD // 4 - 1, i) for i in range(3)]
        Y_ORDER = [(k4, i) for k4 in range(QD) for i in range(3)]

        def tile(t, k, n=1):
            return t[:, k * T:(k + n) * T] if type(k) is int else t[:, bass.ds(k * T, n * T)]

        def col(k):
            return vec[:, k:k + 1] if type(k) is int else vec[:, bass.ds(k, 1)]

        def samples(t, start, width, lo, hi):
            return t[:, start:start + NB * width].rearrange("p (b w) -> p b w", b=NB)[:, :, lo:hi]

        V_MIX_PRE, V_MIX_POST, V_FFN_PRE, V_FFN_POST = 0, KD, 2 * KD, 3 * KD
        V_CONV = 4 * KD
        V_SGU = V_CONV + 3 * NCONV
        V_POOL = V_SGU + NSGU
        V_FCONV = V_POOL + NPOOL
        V_FBIAS = V_FCONV + 3 * NF
        N_VEC0 = V_FCONV
        N_VEC1 = 2 * NF

        def stage_vecs(q):
            rows = 0
            for v in (g_mix_pre, g_mix_post, g_ffn_pre, g_ffn_post, conv_w, sgu_norm, pool_scale):
                n = v.shape[-1] // P * (3 if v is conv_w else 1)
                src = v[0].rearrange("i (j c) -> (i j) c", c=P) if v is conv_w else \
                    v[0].rearrange("(j c) -> j c", c=P)
                yield q.dma_start(vec_raw[rows:rows + n, 0, :], src)
                rows += n
            fc = ffn_conv_w[0].rearrange("i (j c) -> (i j) c", c=P)
            yield q.dma_start(vec_raw[0:2 * NF, 1, :], fc[0:2 * NF, :])
            yield q.dma_start(vec_raw[0:NF, 2, :], fc[2 * NF:3 * NF, :])
            yield q.dma_start(vec_raw[NF:2 * NF, 2, :], ffn_conv_b[0].rearrange("(j c) -> j c", c=P))

        def stage(q):
            yield q.dma_start(pool_raw[:, :, :], state_pool[0].rearrange("b r (g c) -> (b r) g c", c=P))
            yield q.dma_start(conv_raw[:, :], state_conv[0].rearrange("b r (j c) -> j (b r) c", c=P))
            yield q.dma_start(sgu_raw[:, :, :], sgu_w[0].rearrange("h q s -> q h s"))
            sf = state_ffn[0].rearrange("b r (j c) -> j (b r) c", c=P)
            for n in range(6):
                m = min(8, NF - 8 * n)
                yield q.dma_start(ffn_raw[0:16 * m, n, :], sf[8 * n:8 * n + m])
            yield q.dma_start(pool_w_sb[:, :, :], pool_w[0].rearrange("g c d -> c g d"))
            yield q.dma_start(sgu_bias[:, :, :],
                              sgu_b.rearrange("a h q -> a (h q)").to_broadcast([P, NSGU * P]))

        N_VECS, N_STAGED = 10, 3 + 6 + 2

        block = ctx.enter_context(nc.Block())

        @block.sync
        def _(sp):
            up = ffn_up[0].rearrange("(k p) n -> p k n", p=P)
            win_v = w_in[0].rearrange("(k p) n -> p k n", p=P)
            wout_v = w_out[0].rearrange("(k p) n -> p k n", p=P)
            down = ffn_down[0].rearrange("(k p) n -> p k n", p=P)

            def wcols(view, b):
                return view[:, :, b * P:(b + 1) * P] if type(b) is int else view[:, :, bass.ds(b * P, P)]

            def load(q, e, src, blocks=KD):
                if type(q) is not int or q >= 1:
                    sp.wait_ge(w_hi_done, 4 * q + 2 * e - 3)
                off = (q % 2) * (2 * KD * P) + e * KD * P
                dst = raw[:, off:off + blocks * P] if type(q) is int else \
                    raw[:, bass.ds(off, blocks * P)]
                sp.dma_start(dst.rearrange("p (k c) -> p k c", c=P), src).then_inc(landed[e], 16)

            load(0, 0, wcols(win_v, U0))
            xp = x_prompt[0].rearrange("(t p) d -> p t d", p=P)
            for t in range(2):
                sp.dma_start(x_tok[:, t, :], xp[:, t, :]).then_inc(x_in[t], 16)
            sp.dma_start(x_tok[0:TS, 2, :], x_sample.rearrange("b t d -> (b t) d")).then_inc(x_in[2], 16)
            load(0, 1, wcols(win_v, U0 + 1))
            for d in stage(sp):
                d.then_inc(staged, 16)
            for e in range(2):
                load(1, e, wcols(win_v, U0 + 2 + e))
            with sp.Fori(2, NSGU) as q:
                for e in range(2):
                    load(q, e, wcols(win_v, U0 + 2 * q + e))
            for g in range(NPOOL):
                c = C_POOL + g
                load(c // 2, c % 2, wcols(win_v, POOL0 + g))
            with sp.Fori(0, NCONV // 2) as i:
                for n in range(6):
                    load(C_CONV // 2 + 3 * i + n // 2, n % 2,
                         wcols(win_v, (H0, CG0, BG0)[n % 3] + 2 * i + n // 3))
            with sp.Fori(0, KD // 2) as i:
                for e in range(2):
                    load(C_OUT // 2 + i, e, wcols(wout_v, 2 * i + e))
            sp.wait_ge(states_done, 1)
            n_stored = 0
            sp.dma_start(new_pool_prompt[0, 0].rearrange("r (g c) -> g r c", c=P),
                         state_out[0:NPOOL * PH, 0, :]).then_inc(stored, 16)
            for g in range(NPOOL):
                sp.dma_start(new_pool_sample[0, :, PH - TB:PH, g * P:(g + 1) * P],
                             state_out[(g % 2) * TS:(g % 2 + 1) * TS, 1 + g // 2, :]).then_inc(stored, 16)
            sp.dma_start(new_conv_prompt[0, 0].rearrange("r (j c) -> j r c", c=P),
                         state_out[0:NCONV * CH, 3, :]).then_inc(stored, 16)
            sp.dma_start(new_conv_sample[0].rearrange("b r (j c) -> j (b r) c", c=P),
                         state_out[0:NCONV * NB * CH, 4, :]).then_inc(stored, 16)
            n_stored += NPOOL + 3
            with sp.Fori(0, GROUPS) as g:
                with sp.Fori(0, NG) as i:
                    q = C_FFN // 2 + g * (PER_GROUP // 2) + i
                    load(q, 0, wcols(up, g * NG + i))
                    load(q, 1, wcols(up, NF + g * NG + i))
                with sp.Fori(0, KD // 2) as i:
                    q = C_FFN // 2 + g * (PER_GROUP // 2) + NG + i
                    for e in range(2):
                        load(q, e, down[:, bass.ds(g * NG, NG), bass.ds((2 * i + e) * P, P)], NG)

            sp.wait_ge(taken, 1 + max(n for n, u in enumerate(UNITS) if u[1] == "state"))
            sp.dma_start(new_ffn_prompt[0, 0].rearrange("r (j c) -> j r c", c=P),
                         ffn_out[0:NF * CH, 0, :]).then_inc(stored, 16)
            nf = new_ffn_sample[0].rearrange("b r (j c) -> j (b r) c", c=P)
            for n in range(6):
                m = min(8, NF - 8 * n)
                sp.dma_start(nf[8 * n:8 * n + m], ffn_out[0:16 * m, 1 + n, :]).then_inc(stored, 16)
            n_stored += 7
            for n, (k4, i) in enumerate(Y_ORDER):
                t0, nt = TT[i]
                cs = slice(k4 * 512, (k4 + 1) * 512)
                sp.wait_ge(y_done, n + 1)
                dst = y_prompt[0, t0:t0 + P, cs] if i < 2 else \
                    y_sample.rearrange("b t d -> (b t) d")[:, cs]
                sp.dma_start(dst, y_tok[0:nt, i, cs]).then_inc(stored, 16)
                n_stored += 1
            sp.wait_ge(stored, 16 * n_stored)

        @block.tensor
        def _(pe):
            def chunk(q, e, hi, lo, order, ready=None, beside=None):
                pe.wait_ge(w_lo_done, 4 * q + 2 * e + 2)
                if type(q) is not int or q >= 1:
                    pe.wait_ge(drained[e], q)
                out = mm[e][:, 0:T]
                for n, k in enumerate(order):
                    for small in (beside or {}).get(n, ()):
                        small()
                    if ready and ready(n) is not None:
                        pe.wait_ge(*ready(n))
                    s = slice((e * KD + k) * P, (e * KD + k + 1) * P)
                    pe.matmul(out, w_hi[:, s], tile(hi, k), start=(n == 0), stop=False)
                    pe.matmul(out, w_hi[:, s], tile(lo, k), start=False, stop=False)
                    last = pe.matmul(out, w_lo[:, s], tile(hi, k), start=False,
                                     stop=(n == len(order) - 1))
                last.then_inc(used, 1)

            def pair(q, hi, lo, order, ready=None):
                for e in range(2):
                    chunk(q, e, hi, lo, order, ready)

            def token_sums(n):
                pe.wait_ge(summed, SUMMED[n])
                if n:
                    pe.wait_ge(r_done, n)
                for i, t0 in enumerate((0, P, T - P)):
                    last = pe.matmul(tb[5][:, i:i + 1], acc[:, t0:t0 + P], ones[:, 0:1],
                                     start=True, stop=True)
                if n == 4:
                    last = pe.matmul(tb[5][0:TS, 2:3], acc[:, SEQ:T], ones[:, 0:1], start=True, stop=True)
                last.then_inc(total, 1)

            def spread_r(n):
                pe.wait_ge(diag_done, n + 1)
                pe.matmul(tb[5][:, 64:64 + P], ones[:, :], diag[:, 0, :], start=True, stop=True)
                pe.matmul(tb[5][:, 64 + P:64 + SEQ], ones[:, :], diag[:, 1, :], start=True, stop=True)
                pe.matmul(tb[5][:, 64 + SEQ:64 + T], ones[:, :], diag[:, 2, P - TS:P],
                          start=True, stop=True).then_inc(spread, 1)

            pe.wait_ge(consts, 1)
            pe.wait_ge(vecs_in, 16 * N_VECS)
            for i, (n, o) in enumerate(((N_VEC0, 0), (N_VEC1, N_VEC0), (N_VEC1, N_VEC0 + N_VEC1))):
                last = pe.transpose(tb[0][:, o:o + n], vec_raw[0:n, i, :], ident[0:n, 0:n])
            last.then_inc(vecs_t, 1)

            for u in range(3 * (KD // 4)):
                i, k4 = u // (KD // 4), u % (KD // 4)
                if k4 == 0:
                    pe.wait_ge(x_in[i], 16)
                if u >= 5:
                    pe.wait_ge(x_copied, u - 4)
                nt = TT[i][1]
                for k in range(4):
                    b = 4 * k4 + k
                    last = pe.transpose(tb[1 + u % 5][:, k * nt:(k + 1) * nt],
                                        x_tok[0:nt, i, b * P:(b + 1) * P], ident[0:nt, 0:nt])
                last.then_inc(x_turned, 1)

            order = range(KD)
            chunk(0, 0, a_hi, a_lo, order, lambda n: (a_lo_done, n + 1))
            pe.wait_ge(staged, 16 * N_STAGED)
            pe.wait_ge(x_copied, 3 * (KD // 4))
            pe.wait_ge(vecs_done, 1)
            n = NB * PH
            for g in range(NPOOL):
                pe.transpose(tb[1][:, g * n:(g + 1) * n], pool_raw[:, g, :], ident[0:n, 0:n])
            n = NCONV * NB * CH
            pe.transpose(tb[2][:, 0:n], conv_raw[:, :], ident[0:n, 0:n])
            for j in range(NSGU):
                pe.transpose(tb[3 + j // 4][:, (j % 4) * P:(j % 4 + 1) * P], sgu_raw[:, j, :], ident[:, :])
            for j in range(6):
                n = P if j < 5 else 64
                o = tb[5][:, j * P:j * P + n] if j < 4 else tb[4][:, 256 + (j - 4) * P:256 + (j - 4) * P + n]
                last = pe.transpose(o, ffn_raw[0:n, j, :], ident[0:n, 0:n])
            last.then_inc(hists_t, 1)

            def corners():
                pe.wait_ge(tril_done, 1)
                pe.wait_ge(sel_done, 1)
                pe.matmul(tb[0][0:TS, 0:NSGU * TB], sel[:, :], ws[0:TB, :, 0:TB],
                          start=True, stop=True).then_inc(corner_mm, 1)

            chunk(0, 1, a_hi, a_lo, order)
            with pe.Fori(1, NSGU // 2) as q:
                pair(q, a_hi, a_lo, order)
            corners()
            token_sums(0)
            chunk(C_V // 2, 0, a_hi, a_lo, order, beside={9: [lambda: spread_r(0)]})
            chunk(C_V // 2, 1, a_hi, a_lo, order)
            with pe.Fori(C_V // 2 + 1, C_POOL // 2) as q:
                pair(q, a_hi, a_lo, order)

            def pool_map(g):
                pe.wait_ge(pooled_done, g + 1)
                if g:
                    pe.wait_ge(m_lo_done, READY.index(g - 1) + 1)
                pe.matmul(tb[4][:, 0:T], pool_w_sb[:, g, :], pooled[:, :], start=True,
                          stop=True).then_inc(pool_mm, 1)

            def turn_v(j):
                if j >= 2:
                    pe.wait_ge(v_tok_done, j - 1)
                for i, (t0, n) in enumerate(TT):
                    last = pe.transpose(tb[j % 2][0:n, i * P:(i + 1) * P],
                                        f[:, (NSGU + j) * T + t0:(NSGU + j) * T + t0 + n], ident[:, :])
                last.then_inc(v_turned, 1)

            def gate_v(j):
                pe.wait_ge(v_tok_done, j + 1)
                if j >= 2:
                    pe.wait_ge(mix_ready, j - 1)
                out = tb[2 + j % 2]
                for i in range(2):
                    pe.matmul(out[:, i * P:(i + 1) * P], v_tok[:, j % 2, i * P:(i + 1) * P],
                              ws[:, j, :], start=True, stop=True)
                pe.matmul(out[:, SEQ:T], vs_tok[:, j * P:(j + 1) * P],
                          bd[:, j, :, :].rearrange("s b q -> s (b q)"), start=True,
                          stop=True).then_inc(sgu_mm, 1)

            def mixers(g):
                j = 2 * g
                return {1: [lambda: turn_v(j)], 2: [lambda: turn_v(j + 1)], 5: [lambda: pool_map(g)],
                        8: [lambda: gate_v(j)], 10: [lambda: gate_v(j + 1)]}

            chunk(C_POOL // 2, 0, a_hi, a_lo, order, beside={12: [lambda: token_sums(1)]})
            chunk(C_POOL // 2, 1, a_hi, a_lo, order, beside={2: [lambda: spread_r(1)]})
            pe.wait_ge(v_normed, NSGU)
            pe.wait_ge(bd_done, 1)
            chunk(C_POOL // 2 + 1, 0, a_hi, a_lo, order, beside=mixers(0))
            chunk(C_POOL // 2 + 1, 1, a_hi, a_lo, order, beside=mixers(1))
            chunk(C_CONV // 2, 0, a_hi, a_lo, order, beside=mixers(2))
            chunk(C_CONV // 2, 1, a_hi, a_lo, order, beside={5: [lambda: pool_map(3)]})
            with pe.Fori(C_CONV // 2 + 1, C_OUT // 2) as q:
                pair(q, a_hi, a_lo, order)

            chunk(C_OUT // 2, 0, m_hi, m_lo, READY, lambda n: (m_lo_done, n + 1))
            pe.wait_ge(zz_free, NPOOL)
            pe.wait_ge(zc_free, NCONV + 1)
            pe.transpose(tb[0][0:NPOOL * PH, 0:P], pool_tail_p[:, :], ident[:, :])
            for i in range(2):
                pe.transpose(tb[0][:, (i + 1) * P:(i + 2) * P], pool_tail_s[:, i * P:(i + 1) * P], ident[:, :])
            pe.transpose(tb[0][0:NCONV * CH, 3 * P:4 * P], conv_tail_p[:, :], ident[:, :])
            pe.transpose(tb[1][0:NCONV * NB * CH, 0:P], conv_tail_s[:, :], ident[:, :]).then_inc(states_t, 1)
            chunk(C_OUT // 2, 1, m_hi, m_lo, READY)
            with pe.Fori(C_OUT // 2 + 1, C_FFN // 2) as q:
                pair(q, m_hi, m_lo, READY)
            token_sums(2)
            spread_r(2)

            def up_pairs(g, i0):
                with pe.Fori(i0, NG) as i:
                    pair(C_FFN // 2 + g * (PER_GROUP // 2) + i, a_hi, a_lo, order)

            def ready_h(g):
                return lambda n: {0: (h_lo_done, g * NG + NG - 1),
                                  NG - 1: (h_lo_done, g * NG + NG)}.get(n)

            def down_pairs(g):
                with pe.Fori(0, KD // 2) as i:
                    pair(C_FFN // 2 + g * (PER_GROUP // 2) + NG + i, m_hi, m_lo, range(NG), ready_h(g))

            chunk(C_FFN // 2, 0, a_hi, a_lo, order, lambda n: (a_lo_done, KD + n + 1))
            chunk(C_FFN // 2, 1, a_hi, a_lo, order, beside={13: [lambda: token_sums(3)]})
            spread_r(3)
            up_pairs(0, 1)
            down_pairs(0)
            with pe.Fori(1, GROUPS - 1) as g:
                up_pairs(g, 0)
                down_pairs(g)
            up_pairs(GROUPS - 1, 0)

            def turn_unit(n):
                m, what, k4, i = UNITS[n]
                bank = tb[n % 5]
                if n >= 5:
                    pe.wait_ge(taken, n - 4)
                if n == 0:
                    pe.wait_ge(states_done, 1)
                if what == "state":
                    pe.wait_ge(zf_free, NF + 1)
                    if k4 == 0:
                        pe.transpose(bank[0:NF * CH, 0:P], ffn_tail_p[:, :], ident[:, :])
                    for j in range(3) if k4 == 0 else range(3, 6):
                        r, o = (P if j < 5 else 64), (j + 1 if k4 == 0 else j - 3) * P
                        last = pe.transpose(bank[0:r, o:o + P], ffn_tail_s[:, j * P:j * P + r], ident[:, :])
                else:
                    src = xT if what == "x" else f
                    if what == "f":
                        pe.wait_ge(f_gained, 4 * k4 + 4)
                    t0, nt = TT[i]
                    for k in range(4):
                        o = (4 * k4 + k) * T + t0
                        last = pe.transpose(bank[0:nt, k * P:(k + 1) * P], src[:, o:o + nt], ident[:, :])
                last.then_inc(turned, 1)

            g = GROUPS - 1
            for m in range(KD):
                mine = [n for n, u in enumerate(UNITS) if u[0] == m]
                chunk(C_FFN // 2 + g * (PER_GROUP // 2) + NG + m // 2, m % 2, m_hi, m_lo, range(NG),
                      ready_h(g), {3 + 2 * x: [lambda n=n: turn_unit(n)] for x, n in enumerate(mine)})
            for n, u in enumerate(UNITS):
                if u[0] == KD:
                    turn_unit(n)
            token_sums(4)

        @block.scalar
        def _(act):
            for d in stage_vecs(act):
                d.then_inc(vecs_in, 16)
            act.preload_act_table(ACT.Sqrt)

            def split_hi(q, e, blocks=KD):
                act.wait_ge(landed[e], 16 * q + 16)
                if type(q) is not int or q >= 1:
                    act.wait_ge(used, 2 * q + e - 1)
                off = (q % 2) * (2 * KD * P) + e * KD * P
                half = blocks * P // 2
                for h in range(2):
                    o = off + h * half
                    src = raw[:, o:o + half] if type(q) is int else raw[:, bass.ds(o, half)]
                    d = e * KD * P + h * half
                    act.activation(w_hi[:, d:d + half], src, ACT.Copy).then_inc(w_hi_done, 1)

            def root(n):
                act.wait_ge(meaned, n + 1)
                act.activation(cols[:, 1, 0:3], cols[:, 0, 0:3], ACT.Sqrt).then_inc(rooted, 1)

            def keep_r(n):
                act.wait_ge(spread, n + 1)
                if n == 2:
                    act.wait_ge(m_lo_done, KD)
                dst = r_v if n in (1, 3) else r_x
                act.activation(dst[:, :], tb[5][:, 64:64 + T], ACT.Copy).then_inc(r_done, 1)

            split_hi(0, 0)
            for u in range(3 * (KD // 4)):
                i, k4 = u // (KD // 4), u % (KD // 4)
                t0, nt = TT[i]
                act.wait_ge(x_turned, u + 1)
                act.activation(xT[:, :].rearrange("p (k t) -> p k t", t=T)[:, 4 * k4:4 * k4 + 4, t0:t0 + nt],
                               tb[1 + u % 5][:, 0:4 * nt].rearrange("p (k t) -> p k t", k=4),
                               ACT.Copy).then_inc(x_copied, 1)
            act.wait_ge(vecs_done, 1)
            act.wait_ge(x_copied, 3 * (KD // 4))
            for k in range(KD):
                act.activation(tile(a_hi, k), tile(xT, k), ACT.Copy,
                               scale=col(V_MIX_PRE + k)).then_inc(a_hi_done, 1)
            split_hi(0, 1)

            def keep_u(c, j, e):
                act.wait_ge(used, c + 1)
                act.activation(tile(uT, j), mm[e][:, 0:T], ACT.Copy).then_inc(drained[e], 1)

            for c in range(2):
                keep_u(c, c, c)
                split_hi(1, c)
            with act.Fori(1, NSGU // 2) as q:
                for e in range(2):
                    keep_u(2 * q + e, 2 * q + e, e)
                    split_hi(q + 1, e)
            root(0)
            keep_r(0)
            with act.Fori(C_V // 2, C_POOL // 2) as q:
                for e in range(2):
                    split_hi(q + 1, e)

            def pool_hi(g):
                act.wait_ge(pool_mm, g + 1)
                act.activation(tile(m_hi, g), tb[4][:, 0:T], ACT.Copy,
                               scale=col(V_POOL + g)).then_inc(m_hi_done, 1)

            def take_v(j):
                act.wait_ge(v_turned, j + 1)
                if j >= 2:
                    act.wait_ge(sgu_mm, j - 1)
                act.activation(v_tok[:, j % 2, :], tb[j % 2][:, 0:SEQ], ACT.Copy)
                act.activation(vs_tok[:, j * P:(j + 1) * P], tb[j % 2][0:TS, SEQ:SEQ + P],
                               ACT.Copy).then_inc(v_tok_done, 1)

            def sgu_hi(j):
                act.wait_ge(mix_ready, j + 1)
                act.activation(tile(m_hi, M_SGU + j), tile(vT, NSGU + j), ACT.Copy).then_inc(m_hi_done, 1)

            q0 = C_POOL // 2
            root(1)
            split_hi(q0 + 1, 0)
            keep_r(1)
            split_hi(q0 + 1, 1)
            for g in range(NSGU // 2):
                take_v(2 * g)
                take_v(2 * g + 1)
                pool_hi(g)
                sgu_hi(2 * g)
                sgu_hi(2 * g + 1)
                if g < 2:
                    split_hi(q0 + 2, g)
            pool_hi(3)
            with act.Fori(0, NCONV // 2) as i:
                for n in range(6):
                    if n % 3 == 2:
                        act.wait_ge(mix_ready, NSGU + 2 * i + n // 3 + 1)
                        act.activation(tile(m_hi, M_CONV + 2 * i + n // 3), hs[:, :],
                                       ACT.Copy).then_inc(m_hi_done, 1)
                    split_hi(C_CONV // 2 + 3 * i + (n + 2) // 2, n % 2)

            def take_out(c, m, e):
                act.wait_ge(used, c + 1)
                act.wait_ge(summed, SUMMED[1] + m)
                act.activation(sq[:, :], mm[e][:, 0:T], ACT.Square).then_inc(squared, 1)
                act.activation(tile(f, m), mm[e][:, 0:T], ACT.Copy,
                               scale=col(V_MIX_POST + m)).then_inc(drained[e], 1)

            act.wait_ge(zz_free, NPOOL)
            act.wait_ge(zc_free, NCONV + 1)
            for e in range(2):
                take_out(C_OUT + e, e, e)
                split_hi(C_OUT // 2 + 1, e)
                if e == 0:
                    act.wait_ge(states_t, 1)
                    act.activation(state_out[0:60, 0, :], tb[0][0:60, 0:P], ACT.Copy)
                    act.activation(state_out[:, 1:3, :].rearrange("p a c -> p (a c)"),
                                   tb[0][:, P:3 * P], ACT.Copy)
                    act.activation(state_out[0:12, 3, :], tb[0][0:12, 3 * P:4 * P], ACT.Copy)
                    act.activation(state_out[0:96, 4, :], tb[1][0:96, 0:P],
                                   ACT.Copy).then_inc(states_done, 1)
            with act.Fori(1, KD // 2) as i:
                for e in range(2):
                    take_out(C_OUT + 2 * i + e, 2 * i + e, e)
                    split_hi(C_OUT // 2 + i + 1, e)
            root(2)
            keep_r(2)
            for k in range(KD):
                act.wait_ge(x1_done, k + 1)
                act.activation(tile(a_hi, k), tile(xT, k), ACT.Copy,
                               scale=col(V_FFN_PRE + k)).then_inc(a_hi_done, 1)
                act.activation(tile(f, k), tile(xT, k), ACT.Square).then_inc(squared, 1)
            root(3)
            keep_r(3)
            act.preload_act_table(ACT.Gelu_apprx_tanh)

            def up_step(g, i, n):
                q = C_FFN // 2 + g * (PER_GROUP // 2) + i
                split_hi(q + 1, 0)
                act.wait_ge(conv_done, n + 1)
                act.activation(gel[:, 0:SEQ], yf[:, 0:SEQ], ACT.Gelu_apprx_tanh, bias=col(V_FBIAS + n))
                act.activation(gel[:, SEQ:T].rearrange("p (b t) -> p b t", b=NB),
                               samples(yf, LC, WC, 0, TB), ACT.Gelu_apprx_tanh,
                               bias=col(V_FBIAS + n)).then_inc(gelu_done, 1)
                act.wait_ge(h_ready, n + 1)
                act.activation(tile(m_hi, i), val[:, :], ACT.Copy).then_inc(h_hi_done, 1)
                split_hi(q + 1, 1)

            def group(g, last):
                with act.Fori(0, NG) as i:
                    up_step(g, i, g * NG + i)
                qd = C_FFN // 2 + g * (PER_GROUP // 2) + NG
                if not last:
                    with act.Fori(0, KD // 2) as i:
                        for e in range(2):
                            split_hi(qd + i + 1, e)
                    return

                def take_unit(n):
                    m, what, k4, i = UNITS[n]
                    nt, bank = TT[i][1], tb[n % 5]
                    act.wait_ge(turned, n + 1)
                    if what == "x":
                        act.activation(y_tok[0:nt, i, k4 * 512:(k4 + 1) * 512], bank[0:nt, :],
                                       ACT.Copy).then_inc(taken, 1)
                    elif what == "f":
                        act.activation(f_tok[3 * k4 + i][0:nt, :], bank[0:nt, :], ACT.Copy).then_inc(taken, 1)
                    elif k4 == 0:
                        act.activation(ffn_out[0:NF * CH, 0, :], bank[0:NF * CH, 0:P], ACT.Copy)
                        act.activation(ffn_out[:, 1:4, :].rearrange("p a c -> p (a c)"),
                                       bank[:, P:4 * P], ACT.Copy).then_inc(taken, 1)
                    else:
                        act.activation(ffn_out[:, 4:6, :].rearrange("p a c -> p (a c)"),
                                       bank[:, 0:2 * P], ACT.Copy)
                        act.activation(ffn_out[0:64, 6, :], bank[0:64, 2 * P:3 * P],
                                       ACT.Copy).then_inc(taken, 1)

                act.preload_act_table(ACT.Sqrt)
                for m in range(KD):
                    if m == 0:
                        take_unit(0)
                    if m < KD - 2:
                        split_hi(qd + m // 2 + 1, m % 2, NG)
                    act.wait_ge(drained[m % 2], qd + m // 2 + 1)
                    act.wait_ge(summed, SUMMED[3] + m)
                    act.activation(sq[:, :], tile(f, m), ACT.Square).then_inc(squared, 1)
                    act.wait_ge(squared, 2 * KD + m + 1)
                    act.activation(tile(f, m), tile(f, m), ACT.Copy,
                                   scale=col(V_FFN_POST + m)).then_inc(f_gained, 1)
                    for n, u in enumerate(UNITS):
                        if u[0] == m + 1 and m + 1 < KD:
                            take_unit(n)

            with act.Fori(0, GROUPS - 1) as g:
                group(g, False)
            group(GROUPS - 1, True)
            root(4)

        @block.vector
        def _(dve):
            def split_lo(q, e, blocks=KD):
                off = (q % 2) * (2 * KD * P) + e * KD * P
                half = blocks * P // 2
                for h in range(2):
                    dve.wait_ge(w_hi_done, 4 * q + 2 * e + h + 1)
                    o = off + h * half
                    src = raw[:, o:o + half] if type(q) is int else raw[:, bass.ds(o, half)]
                    d = slice(e * KD * P + h * half, e * KD * P + (h + 1) * half)
                    dve.tensor_tensor(w_lo[:, d], src, w_hi[:, d].bitcast(F32),
                                      ALU.subtract).then_inc(w_lo_done, 1)

            steps = [0]

            def step(ins):
                steps[0] += 1
                ins.then_inc(dstep, 1)
                dve.wait_ge(dstep, steps[0])

            def stats(n, width):
                v, root, r, t = (cols[:, x, 0:3] for x in range(4))
                dve.wait_ge(total, n + 1)
                dve.tensor_scalar(v, tb[5][:, 0:3], 1.0 / width, EPS, ALU.mult, ALU.add).then_inc(meaned, 1)
                dve.wait_ge(rooted, n + 1)
                step(dve.reciprocal(r, root))
                step(dve.tensor_tensor(t, r, r, ALU.mult))
                step(dve.tensor_tensor(t, t, v, ALU.mult))
                step(dve.tensor_scalar(t, t, -0.5, 1.5, ALU.mult, ALU.add))
                step(dve.tensor_tensor(r, r, t, ALU.mult))
                if n < 4:
                    dve.tensor_tensor(diag[:, :, :],
                                      ident[:, :].rearrange("p (a c) -> p a c", a=1).to_broadcast([P, 3, P]),
                                      r.rearrange("p (a c) -> p a c", c=1).to_broadcast([P, 3, P]),
                                      ALU.mult).then_inc(diag_done, 1)

            dve.wait_ge(consts, 1)
            dve.tensor_copy(sel[:, :].rearrange("s (b t) -> s b t", b=NB),
                            ident[0:TB, 0:TB].rearrange("s (a t) -> s a t", a=1).to_broadcast([TB, NB, TB])
                            ).then_inc(sel_done, 1)
            dve.wait_ge(vecs_t, 1)
            dve.tensor_copy(vec[:, :], tb[0][:, 0:268]).then_inc(vecs_done, 1)
            dve.wait_ge(vecs_done, 1)
            split_lo(0, 0)
            for k in range(KD):
                dve.wait_ge(a_hi_done, k + 1)
                dve.scalar_tensor_tensor(out=tile(a_lo, k), in0=tile(xT, k), scalar=col(V_MIX_PRE + k),
                                         in1=tile(a_hi, k).bitcast(F32), op0=ALU.mult,
                                         op1=ALU.subtract).then_inc(a_lo_done, 1)
            split_lo(0, 1)
            dve.wait_ge(hists_t, 1)
            dve.tensor_copy(pool_hist[:, :, :, :].rearrange("p g b r -> p (g b r)"), tb[1][:, 0:480])
            dve.tensor_copy(conv_hist[:, :], tb[2][:, 0:96])
            dve.tensor_copy(ws[:, 0:4, :].rearrange("p j q -> p (j q)"), tb[3][:, :])
            dve.tensor_copy(ws[:, 4:6, :].rearrange("p j q -> p (j q)"), tb[4][:, 0:256])
            dve.tensor_copy(ffn_hist[:, 0:512], tb[5][:, :])
            dve.tensor_copy(ffn_hist[:, 512:704], tb[4][:, 256:448]).then_inc(hists_done, 1)
            for e in range(2):
                split_lo(1, e)
            with dve.Fori(1, NSGU // 2) as q:
                for e in range(2):
                    split_lo(q + 1, e)
            dve.wait_ge(corner_mm, 1)
            dve.tensor_copy(bd[:, :, :, :],
                            tb[0][0:TS, 0:NSGU * TB].rearrange("s (j a q) -> s j a q", j=NSGU, a=1)
                            .to_broadcast([TS, NSGU, NB, TB])).then_inc(corner_done, 1)
            stats(0, D)
            dve.wait_ge(r_done, 1)

            with dve.Fori(C_V // 2, C_POOL // 2) as q:
                for e in range(2):
                    dve.wait_ge(used, 2 * q + e + 1)
                    dve.tensor_tensor(tile(vT, 2 * q + e), mm[e][:, 0:T], r_x[:, :],
                                      ALU.mult).then_inc(drained[e], 1)
                    split_lo(q + 1, e)

            def fill_zz(g, c, e):
                dve.wait_ge(used, c + 1)
                if g:
                    dve.wait_ge(zz_free, g)
                dve.tensor_copy(samples(zz, LP, WP, 0, PH), pool_hist[:, g, :, :])
                dve.tensor_tensor(zz[:, PH:LP], mp[e], r_x[:, 0:SEQ], ALU.mult)
                dve.tensor_tensor(samples(zz, LP, WP, PH, WP), ms[e],
                                  r_x[:, SEQ:T].rearrange("p (b t) -> p b t", b=NB),
                                  ALU.mult).then_inc(drained[e], 1)
                dve.wait_ge(drained[e], c // 2 + 1)

            def pool_windows(g):
                w = WINDOWS[g]
                src, d, n = zz, 1, 0
                while d < w:
                    dst = win[n % 2]
                    o = 2 * d - 1
                    step(dve.tensor_tensor(dst[:, o:ZP], src[:, o:ZP], src[:, o - d:ZP - d], ALU.add))
                    src, d, n = dst, 2 * d, n + 1
                if g:
                    dve.wait_ge(pool_mm, g)
                dve.scalar_tensor_tensor(out=pooled[:, 0:SEQ], in0=src[:, PH:LP], scalar=1.0 / w,
                                         in1=zz[:, PH:LP], op0=ALU.mult, op1=ALU.subtract)
                step(dve.scalar_tensor_tensor(
                    out=pooled[:, SEQ:T].rearrange("p (b t) -> p b t", b=NB),
                    in0=samples(src, LP, WP, PH, WP), scalar=1.0 / w,
                    in1=samples(zz, LP, WP, PH, WP), op0=ALU.mult, op1=ALU.subtract))
                step(dve.tensor_tensor(pooled[:, 0:16], src[:, PH:PH + 16], icnt[:, g, :], ALU.mult))
                dve.tensor_tensor(pooled[:, 0:16], pooled[:, 0:16], zz[:, PH:PH + 16],
                                  ALU.subtract).then_inc(pooled_done, 1)
                dve.wait_ge(pooled_done, g + 1)

            def pool_lo(g):
                dve.wait_ge(m_hi_done, READY.index(g) + 1)
                dve.scalar_tensor_tensor(out=tile(m_lo, g), in0=tb[4][:, 0:T], scalar=col(V_POOL + g),
                                         in1=tile(m_hi, g).bitcast(F32), op0=ALU.mult,
                                         op1=ALU.subtract).then_inc(m_lo_done, 1)

            def gate(j):
                dve.wait_ge(sgu_mm, j + 1)
                out = tb[2 + j % 2]
                v0 = (NSGU + j) * T
                bias = sgu_bias[:, j:j + 1, :]
                dve.tensor_tensor(f[:, v0:v0 + SEQ].rearrange("p (n q) -> p n q", n=2),
                                  out[:, 0:SEQ].rearrange("p (n q) -> p n q", n=2),
                                  bias.to_broadcast([P, 2, P]), ALU.add)
                step(dve.tensor_tensor(f[:, v0 + SEQ:v0 + T].rearrange("p (b q) -> p b q", b=NB),
                                       out[:, SEQ:T].rearrange("p (b q) -> p b q", b=NB),
                                       bias[:, :, 0:TB].to_broadcast([P, NB, TB]), ALU.add))
                dve.wait_ge(u_scaled, j + 1)
                dve.tensor_tensor(tile(f, NSGU + j), tile(f, NSGU + j), tile(uT, j),
                                  ALU.mult).then_inc(mix_ready, 1)
                dve.wait_ge(m_hi_done, READY.index(M_SGU + j) + 1)
                dve.tensor_tensor(tile(m_lo, M_SGU + j), tile(f, NSGU + j),
                                  tile(m_hi, M_SGU + j).bitcast(F32), ALU.subtract).then_inc(m_lo_done, 1)

            q0 = C_POOL // 2
            stats(1, NSGU * P)
            dve.wait_ge(pads_done, 1)
            dve.wait_ge(hists_done, 1)
            fill_zz(0, C_POOL, 0)
            split_lo(q0 + 1, 0)
            dve.wait_ge(r_done, 2)
            for j in range(NSGU):
                dve.scalar_tensor_tensor(out=tile(vT, NSGU + j), in0=tile(vT, NSGU + j),
                                         scalar=col(V_SGU + j), in1=r_v[:, :], op0=ALU.mult,
                                         op1=ALU.mult).then_inc(v_normed, 1)
            pool_windows(0)
            for g in range(1, NPOOL):
                fill_zz(g, C_POOL + g, g % 2)
                split_lo(q0 + 1 + g // 2, g % 2)
                pool_windows(g)
                pool_lo(g - 1)
                gate(2 * g - 2)
                gate(2 * g - 1)
            pool_lo(3)

            dve.wait_ge(zz_free, NPOOL)
            dve.memset(zc[:, 0:CH], 0.0).then_inc(zc_free, 1)
            head_base, PER_HEAD = steps[0], 4
            with dve.Fori(0, NCONV // 2) as i:
                q = C_CONV // 2 + 3 * i
                for h2 in range(2):
                    j = 2 * i + h2
                    made = [head_base + PER_HEAD * h2]

                    def head_step(ins):
                        made[0] += 1
                        ins.then_inc(dstep, 1)
                        dve.wait_ge(dstep, made[0] + 2 * PER_HEAD * i)

                    n = 3 * h2
                    e = n % 2
                    dve.wait_ge(used, 2 * q + n + 1)
                    dve.tensor_tensor(hs[:, :], mm[e][:, 0:T], r_x[:, :], ALU.mult).then_inc(drained[e], 1)
                    dve.wait_ge(drained[e], q + n // 2 + 1)
                    head_step(dve.tensor_tensor(hs[:, :], hs[:, :], r_x[:, :], ALU.mult))
                    split_lo(q + (n + 2) // 2, e)
                    n = 3 * h2 + 1
                    e = n % 2
                    dve.wait_ge(used, 2 * q + n + 1)
                    dve.wait_ge(zc_free, j + 1)
                    dve.tensor_copy(samples(zc, LC, WC, 0, CH),
                                    conv_hist[:, bass.ds(j * (NB * CH), NB * CH)]
                                    .rearrange("p (b r) -> p b r", b=NB))
                    dve.tensor_tensor(zc[:, CH:LC], mp[e], hs[:, 0:SEQ], ALU.mult)
                    dve.tensor_tensor(samples(zc, LC, WC, CH, WC), ms[e],
                                      hs[:, SEQ:T].rearrange("p (b t) -> p b t", b=NB),
                                      ALU.mult).then_inc(drained[e], 1)
                    dve.wait_ge(drained[e], q + n // 2 + 1)
                    head_step(dve.tensor_scalar(yc[:, 0:YC], zc[:, 0:YC], col(V_CONV + j), None, ALU.mult))
                    for t in range(1, 3):
                        head_step(dve.scalar_tensor_tensor(out=yc[:, 0:YC], in0=zc[:, t:t + YC],
                                                           scalar=col(V_CONV + t * NCONV + j),
                                                           in1=yc[:, 0:YC], op0=ALU.mult, op1=ALU.add))
                    split_lo(q + (n + 2) // 2, e)
                    n = 3 * h2 + 2
                    e = n % 2
                    dve.wait_ge(used, 2 * q + n + 1)
                    dve.tensor_tensor(hs[:, :], mm[e][:, 0:T], r_x[:, :], ALU.mult).then_inc(drained[e], 1)
                    dve.wait_ge(drained[e], q + n // 2 + 1)
                    dve.tensor_tensor(hs[:, 0:SEQ], hs[:, 0:SEQ], yc[:, 0:SEQ], ALU.mult)
                    hv = hs[:, SEQ:T].rearrange("p (b t) -> p b t", b=NB)
                    dve.tensor_tensor(hv, hv, samples(yc, LC, WC, 0, TB), ALU.mult).then_inc(mix_ready, 1)
                    dve.wait_ge(m_hi_done, NPOOL + NSGU + j + 1)
                    dve.wait_ge(v_stored, 16)
                    dve.tensor_tensor(tile(m_lo, M_CONV + j), hs[:, :],
                                      tile(m_hi, M_CONV + j).bitcast(F32),
                                      ALU.subtract).then_inc(m_lo_done, 1)
                    dve.wait_ge(m_lo_done, NPOOL + NSGU + j + 1)
                    split_lo(q + (n + 2) // 2, e)
            steps[0] += PER_HEAD * NCONV

            dve.wait_ge(spread, 2)
            step(dve.memset(acc[:, :], 0.0))
            with dve.Fori(0, KD // 2) as i:
                for e in range(2):
                    dve.wait_ge(squared, 2 * i + e + 1)
                    dve.wait_ge(summed, SUMMED[1] + 2 * i + e)
                    dve.tensor_tensor(acc[:, :], acc[:, :], sq[:, :], ALU.add).then_inc(summed, 1)
                    split_lo(C_OUT // 2 + i + 1, e)
            stats(2, D)
            dve.memset(zf[:, 0:CH], 0.0).then_inc(zf_free, 1)
            dve.wait_ge(r_done, 3)

            def scale_out(k):
                dve.tensor_tensor(tile(f, k), tile(f, k), r_x[:, :], ALU.mult).then_inc(f_scaled, 1)

            def x1_lo(k):
                dve.wait_ge(a_hi_done, KD + k + 1)
                dve.scalar_tensor_tensor(out=tile(a_lo, k), in0=tile(xT, k), scalar=col(V_FFN_PRE + k),
                                         in1=tile(a_hi, k).bitcast(F32), op0=ALU.mult,
                                         op1=ALU.subtract).then_inc(a_lo_done, 1)

            AHEAD = 3
            for k in range(KD + AHEAD):
                if k < KD:
                    scale_out(k)
                if k >= AHEAD:
                    x1_lo(k - AHEAD)
            dve.wait_ge(squared, 2 * KD)
            dve.wait_ge(spread, 3)
            dve.tensor_reduce(acc[:, :], f[:, :].rearrange("p (k t) -> p t k", k=KD),
                              mybir.AxisListType.X, ALU.add).then_inc(summed, 1)
            stats(3, D)
            dve.wait_ge(r_done, 4)

            block_base, PER_BLOCK = steps[0], 2

            def up_step(g, i, n):
                q = C_FFN // 2 + g * (PER_GROUP // 2) + i
                dve.wait_ge(used, 2 * q + 1)
                dve.wait_ge(zf_free, n + 1)
                dve.tensor_copy(samples(zf, LC, WC, 0, CH),
                                ffn_hist[:, bass.ds(n * (NB * CH), NB * CH)]
                                .rearrange("p (b r) -> p b r", b=NB))
                dve.tensor_tensor(zf[:, CH:LC], mp[0], r_v[:, 0:SEQ], ALU.mult)
                dve.tensor_tensor(samples(zf, LC, WC, CH, WC), ms[0],
                                  r_v[:, SEQ:T].rearrange("p (b t) -> p b t", b=NB),
                                  ALU.mult).then_inc(drained[0], 1)
                dve.wait_ge(drained[0], q + 1)
                dve.tensor_scalar(yf[:, 0:YC], zf[:, 0:YC], col(V_FCONV + n), None,
                                  ALU.mult).then_inc(dstep, 1)
                dve.wait_ge(dstep, block_base + PER_BLOCK * n + 1)
                dve.scalar_tensor_tensor(out=yf[:, 0:YC], in0=zf[:, 1:1 + YC], scalar=col(V_FCONV + NF + n),
                                         in1=yf[:, 0:YC], op0=ALU.mult, op1=ALU.add).then_inc(dstep, 1)
                dve.wait_ge(dstep, block_base + PER_BLOCK * n + 2)
                dve.scalar_tensor_tensor(out=yf[:, 0:YC], in0=zf[:, 2:2 + YC],
                                         scalar=col(V_FCONV + 2 * NF + n), in1=yf[:, 0:YC],
                                         op0=ALU.mult, op1=ALU.add).then_inc(conv_done, 1)
                split_lo(q + 1, 0)
                dve.wait_ge(used, 2 * q + 2)
                dve.tensor_tensor(val[:, :], mm[1][:, 0:T], r_v[:, :], ALU.mult).then_inc(drained[1], 1)
                dve.wait_ge(drained[1], q + 1)
                dve.wait_ge(gelu_done, n + 1)
                dve.tensor_tensor(val[:, :], val[:, :], gel[:, :], ALU.mult).then_inc(h_ready, 1)
                dve.wait_ge(h_hi_done, n + 1)
                dve.tensor_tensor(tile(m_lo, i), val[:, :], tile(m_hi, i).bitcast(F32),
                                  ALU.subtract).then_inc(h_lo_done, 1)
                dve.wait_ge(h_lo_done, n + 1)
                split_lo(q + 1, 1)

            def add_down(q, e, m):
                dve.wait_ge(used, 2 * q + e + 1)
                dve.tensor_tensor(tile(f, m), mm[e][:, 0:T], tile(f, m), ALU.add).then_inc(drained[e], 1)

            def group(g, last):
                with dve.Fori(0, NG) as i:
                    up_step(g, i, g * NG + i)
                dve.wait_ge(f_zeroed, 1)
                qd = C_FFN // 2 + g * (PER_GROUP // 2) + NG
                if not last:
                    with dve.Fori(0, KD // 2) as i:
                        for e in range(2):
                            add_down(qd + i, e, 2 * i + e)
                            split_lo(qd + i + 1, e)
                    return

                def add_square(m):
                    dve.wait_ge(squared, 2 * KD + m + 1)
                    dve.wait_ge(summed, SUMMED[3] + m)
                    dve.tensor_tensor(acc[:, :], acc[:, :], sq[:, :], ALU.add).then_inc(summed, 1)

                dve.wait_ge(spread, 4)
                step(dve.memset(acc[:, :], 0.0))
                for m in range(KD):
                    add_down(qd + m // 2, m % 2, m)
                    if m:
                        add_square(m - 1)
                    if m < KD - 2:
                        split_lo(qd + m // 2 + 1, m % 2, NG)
                add_square(KD - 1)

            with dve.Fori(0, GROUPS - 1) as g:
                group(g, 0)
            steps[0] += PER_BLOCK * NF
            group(GROUPS - 1, 1)

            stats(4, D)
            n_taken = sum(u[0] < KD for u in UNITS)
            dve.wait_ge(taken, n_taken)
            for k4, i in Y_ORDER:
                nt = TT[i][1]
                piece = y_tok[0:nt, i, k4 * 512:(k4 + 1) * 512]
                down = f_tok[3 * k4 + i] if k4 < QD - 1 else tb[(n_taken + i) % 5]
                dve.scalar_tensor_tensor(out=piece, in0=down[0:nt, :], scalar=cols[0:nt, 2, i:i + 1],
                                         in1=piece, op0=ALU.mult, op1=ALU.add).then_inc(y_done, 1)

        @block.gpsimd
        def _(pool):
            own = sem("own")
            steps = [0]

            def step(ins):
                steps[0] += 1
                ins.then_inc(own, 1)
                pool.wait_ge(own, steps[0])

            pool.dma_start(new_pool_sample[0, :, 0:PH - TB, :],
                           state_pool[0, :, TB:PH, :]).then_inc(hist_stored, 16)
            step(pool.memset(ident[:, :], 0.0))
            pool.memset(ones[:, :], 1.0)
            pool.affine_select(out=ident[:, :], in_=ident[:, :], compare_op=ALU.not_equal, fill=1.0,
                               base=0, pattern=[[-1, P]], channel_multiplier=1).then_inc(consts, 1)
            for g, w in enumerate(WINDOWS):
                pool.memset(icnt[:, g, w - 1:16], 1.0 / w)
                for t in range(w - 1):
                    pool.memset(icnt[:, g, t:t + 1], 1.0 / (t + 1))

            def add_square(src, first, last):
                dst = acc if first else sq
                ins = pool.tensor_tensor(dst[:, :], src, src, ALU.mult)
                step(ins)
                if not first:
                    ins = pool.tensor_tensor(acc[:, :], acc[:, :], sq[:, :], ALU.add)
                    if last:
                        ins.then_inc(summed, 1)
                    else:
                        step(ins)

            pool.wait_ge(x_copied, 3 * (KD // 4))
            for k in range(KD):
                if k == KD // 2:
                    pool.wait_ge(hists_done, 1)
                    pool.affine_select(out=ws[:, :, :], in_=ws[:, :, :], compare_op=ALU.is_ge, fill=0.0,
                                       base=0, pattern=[[0, NSGU], [1, P]],
                                       channel_multiplier=-1).then_inc(tril_done, 1)
                add_square(tile(xT, k), k == 0, k == KD - 1)

            pool.wait_ge(x_turned, 3 * (KD // 4))
            pool.memset(zz[:, 0:PH], 0.0).then_inc(pads_done, 1)

            pool.wait_ge(corner_done, 1)
            step(pool.affine_select(out=bd[:, :, :, :], in_=bd[:, :, :, :], compare_op=ALU.is_ge, fill=0.0,
                                    base=0, pattern=[[0, NSGU], [-TB, NB], [0, TB]], channel_multiplier=1))
            pool.affine_select(out=bd[:, :, :, :], in_=bd[:, :, :, :], compare_op=ALU.is_ge, fill=0.0,
                               base=TB - 1, pattern=[[0, NSGU], [TB, NB], [0, TB]],
                               channel_multiplier=-1).then_inc(bd_done, 1)

            pool.wait_ge(r_done, 1)
            pool.wait_ge(drained[1], NSGU // 2)
            for j in range(NSGU):
                pool.tensor_tensor(tile(uT, j), tile(uT, j), r_x[:, :], ALU.mult).then_inc(u_scaled, 1)

            pool.wait_ge(spread, 1)
            for j in range(NSGU):
                c = C_V + j
                pool.wait_ge(drained[c % 2], c // 2 + 1)
                add_square(tile(vT, NSGU + j), j == 0, j == NSGU - 1)

            for g in range(NPOOL):
                c = C_POOL + g
                pool.wait_ge(drained[c % 2], c // 2 + 1)
                pool.tensor_copy(pool_tail_p[:, g * PH:(g + 1) * PH], zz[:, LP - PH:LP])
                pool.tensor_copy(pool_tail_s[:, g * TS:(g + 1) * TS].rearrange("p (b t) -> p b t", b=NB),
                                 samples(zz, LP, WP, PH, WP)).then_inc(zz_free, 1)
            pool.wait_ge(v_tok_done, NSGU)
            pool.dma_start(new_chunk_v[0].rearrange("b t c -> (b t) c"), vs_tok[:, :]).then_inc(v_stored, 16)

            with pool.Fori(0, NCONV // 2) as i:
                for h2 in range(2):
                    c = 3 * h2 + 1
                    j = 2 * i + h2
                    pool.wait_ge(drained[c % 2], C_CONV // 2 + 3 * i + c // 2 + 1)
                    pool.tensor_copy(conv_tail_p[:, bass.ds(j * CH, CH)], zc[:, LC - CH:LC])
                    pool.tensor_copy(conv_tail_s[:, bass.ds(j * (NB * CH), NB * CH)]
                                     .rearrange("p (b r) -> p b r", b=NB),
                                     samples(zc, LC, WC, WC - CH, WC)).then_inc(zc_free, 1)

            for k in range(KD):
                pool.wait_ge(f_scaled, k + 1)
                pool.tensor_tensor(tile(xT, k), tile(xT, k), tile(f, k), ALU.add).then_inc(x1_done, 1)
            pool.wait_ge(summed, SUMMED[3])
            pool.memset(f[:, :], 0.0).then_inc(f_zeroed, 1)

            def save_zf(g, i, n):
                pool.wait_ge(drained[0], C_FFN // 2 + g * (PER_GROUP // 2) + i + 1)
                pool.tensor_copy(ffn_tail_p[:, bass.ds(n * CH, CH)], zf[:, LC - CH:LC])
                pool.tensor_copy(ffn_tail_s[:, bass.ds(n * (NB * CH), NB * CH)]
                                 .rearrange("p (b r) -> p b r", b=NB),
                                 samples(zf, LC, WC, WC - CH, WC)).then_inc(zf_free, 1)

            with pool.Fori(0, GROUPS) as g:
                with pool.Fori(0, NG) as i:
                    save_zf(g, i, g * NG + i)

            pool.wait_ge(hist_stored, 16)


_INS = ['x_prompt', 'x_sample', 'state_pool', 'state_conv', 'state_ffn', 'g_mix_pre', 'g_mix_post',
        'g_ffn_pre', 'g_ffn_post', 'w_in', 'pool_w', 'pool_scale', 'conv_w', 'sgu_norm', 'sgu_w',
        'sgu_b', 'w_out', 'ffn_up', 'ffn_conv_w', 'ffn_conv_b', 'ffn_down']


def kernel(**inputs):
    import numpy as _np
    import concourse.bacc as _bacc
    from concourse import mybir as _mybir
    from concourse.bass_utils import run_bass_kernel_spmd as _run

    nc = _bacc.Bacc("TRN2", target_bir_lowering=False, num_devices=1)
    arrays, args = {}, []
    for name in _INS:
        a = _np.ascontiguousarray(inputs[name])
        arrays[f"in_{name}_dram"] = a
        args.append(nc.dram_tensor(f"in_{name}_dram", a.shape, _mybir.dt.from_np(a.dtype),
                                   kind="ExternalInput").ap())
    n, b, t = (1,) + inputs["x_sample"].shape[:2]
    outs = [inputs["x_prompt"].shape, inputs["x_sample"].shape]
    for name in ("state_pool", "state_conv", "state_ffn"):
        s = inputs[name].shape
        outs += [(s[0], inputs["x_prompt"].shape[0]) + tuple(s[2:]), s]
    outs.append((inputs["sgu_norm"].shape[0], b, t, inputs["sgu_norm"].shape[1]))
    for i, shape in enumerate(outs):
        args.append(nc.dram_tensor(f"out_{i}_dram", tuple(shape), _mybir.dt.float32,
                                   kind="ExternalOutput").ap())
    hybrid_layer(nc, *args)
    r = _run(nc, [arrays], core_ids=[0])
    return tuple(r.results[0][f"out_{i}_dram"] for i in range(len(outs)))
```

```python
from contextlib import ExitStack

import concourse.bass as bass
from concourse import mybir

F32 = mybir.dt.float32
F32R = mybir.dt.float32r
ACT = mybir.ActivationFunctionType
ALU = mybir.AluOpType

P = 128
EPS = 1e-6
WINDOWS = (2, 4, 8, 16)


def hybrid_layer(nc, x_prompt, x_sample, state_pool, state_conv, state_ffn, g_mix_pre, g_mix_post,
                 g_ffn_pre, g_ffn_post, w_in, pool_w, pool_scale, conv_w, sgu_norm, sgu_w, sgu_b,
                 w_out, ffn_up, ffn_conv_w, ffn_conv_b, ffn_down,
                 y_prompt, y_sample, new_pool_prompt, new_pool_sample, new_conv_prompt,
                 new_conv_sample, new_ffn_prompt, new_ffn_sample, new_chunk_v):
    SEQ, D = x_prompt.shape[1:]
    NB, TB = x_sample.shape[:2]
    TS = NB * TB
    T = SEQ + TS
    KD = D // P
    NPOOL = len(WINDOWS)
    NCONV = conv_w.shape[2] // P
    NSGU = sgu_norm.shape[1] // P
    NF = ffn_conv_b.shape[1] // P
    PH = state_pool.shape[2]
    CH = state_conv.shape[2]
    GROUPS = 4
    NG = NF // GROUPS
    TT = [(0, P), (P, P), (2 * P, TS)]
    assert SEQ == 2 * P and D == 16 * P and TS == 64 and NG * GROUPS == NF and NF % 2 == 0

    POOL0, H0 = 0, NPOOL
    BG0 = H0 + NCONV
    CG0 = BG0 + NCONV
    U0 = CG0 + NCONV
    M_CONV, M_SGU = NPOOL, NPOOL + NCONV
    READY = [0, M_SGU, M_SGU + 1, 1, M_SGU + 2, M_SGU + 3, 2, M_SGU + 4, M_SGU + 5, 3] + \
            [M_CONV + j for j in range(NCONV)]

    C_V = NSGU
    C_POOL = 2 * NSGU
    C_CONV = C_POOL + NPOOL
    C_OUT = C_CONV + 3 * NCONV
    C_FFN = C_OUT + KD
    PER_GROUP = 2 * NG + KD

    LP = PH + SEQ
    WP = PH + TB
    ZP = LP + NB * WP
    LC = CH + SEQ
    WC = CH + TB
    ZC = LC + NB * WC
    YC = ZC - CH

    CHUNK_B, TILE_B = KD * P * 4, T * 4
    at = {}
    top = [(nc.sbuf_base + 31) // 32 * 32]

    def region(name, size):
        at[name] = top[0]
        top[0] += (size + 31) // 32 * 32

    for name, size in (("raw", 4 * CHUNK_B), ("w_hi", 2 * CHUNK_B), ("w_lo", 2 * CHUNK_B),
                       ("xT", KD * TILE_B), ("a_hi", KD * TILE_B), ("a_lo", KD * TILE_B),
                       ("m_hi", KD * TILE_B), ("m_lo", KD * TILE_B), ("f", KD * TILE_B),
                       ("ident", 512), ("ones", 512), ("vec", 4 * 268), ("r_x", TILE_B),
                       ("r_v", TILE_B), ("acc", TILE_B), ("sq", TILE_B), ("cols", 64),
                       ("ffn_hist", 4 * NF * NB * CH), ("ffn_tail_s", 4 * NF * NB * CH),
                       ("ffn_tail_p", 4 * NF * CH), ("ws", 4 * NSGU * P), ("bd", 4 * NSGU * TS),
                       ("pool_w", 4 * NPOOL * P), ("pool_hist", 4 * NPOOL * NB * PH),
                       ("conv_hist", 4 * NCONV * NB * CH), ("pool_tail_p", 4 * NPOOL * PH),
                       ("pool_tail_s", 4 * NPOOL * TS), ("conv_tail_p", 4 * NCONV * CH),
                       ("conv_tail_s", 4 * NCONV * NB * CH), ("icnt", 4 * NPOOL * 16)):
        region(name, size)
    assert top[0] <= nc.sbuf_usable_end, top[0]

    def sb(name, shape, dt=F32, where=None, plus=0):
        return nc.alloc_sbuf_tensor_at(name, shape, dt, offset=at[where or name] + plus)

    raw = sb("raw", [P, 4 * KD * P])
    w_hi = sb("w_hi", [P, 2 * KD * P], F32R)
    w_lo = sb("w_lo", [P, 2 * KD * P], F32R)
    xT = sb("xT", [P, KD * T])
    a_hi = sb("a_hi", [P, KD * T], F32R)
    a_lo = sb("a_lo", [P, KD * T], F32R)
    m_hi = sb("m_hi", [P, KD * T], F32R)
    m_lo = sb("m_lo", [P, KD * T], F32R)
    f = sb("f", [P, KD * T])
    ident = sb("ident", [P, P])
    ones = sb("ones", [P, P])
    vec = sb("vec", [P, 268])
    r_x = sb("r_x", [P, T])
    r_v = sb("r_v", [P, T])
    acc = sb("acc", [P, T])
    sq = sb("sq", [P, T])
    cols = sb("cols", [P, 4, 4])
    diag = sb("diag", [P, 3, P], where="acc")
    ffn_hist = sb("ffn_hist", [P, NF * NB * CH])
    ffn_tail_s = sb("ffn_tail_s", [P, NF * NB * CH])
    ffn_tail_p = sb("ffn_tail_p", [P, NF * CH])
    ws = sb("ws", [P, NSGU, P])
    bd = sb("bd", [TS, NSGU, NB, TB])
    pool_w_sb = sb("pool_w", [P, NPOOL, P])
    pool_hist = sb("pool_hist", [P, NPOOL, NB, PH])
    conv_hist = sb("conv_hist", [P, NCONV * NB * CH])
    pool_tail_p = sb("pool_tail_p", [P, NPOOL * PH])
    pool_tail_s = sb("pool_tail_s", [P, NPOOL * TS])
    conv_tail_p = sb("conv_tail_p", [P, NCONV * CH])
    conv_tail_s = sb("conv_tail_s", [P, NCONV * NB * CH])
    icnt = sb("icnt", [P, NPOOL, 16])
    sel = sb("sel", [TB, TS], where="conv_tail_s")

    x_tok = sb("x_tok", [P, 3, D], where="m_hi")
    sgu_raw = sb("sgu_raw", [P, NSGU, P], where="m_lo", plus=11264)
    ffn_raw = sb("ffn_raw", [P, 6, P], where="m_lo", plus=11264 + 3072)
    vec_raw = sb("vec_raw", [P, 3, P], where="f", plus=12 * TILE_B)
    pool_raw = sb("pool_raw", [NB * PH, NPOOL, P], where="f", plus=12 * TILE_B + 1536)
    conv_raw = sb("conv_raw", [NCONV * NB * CH, P], where="f", plus=12 * TILE_B + 3584)
    zz = sb("zz", [P, ZP], where="m_hi", plus=4 * TILE_B)
    win = [sb(f"win{i}", [P, ZP], where="m_hi", plus=4 * TILE_B + (i + 1) * 1824) for i in range(2)]
    v_tok = sb("v_tok", [P, 2, 2 * P], where="m_hi", plus=4 * TILE_B + 3 * 1824)
    sgu_bias = sb("sgu_bias", [P, NSGU, P], where="m_lo", plus=4 * TILE_B)
    vs_tok = sb("vs_tok", [TS, NSGU * P], where="m_lo", plus=8192)
    pooled = sb("pooled", [P, T], where="m_lo", plus=9 * TILE_B)
    hs = sb("hs", [P, T], where="f", plus=12 * TILE_B)
    zc = sb("zc", [P, ZC], where="f", plus=13 * TILE_B)
    yc = sb("yc", [P, ZC], where="f", plus=13 * TILE_B + 1376)
    uT, vT = f, f
    state_out = sb("state_out", [P, 5, P], where="ws")
    zf = sb("zf", [P, ZC], where="m_hi", plus=NG * TILE_B)
    yf = sb("yf", [P, ZC], where="m_hi", plus=NG * TILE_B + 1376)
    gel = sb("gel", [P, T], where="m_lo", plus=NG * TILE_B)
    val = sb("val", [P, T], where="m_lo", plus=(NG + 1) * TILE_B)
    y_tok = sb("y_tok", [P, 3, D], where="a_hi")
    QD = D // 512
    f_tok = [sb(f"f_tok{n}", [P, 512], where="a_hi" if n < 8 else "m_hi",
                plus=24576 + 2048 * n if n < 8 else NG * TILE_B) for n in range(3 * (QD - 1))]
    ffn_out = sb("ffn_out", [P, 7, P], where="m_hi", plus=NG * TILE_B + 2048)

    with ExitStack() as ctx:
        def sem(name):
            return ctx.enter_context(nc.semaphore(name))

        mm = [ctx.enter_context(nc.psum_tensor(f"mm{i}", [P, 512], F32)) for i in range(2)]
        tb = [ctx.enter_context(nc.psum_tensor(f"tb{i}", [P, 512], F32)) for i in range(6)]
        mp = [m[:, 0:SEQ] for m in mm]
        ms = [m[:, SEQ:T].rearrange("p (b t) -> p b t", b=NB) for m in mm]

        landed = [sem(f"landed{i}") for i in range(2)]
        w_hi_done = sem("w_hi_done")
        w_lo_done = sem("w_lo_done")
        used = sem("used")
        drained = [sem(f"drained{i}") for i in range(2)]
        x_in = [sem(f"x_in{i}") for i in range(KD // 4)]
        gain_in = sem("gain_in")
        vecs_in = sem("vecs_in")
        staged = sem("staged")
        consts = sem("consts")
        vecs_t = sem("vecs_t")
        vecs_done = sem("vecs_done")
        hists_t = sem("hists_t")
        hists_done = sem("hists_done")
        tril_done = sem("tril_done")
        corner_mm = sem("corner_mm")
        sel_done = sem("sel_done")
        corner_done = sem("corner_done")
        bd_done = sem("bd_done")
        pads_done = sem("pads_done")
        x_turned = sem("x_turned")
        a_hi_done = sem("a_hi_done")
        x_copied = [sem(f"x_copied{i}") for i in range(2)]
        a_lo_done = sem("a_lo_done")
        summed = sem("summed")
        total = sem("total")
        meaned = sem("meaned")
        rooted = sem("rooted")
        diag_done = sem("diag_done")
        spread = sem("spread")
        r_done = sem("r_done")
        squared = sem("squared")
        u_scaled = sem("u_scaled")
        v_normed = sem("v_normed")
        v_turned = sem("v_turned")
        v_tok_done = sem("v_tok_done")
        sgu_mm = sem("sgu_mm")
        dstep = sem("dstep")
        mix_ready = sem("mix_ready")
        m_hi_done = sem("m_hi_done")
        m_lo_done = sem("m_lo_done")
        zz_free = sem("zz_free")
        pooled_done = sem("pooled_done")
        pool_mm = sem("pool_mm")
        zc_free = sem("zc_free")
        states_t = sem("states_t")
        states_done = sem("states_done")
        f_scaled = sem("f_scaled")
        x1_done = sem("x1_done")
        merged = sem("merged")
        f_zeroed = sem("f_zeroed")
        zf_free = sem("zf_free")
        conv_done = sem("conv_done")
        gelu_done = sem("gelu_done")
        h_ready = sem("h_ready")
        h_hi_done = sem("h_hi_done")
        h_lo_done = sem("h_lo_done")
        f_gained = sem("f_gained")
        turned = sem("turned")
        taken = sem("taken")
        y_done = sem("y_done")
        y_factors = sem("y_factors")
        y_scaled = sem("y_scaled")
        y_pool_done = sem("y_pool_done")
        v_stored = sem("v_stored")
        hist_stored = sem("hist_stored")
        stored = sem("stored")

        SUMMED = [1, 2, 1 + KD, 2 + KD, 1 + 2 * KD]

        UNITS = sorted([(m, "x", m // 3, m % 3) for m in range(3 * (KD // 4))] +
                       [(4 * k4 + 5 + i, "f", k4, i) for k4 in range(KD // 4 - 1) for i in range(3)] +
                       [(12, "state", n, 0) for n in range(2)])
        UNITS += [(KD, "f", KD // 4 - 1, i) for i in range(3)]
        Y_POOL = [(1, 0), (1, 2), (2, 2)]
        Y_ORDER = [(k4, i) for k4 in range(QD) for i in range(3) if (k4, i) not in Y_POOL]

        def tile(t, k, n=1):
            return t[:, k * T:(k + n) * T] if type(k) is int else t[:, bass.ds(k * T, n * T)]

        X_UNITS = 3 * (KD // 4)
        MERGED = (4, 9)
        EARLY = 2

        def x_units(k4, e):
            return [u for u in range(3 * k4, 3 * k4 + 3) if u % 2 == e] if k4 < KD // 4 else []

        def wait_x(engine, k4):
            for e in range(2):
                engine.wait_ge(x_copied[e], (3 * k4 + 4 - e) // 2)

        def x_unit(u):
            k4, i = u // 3, u % 3
            t0, nt = TT[i]
            return (xT[:, :].rearrange("p (k t) -> p k t", t=T)[:, 4 * k4:4 * k4 + 4, t0:t0 + nt],
                    tb[1 + u % 5][:, 0:4 * nt].rearrange("p (k t) -> p k t", k=4))

        def col(k):
            return vec[:, k:k + 1] if type(k) is int else vec[:, bass.ds(k, 1)]

        def samples(t, start, width, lo, hi):
            return t[:, start:start + NB * width].rearrange("p (b w) -> p b w", b=NB)[:, :, lo:hi]

        V_MIX_PRE, V_MIX_POST, V_FFN_PRE, V_FFN_POST = 0, KD, 2 * KD, 3 * KD
        V_CONV = 4 * KD
        V_SGU = V_CONV + 3 * NCONV
        V_POOL = V_SGU + NSGU
        V_FCONV = V_POOL + NPOOL
        V_FBIAS = V_FCONV + 3 * NF
        N_VEC0 = V_FCONV
        N_VEC1 = 2 * NF

        def stage_vecs(q):
            rows = 0
            for v in (g_mix_pre, g_mix_post, g_ffn_pre, g_ffn_post, conv_w, sgu_norm, pool_scale):
                n = v.shape[-1] // P * (3 if v is conv_w else 1)
                src = v[0].rearrange("i (j c) -> (i j) c", c=P) if v is conv_w else \
                    v[0].rearrange("(j c) -> j c", c=P)
                yield q.dma_start(vec_raw[rows:rows + n, 0, :], src)
                rows += n
            fc = ffn_conv_w[0].rearrange("i (j c) -> (i j) c", c=P)
            yield q.dma_start(vec_raw[0:2 * NF, 1, :], fc[0:2 * NF, :])
            yield q.dma_start(vec_raw[0:NF, 2, :], fc[2 * NF:3 * NF, :])
            yield q.dma_start(vec_raw[NF:2 * NF, 2, :], ffn_conv_b[0].rearrange("(j c) -> j c", c=P))

        def stage(q):
            yield q.dma_start(pool_raw[:, :, :], state_pool[0].rearrange("b r (g c) -> (b r) g c", c=P))
            yield q.dma_start(conv_raw[:, :], state_conv[0].rearrange("b r (j c) -> j (b r) c", c=P))
            yield q.dma_start(sgu_raw[:, :, :], sgu_w[0].rearrange("h q s -> q h s"))
            sf = state_ffn[0].rearrange("b r (j c) -> j (b r) c", c=P)
            for n in range(6):
                m = min(8, NF - 8 * n)
                yield q.dma_start(ffn_raw[0:16 * m, n, :], sf[8 * n:8 * n + m])
            yield q.dma_start(pool_w_sb[:, :, :], pool_w[0].rearrange("g c d -> c g d"))
            yield q.dma_start(sgu_bias[:, :, :],
                              sgu_b.rearrange("a h q -> a (h q)").to_broadcast([P, NSGU * P]))

        N_VECS, N_STAGED = 6 + 3, 3 + 6 + 2

        block = ctx.enter_context(nc.Block())

        @block.sync
        def _(sp):
            up = ffn_up[0].rearrange("(k p) n -> p k n", p=P)
            win_v = w_in[0].rearrange("(k p) n -> p k n", p=P)
            wout_v = w_out[0].rearrange("(k p) n -> p k n", p=P)
            down = ffn_down[0].rearrange("(k p) n -> p k n", p=P)

            def wcols(view, b):
                return view[:, :, b * P:(b + 1) * P] if type(b) is int else view[:, :, bass.ds(b * P, P)]

            def load(q, e, src, blocks=KD):
                if type(q) is not int or q >= 1:
                    sp.wait_ge(w_hi_done, 4 * q + 2 * e - 3)
                off = (q % 2) * (2 * KD * P) + e * KD * P
                dst = raw[:, off:off + blocks * P] if type(q) is int else \
                    raw[:, bass.ds(off, blocks * P)]
                sp.dma_start(dst.rearrange("p (k c) -> p k c", c=P), src).then_inc(landed[e], 16)

            load(0, 0, wcols(win_v, U0))
            xp = x_prompt[0].rearrange("(t p) d -> p t d", p=P)
            vecs = stage_vecs(sp)
            next(vecs).then_inc(gain_in, 16)
            for k4 in range(KD // 4):
                cs = slice(k4 * 512, (k4 + 1) * 512)
                sp.dma_start(x_tok[:, 0:2, cs], xp[:, :, cs]).then_inc(x_in[k4], 16)
                sp.dma_start(x_tok[0:TS, 2, cs],
                             x_sample.rearrange("b t d -> (b t) d")[:, cs]).then_inc(x_in[k4], 16)
            load(0, 1, wcols(win_v, U0 + 1))
            for d in vecs:
                d.then_inc(vecs_in, 16)
            for d in stage(sp):
                d.then_inc(staged, 16)
            for e in range(2):
                load(1, e, wcols(win_v, U0 + 2 + e))
            with sp.Fori(2, NSGU) as q:
                for e in range(2):
                    load(q, e, wcols(win_v, U0 + 2 * q + e))
            for g in range(NPOOL):
                c = C_POOL + g
                load(c // 2, c % 2, wcols(win_v, POOL0 + g))
            with sp.Fori(0, NCONV // 2) as i:
                for n in range(6):
                    load(C_CONV // 2 + 3 * i + n // 2, n % 2,
                         wcols(win_v, (H0, CG0, BG0)[n % 3] + 2 * i + n // 3))
            with sp.Fori(0, KD // 2) as i:
                for e in range(2):
                    load(C_OUT // 2 + i, e, wcols(wout_v, 2 * i + e))
            sp.wait_ge(states_done, 1)
            n_stored = 0
            sp.dma_start(new_pool_prompt[0, 0].rearrange("r (g c) -> g r c", c=P),
                         state_out[0:NPOOL * PH, 0, :]).then_inc(stored, 16)
            for g in range(NPOOL):
                sp.dma_start(new_pool_sample[0, :, PH - TB:PH, g * P:(g + 1) * P],
                             state_out[(g % 2) * TS:(g % 2 + 1) * TS, 1 + g // 2, :]).then_inc(stored, 16)
            sp.dma_start(new_conv_prompt[0, 0].rearrange("r (j c) -> j r c", c=P),
                         state_out[0:NCONV * CH, 3, :]).then_inc(stored, 16)
            sp.dma_start(new_conv_sample[0].rearrange("b r (j c) -> j (b r) c", c=P),
                         state_out[0:NCONV * NB * CH, 4, :]).then_inc(stored, 16)
            n_stored += NPOOL + 3
            with sp.Fori(0, GROUPS) as g:
                with sp.Fori(0, NG) as i:
                    q = C_FFN // 2 + g * (PER_GROUP // 2) + i
                    load(q, 0, wcols(up, g * NG + i))
                    load(q, 1, wcols(up, NF + g * NG + i))
                with sp.Fori(0, KD // 2) as i:
                    q = C_FFN // 2 + g * (PER_GROUP // 2) + NG + i
                    for e in range(2):
                        load(q, e, down[:, bass.ds(g * NG, NG), bass.ds((2 * i + e) * P, P)], NG)

            sp.wait_ge(taken, 1 + max(n for n, u in enumerate(UNITS) if u[1] == "state"))
            sp.dma_start(new_ffn_prompt[0, 0].rearrange("r (j c) -> j r c", c=P),
                         ffn_out[0:NF * CH, 0, :]).then_inc(stored, 16)
            nf = new_ffn_sample[0].rearrange("b r (j c) -> j (b r) c", c=P)
            for n in range(6):
                m = min(8, NF - 8 * n)
                sp.dma_start(nf[8 * n:8 * n + m], ffn_out[0:16 * m, 1 + n, :]).then_inc(stored, 16)
            n_stored += 7
            leaving = [(y_done, n + 1, *piece) for n, piece in enumerate(Y_ORDER)]
            for n, piece in enumerate(Y_POOL):
                leaving.insert(4 * n + 3, (y_pool_done, n + 1, *piece))
            for done, n, k4, i in leaving:
                t0, nt = TT[i]
                cs = slice(k4 * 512, (k4 + 1) * 512)
                sp.wait_ge(done, n)
                dst = y_prompt[0, t0:t0 + P, cs] if i < 2 else \
                    y_sample.rearrange("b t d -> (b t) d")[:, cs]
                sp.dma_start(dst, y_tok[0:nt, i, cs]).then_inc(stored, 16)
                n_stored += 1
            sp.wait_ge(stored, 16 * n_stored)

        @block.tensor
        def _(pe):
            def passes(out, e, k, hi, lo, start, stop, ready_hi=None, ready_lo=None):
                s = slice((e * KD + k) * P, (e * KD + k + 1) * P)
                if ready_hi:
                    pe.wait_ge(*ready_hi)
                pe.matmul(out, w_hi[:, s], tile(hi, k), start=start, stop=False)
                pe.matmul(out, w_lo[:, s], tile(hi, k), start=False, stop=False)
                if ready_lo:
                    pe.wait_ge(*ready_lo)
                return pe.matmul(out, w_hi[:, s], tile(lo, k), start=False, stop=stop)

            def chunk(q, e, hi, lo, order, ready_hi=None, ready_lo=None, beside=None, bank=None,
                      hurry=False):
                pe.wait_ge(w_lo_done, 4 * q + 2 * e + 2 - hurry)
                if bank is None and (type(q) is not int or q >= 1):
                    pe.wait_ge(drained[e], q)
                out = (bank or mm[e])[:, 0:T]
                for n, k in enumerate(order):
                    if hurry and n == KD // 2:
                        pe.wait_ge(w_lo_done, 4 * q + 2 * e + 2)
                    for small in (beside or {}).get(n, ()):
                        small()
                    last = passes(out, e, k, hi, lo, n == 0, n == len(order) - 1,
                                  ready_hi and ready_hi(n), ready_lo and ready_lo(n))
                last.then_inc(used, 1)

            def pair(q, hi, lo, order, ready_hi=None, ready_lo=None):
                for e in range(2):
                    chunk(q, e, hi, lo, order, ready_hi, ready_lo)

            def token_sums(n):
                pe.wait_ge(summed, SUMMED[n])
                if n:
                    pe.wait_ge(r_done, n - (n > 2))
                if n == 3:
                    pe.wait_ge(f_scaled, KD)
                tiles = TT if n == 4 else [(0, P), (P, P), (T - P, P)]
                parts = [acc, sq] if n in (2, 4) else [acc]
                if n in (2, 4):
                    pe.wait_ge(squared, KD if n == 2 else 3 * KD)
                for i, (t0, nt) in enumerate(tiles):
                    for part in parts:
                        last = pe.matmul(tb[5][0:nt, i:i + 1], part[:, t0:t0 + nt], ones[:, 0:1],
                                         start=(part is acc), stop=(part is parts[-1]))
                last.then_inc(total, 1)

            def spread_r(n):
                pe.wait_ge(diag_done, n + 1)
                pe.matmul(tb[5][:, 64:64 + P], ones[:, :], diag[:, 0, :], start=True, stop=True)
                pe.matmul(tb[5][:, 64 + P:64 + SEQ], ones[:, :], diag[:, 1, :], start=True, stop=True)
                pe.matmul(tb[5][:, 64 + SEQ:64 + T], ones[:, :], diag[:, 2, P - TS:P],
                          start=True, stop=True).then_inc(spread, 1)

            pe.wait_ge(consts, 1)

            def turn_x(k4):
                pe.wait_ge(x_in[k4], 32)
                for i in range(3):
                    u = 3 * k4 + i
                    if u >= 5:
                        pe.wait_ge(x_copied[(u - 5) % 2], (u - 5) // 2 + 1)
                    nt = TT[i][1]
                    for k in range(4):
                        b = 4 * k4 + k
                        last = pe.transpose(tb[1 + u % 5][:, k * nt:(k + 1) * nt],
                                            x_tok[0:nt, i, b * P:(b + 1) * P], ident[0:nt, 0:nt])
                    last.then_inc(x_turned, 1)

            pe.wait_ge(gain_in, 16)
            pe.transpose(tb[0][:, 0:KD], vec_raw[0:KD, 0, :], ident[0:KD, 0:KD]).then_inc(vecs_t, 1)

            order = range(KD)
            turn_x(0)
            chunk(0, 0, a_hi, a_lo, order, lambda n: (a_hi_done, n + 1), lambda n: (a_lo_done, n + 1),
                  {n: [lambda k4=k4: turn_x(k4)] for k4, n in ((1, 0), (2, 1), (3, 5))})

            def small_inputs():
                pe.wait_ge(vecs_in, 16 * N_VECS)
                pe.wait_ge(vecs_done, 1)
                for j, (n, o) in enumerate(((N_VEC0, 0), (N_VEC1, N_VEC0), (N_VEC1, N_VEC0 + N_VEC1))):
                    pe.transpose(tb[0][:, o:o + n], vec_raw[0:n, j, :], ident[0:n, 0:n])
                pe.wait_ge(staged, 16 * N_STAGED)
                for e in range(2):
                    pe.wait_ge(x_copied[e], X_UNITS // 2)
                n = NB * PH
                for g in range(NPOOL):
                    pe.transpose(tb[1][:, g * n:(g + 1) * n], pool_raw[:, g, :], ident[0:n, 0:n])
                n = NCONV * NB * CH
                pe.transpose(tb[2][:, 0:n], conv_raw[:, :], ident[0:n, 0:n])
                for j in range(NSGU):
                    pe.transpose(tb[3 + j // 4][:, (j % 4) * P:(j % 4 + 1) * P], sgu_raw[:, j, :], ident[:, :])
                for j in range(6):
                    n = P if j < 5 else 64
                    o = tb[5][:, j * P:j * P + n] if j < 4 else \
                        tb[4][:, 256 + (j - 4) * P:256 + (j - 4) * P + n]
                    last = pe.transpose(o, ffn_raw[0:n, j, :], ident[0:n, 0:n])
                last.then_inc(hists_t, 1)

            def corners():
                pe.wait_ge(tril_done, 1)
                pe.wait_ge(sel_done, 1)
                pe.matmul(tb[0][0:TS, 0:NSGU * TB], sel[:, :], ws[0:TB, :, 0:TB],
                          start=True, stop=True).then_inc(corner_mm, 1)

            small_inputs()
            chunk(0, 1, a_hi, a_lo, order, hurry=True)
            with pe.Fori(1, NSGU // 2) as q:
                pair(q, a_hi, a_lo, order)
            corners()
            token_sums(0)
            chunk(C_V // 2, 0, a_hi, a_lo, order)
            chunk(C_V // 2, 1, a_hi, a_lo, order, beside={1: [lambda: spread_r(0)]})
            with pe.Fori(C_V // 2 + 1, C_POOL // 2) as q:
                pair(q, a_hi, a_lo, order)

            def pool_map(g):
                pe.wait_ge(pooled_done, g + 1)
                if g:
                    pe.wait_ge(m_lo_done, READY.index(g - 1) + 1)
                pe.matmul(tb[4][:, 0:T], pool_w_sb[:, g, :], pooled[:, :], start=True,
                          stop=True).then_inc(pool_mm, 1)

            def turn_v(j):
                if j >= 2:
                    pe.wait_ge(v_tok_done, j - 1)
                for i, (t0, n) in enumerate(TT):
                    last = pe.transpose(tb[j % 2][0:n, i * P:(i + 1) * P],
                                        f[:, (NSGU + j) * T + t0:(NSGU + j) * T + t0 + n], ident[:, :])
                last.then_inc(v_turned, 1)

            def gate_v(j):
                pe.wait_ge(v_tok_done, j + 1)
                if j >= 2:
                    pe.wait_ge(mix_ready, j - 1)
                out = tb[2 + j % 2]
                for i in range(2):
                    pe.matmul(out[:, i * P:(i + 1) * P], v_tok[:, j % 2, i * P:(i + 1) * P],
                              ws[:, j, :], start=True, stop=True)
                pe.matmul(out[:, SEQ:T], vs_tok[:, j * P:(j + 1) * P],
                          bd[:, j, :, :].rearrange("s b q -> s (b q)"), start=True,
                          stop=True).then_inc(sgu_mm, 1)

            def mixers(g):
                j = 2 * g
                return {1: [lambda: turn_v(j)], 2: [lambda: turn_v(j + 1)], 5: [lambda: pool_map(g)],
                        8: [lambda: gate_v(j)], 10: [lambda: gate_v(j + 1)]}

            chunk(C_POOL // 2, 0, a_hi, a_lo, order, beside={12: [lambda: token_sums(1)]})
            chunk(C_POOL // 2, 1, a_hi, a_lo, order, beside={2: [lambda: spread_r(1)]})
            pe.wait_ge(v_normed, NSGU)
            pe.wait_ge(bd_done, 1)
            chunk(C_POOL // 2 + 1, 0, a_hi, a_lo, order, beside=mixers(0))
            chunk(C_POOL // 2 + 1, 1, a_hi, a_lo, order, beside=mixers(1))
            chunk(C_CONV // 2, 0, a_hi, a_lo, order, beside=mixers(2))
            chunk(C_CONV // 2, 1, a_hi, a_lo, order, beside={5: [lambda: pool_map(3)]})
            with pe.Fori(C_CONV // 2 + 1, C_OUT // 2) as q:
                pair(q, a_hi, a_lo, order)

            chunk(C_OUT // 2, 0, m_hi, m_lo, READY, lambda n: (m_hi_done, n + 1),
                  lambda n: (m_lo_done, n + 1))
            pe.wait_ge(zz_free, NPOOL)
            pe.wait_ge(zc_free, NCONV + 1)
            pe.transpose(tb[0][0:NPOOL * PH, 0:P], pool_tail_p[:, :], ident[:, :])
            for i in range(2):
                pe.transpose(tb[0][:, (i + 1) * P:(i + 2) * P], pool_tail_s[:, i * P:(i + 1) * P], ident[:, :])
            pe.transpose(tb[0][0:NCONV * CH, 3 * P:4 * P], conv_tail_p[:, :], ident[:, :])
            pe.transpose(tb[1][0:NCONV * NB * CH, 0:P], conv_tail_s[:, :], ident[:, :]).then_inc(states_t, 1)
            chunk(C_OUT // 2, 1, m_hi, m_lo, READY)
            with pe.Fori(C_OUT // 2 + 1, C_FFN // 2) as q:
                pair(q, m_hi, m_lo, READY)
            token_sums(2)
            spread_r(2)

            def up_pairs(g, i0):
                with pe.Fori(i0, NG) as i:
                    pair(C_FFN // 2 + g * (PER_GROUP // 2) + i, a_hi, a_lo, order)

            def ready_h(done, g):
                return lambda n: {0: (done, g * NG + NG - 1), NG - 1: (done, g * NG + NG)}.get(n)

            def down_pairs(g):
                with pe.Fori(0, KD // 2) as i:
                    pair(C_FFN // 2 + g * (PER_GROUP // 2) + NG + i, m_hi, m_lo, range(NG),
                         ready_h(h_hi_done, g), ready_h(h_lo_done, g))

            q0, LAG = C_FFN // 2, 6
            pe.wait_ge(states_done, 1)
            for n in range(KD + LAG):
                for e, k in ((0, n), (1, n - LAG)):
                    if not 0 <= k < KD:
                        continue
                    if k == 0:
                        pe.wait_ge(w_lo_done, 4 * q0 + 2 * e + 2)
                    last = passes(tb[e][:, 0:T], e, k, a_hi, a_lo, k == 0, k == KD - 1,
                                  *((a_hi_done, KD + k + 1), (a_lo_done, KD + k + 1)) if e == 0 else ())
                    if k == KD - 1:
                        last.then_inc(used, 1)
            chunk(q0 + 1, 0, a_hi, a_lo, order, beside={9: [lambda: token_sums(3)]}, bank=tb[2],
                  hurry=True)
            chunk(q0 + 1, 1, a_hi, a_lo, order, beside={1: [lambda: spread_r(3)]}, bank=tb[3])
            for e in range(2):
                pe.wait_ge(drained[e], q0)
                chunk(q0 + 2, e, a_hi, a_lo, order, bank=mm[e])
            up_pairs(0, EARLY + 1)
            down_pairs(0)
            with pe.Fori(1, GROUPS - 1) as g:
                up_pairs(g, 0)
                down_pairs(g)
            up_pairs(GROUPS - 1, 0)

            def turn_unit(n):
                m, what, k4, i = UNITS[n]
                bank = tb[n % 5]
                if n >= 5:
                    pe.wait_ge(taken, n - 4)
                if n == 0:
                    pe.wait_ge(states_done, 1)
                if what == "state":
                    pe.wait_ge(zf_free, NF + 1)
                    if k4 == 0:
                        pe.transpose(bank[0:NF * CH, 0:P], ffn_tail_p[:, :], ident[:, :])
                    for j in range(3) if k4 == 0 else range(3, 6):
                        r, o = (P if j < 5 else 64), (j + 1 if k4 == 0 else j - 3) * P
                        last = pe.transpose(bank[0:r, o:o + P], ffn_tail_s[:, j * P:j * P + r], ident[:, :])
                else:
                    src = xT if what == "x" else f
                    if what == "f":
                        pe.wait_ge(f_gained, 4 * k4 + 4)
                    t0, nt = TT[i]
                    for k in range(4):
                        o = (4 * k4 + k) * T + t0
                        last = pe.transpose(bank[0:nt, k * P:(k + 1) * P], src[:, o:o + nt], ident[:, :])
                last.then_inc(turned, 1)

            g = GROUPS - 1
            for m in range(KD):
                mine = [n for n, u in enumerate(UNITS) if u[0] == m]
                chunk(C_FFN // 2 + g * (PER_GROUP // 2) + NG + m // 2, m % 2, m_hi, m_lo, range(NG),
                      ready_h(h_hi_done, g), ready_h(h_lo_done, g),
                      {3 + 2 * x: [lambda n=n: turn_unit(n)] for x, n in enumerate(mine)})
            token_sums(4)
            for n, u in enumerate(UNITS):
                if u[0] == KD:
                    turn_unit(n)

        @block.scalar
        def _(act):
            act.preload_act_table(ACT.Sqrt)

            def split_hi(q, e, blocks=KD):
                act.wait_ge(landed[e], 16 * q + 16)
                if type(q) is not int or q >= 1:
                    act.wait_ge(used, 2 * q + e - 1)
                off = (q % 2) * (2 * KD * P) + e * KD * P
                half = blocks * P // 2
                for h in range(2):
                    o = off + h * half
                    src = raw[:, o:o + half] if type(q) is int else raw[:, bass.ds(o, half)]
                    d = e * KD * P + h * half
                    act.activation(w_hi[:, d:d + half], src, ACT.Copy).then_inc(w_hi_done, 1)

            def root(n):
                act.wait_ge(meaned, n + 1)
                act.activation(cols[:, 1, 0:3], cols[:, 0, 0:3], ACT.Sqrt).then_inc(rooted, 1)

            def keep_r(n):
                act.wait_ge(spread, n + 1)
                dst = r_x if n == 0 else r_v
                act.activation(dst[:, :], tb[5][:, 64:64 + T], ACT.Copy).then_inc(r_done, 1)

            split_hi(0, 0)

            def copy_x(k4):
                for u in x_units(k4, 0):
                    act.wait_ge(x_turned, u + 1)
                    act.activation(*x_unit(u), ACT.Copy).then_inc(x_copied[0], 1)

            copy_x(0)
            act.wait_ge(vecs_done, 1)
            for k in range(KD):
                if k % 4 == 1:
                    copy_x(k // 4 + 1)
                if k % 4 == 0:
                    wait_x(act, k // 4)
                act.activation(tile(a_hi, k), tile(xT, k), ACT.Copy,
                               scale=col(V_MIX_PRE + k)).then_inc(a_hi_done, 1)
            split_hi(0, 1)

            def keep_u(c, j, e):
                act.wait_ge(used, c + 1)
                act.activation(tile(uT, j), mm[e][:, 0:T], ACT.Copy).then_inc(drained[e], 1)

            for c in range(2):
                keep_u(c, c, c)
                split_hi(1, c)
            with act.Fori(1, NSGU // 2) as q:
                for e in range(2):
                    keep_u(2 * q + e, 2 * q + e, e)
                    split_hi(q + 1, e)
            root(0)
            keep_r(0)
            with act.Fori(C_V // 2, C_POOL // 2) as q:
                for e in range(2):
                    split_hi(q + 1, e)

            def pool_hi(g):
                act.wait_ge(pool_mm, g + 1)
                act.activation(tile(m_hi, g), tb[4][:, 0:T], ACT.Copy,
                               scale=col(V_POOL + g)).then_inc(m_hi_done, 1)

            def take_v(j):
                act.wait_ge(v_turned, j + 1)
                if j >= 2:
                    act.wait_ge(sgu_mm, j - 1)
                act.activation(v_tok[:, j % 2, :], tb[j % 2][:, 0:SEQ], ACT.Copy)
                act.activation(vs_tok[:, j * P:(j + 1) * P], tb[j % 2][0:TS, SEQ:SEQ + P],
                               ACT.Copy).then_inc(v_tok_done, 1)

            def sgu_hi(j):
                act.wait_ge(mix_ready, j + 1)
                act.activation(tile(m_hi, M_SGU + j), tile(vT, NSGU + j), ACT.Copy).then_inc(m_hi_done, 1)

            q0 = C_POOL // 2
            root(1)
            split_hi(q0 + 1, 0)
            keep_r(1)
            split_hi(q0 + 1, 1)
            for g in range(NSGU // 2):
                take_v(2 * g)
                take_v(2 * g + 1)
                pool_hi(g)
                sgu_hi(2 * g)
                sgu_hi(2 * g + 1)
                split_hi(q0 + 2 + g // 2, g % 2)
            pool_hi(3)
            with act.Fori(0, NCONV // 2) as i:
                for n in range(6):
                    if n % 3 == 2:
                        act.wait_ge(mix_ready, NSGU + 2 * i + n // 3 + 1)
                        act.activation(tile(m_hi, M_CONV + 2 * i + n // 3), hs[:, :],
                                       ACT.Copy).then_inc(m_hi_done, 1)
                    split_hi(C_CONV // 2 + 3 * i + (n + 3) // 2, (n + 1) % 2)

            def take_out(c, m, e):
                act.wait_ge(used, c + 1)
                act.wait_ge(summed, SUMMED[1] + m)
                act.activation(sq[:, :], mm[e][:, 0:T], ACT.Square).then_inc(squared, 1)
                act.activation(tile(f, m), mm[e][:, 0:T], ACT.Copy,
                               scale=col(V_MIX_POST + m)).then_inc(drained[e], 1)

            act.wait_ge(zz_free, NPOOL)
            act.wait_ge(zc_free, NCONV + 1)
            for e in range(2):
                take_out(C_OUT + e, e, e)
                if e == 1:
                    split_hi(C_OUT // 2 + 1, 1)
                if e == 0:
                    act.wait_ge(states_t, 1)
                    act.activation(state_out[0:NPOOL * PH, 0, :], tb[0][0:NPOOL * PH, 0:P], ACT.Copy)
                    act.activation(state_out[:, 1:3, :].rearrange("p a c -> p (a c)"),
                                   tb[0][:, P:3 * P], ACT.Copy)
                    act.activation(state_out[0:NCONV * CH, 3, :],
                                   tb[0][0:NCONV * CH, 3 * P:4 * P], ACT.Copy)
                    act.activation(state_out[0:NCONV * NB * CH, 4, :], tb[1][0:NCONV * NB * CH, 0:P],
                                   ACT.Copy).then_inc(states_done, 1)
            with act.Fori(1, KD // 2 - 1) as i:
                for e in range(2):
                    take_out(C_OUT + 2 * i + e, 2 * i + e, e)
                    split_hi(C_OUT // 2 + i + 1, e)
            take_out(C_FFN - 2, KD - 2, 0)
            split_hi(C_FFN // 2, 0)
            take_out(C_FFN - 1, KD - 1, 1)
            root(2)
            split_hi(C_FFN // 2, 1)
            for k in range(KD):
                act.wait_ge(x1_done, k + 1)
                act.activation(tile(a_hi, k), tile(xT, k), ACT.Copy,
                               scale=col(V_FFN_PRE + k)).then_inc(a_hi_done, 1)
                act.activation(tile(f, k), tile(xT, k), ACT.Square).then_inc(squared, 1)
            for e in range(2):
                split_hi(C_FFN // 2 + 1, e)
            root(3)
            keep_r(3)
            split_hi(C_FFN // 2 + EARLY, 0)
            act.preload_act_table(ACT.Gelu_apprx_tanh)

            def up_step(g, i, n, early=False, blocks=KD):
                q = C_FFN // 2 + g * (PER_GROUP // 2) + i
                if not early:
                    split_hi(q + 1, 0, blocks)
                act.wait_ge(conv_done, n + 1)
                act.activation(gel[:, 0:SEQ], yf[:, 0:SEQ], ACT.Gelu_apprx_tanh, bias=col(V_FBIAS + n))
                act.activation(gel[:, SEQ:T].rearrange("p (b t) -> p b t", b=NB),
                               samples(yf, LC, WC, 0, TB), ACT.Gelu_apprx_tanh,
                               bias=col(V_FBIAS + n)).then_inc(gelu_done, 1)
                act.wait_ge(h_ready, n + 1)
                act.activation(tile(m_hi, i), val[:, :], ACT.Copy).then_inc(h_hi_done, 1)
                if not early:
                    split_hi(q + 1, 1, blocks)

            def up_steps(g, i0=0):
                with act.Fori(i0, NG - 1) as i:
                    up_step(g, i, g * NG + i)
                up_step(g, NG - 1, g * NG + NG - 1, blocks=NG)

            def group(g, last):
                qd = C_FFN // 2 + g * (PER_GROUP // 2) + NG
                if not last:
                    with act.Fori(0, KD // 2 - 1) as i:
                        for e in range(2):
                            split_hi(qd + i + 1, e, NG)
                    for e in range(2):
                        split_hi(qd + KD // 2, e)
                    return

                def take_unit(n):
                    m, what, k4, i = UNITS[n]
                    nt, bank = TT[i][1], tb[n % 5]
                    act.wait_ge(turned, n + 1)
                    if what == "x":
                        act.activation(y_tok[0:nt, i, k4 * 512:(k4 + 1) * 512], bank[0:nt, :],
                                       ACT.Copy).then_inc(taken, 1)
                    elif what == "f":
                        act.activation(f_tok[3 * k4 + i][0:nt, :], bank[0:nt, :], ACT.Copy).then_inc(taken, 1)
                    elif k4 == 0:
                        act.activation(ffn_out[0:NF * CH, 0, :], bank[0:NF * CH, 0:P], ACT.Copy)
                        act.activation(ffn_out[:, 1:4, :].rearrange("p a c -> p (a c)"),
                                       bank[:, P:4 * P], ACT.Copy).then_inc(taken, 1)
                    else:
                        act.activation(ffn_out[:, 4:6, :].rearrange("p a c -> p (a c)"),
                                       bank[:, 0:2 * P], ACT.Copy)
                        act.activation(ffn_out[0:64, 6, :], bank[0:64, 2 * P:3 * P],
                                       ACT.Copy).then_inc(taken, 1)

                act.preload_act_table(ACT.Sqrt)
                for m in range(KD):
                    if m == 0:
                        take_unit(0)
                    if m < KD - 2:
                        split_hi(qd + m // 2 + 1, m % 2, NG)
                    act.wait_ge(drained[m % 2], qd + m // 2 + 1)
                    act.wait_ge(summed, SUMMED[3] + m)
                    act.activation(sq[:, :], tile(f, m), ACT.Square).then_inc(squared, 1)
                    act.wait_ge(squared, 2 * KD + m + 1)
                    act.activation(tile(f, m), tile(f, m), ACT.Copy,
                                   scale=col(V_FFN_POST + m)).then_inc(f_gained, 1)
                    for n, u in enumerate(UNITS):
                        if u[0] == m + 1 and m + 1 < KD:
                            take_unit(n)

            up_step(0, 0, 0, early=True)
            split_hi(C_FFN // 2 + EARLY, 1)
            up_step(0, 1, 1, early=True)
            up_steps(0, EARLY)
            group(0, False)
            with act.Fori(1, GROUPS - 1) as g:
                up_steps(g)
                group(g, False)
            up_steps(GROUPS - 1)
            group(GROUPS - 1, True)
            root(4)
            act.wait_ge(y_factors, 1)
            for k4, i in Y_POOL:
                nt = TT[i][1]
                act.activation(f_tok[3 * k4 + i][0:nt, :], f_tok[3 * k4 + i][0:nt, :], ACT.Copy,
                               scale=cols[0:nt, 2, i:i + 1]).then_inc(y_scaled, 1)

        @block.vector
        def _(dve):
            def split_lo(q, e, blocks=KD):
                off = (q % 2) * (2 * KD * P) + e * KD * P
                half = blocks * P // 2
                for h in range(2):
                    dve.wait_ge(w_hi_done, 4 * q + 2 * e + h + 1)
                    o = off + h * half
                    src = raw[:, o:o + half] if type(q) is int else raw[:, bass.ds(o, half)]
                    d = slice(e * KD * P + h * half, e * KD * P + (h + 1) * half)
                    dve.tensor_tensor(w_lo[:, d], src, w_hi[:, d].bitcast(F32),
                                      ALU.subtract).then_inc(w_lo_done, 1)

            steps = [0]

            def step(ins):
                steps[0] += 1
                ins.then_inc(dstep, 1)
                dve.wait_ge(dstep, steps[0])

            def stats(n, width):
                v, root, r, t = (cols[:, x, 0:3] for x in range(4))
                dve.wait_ge(total, n + 1)
                dve.tensor_scalar(v, tb[5][:, 0:3], 1.0 / width, EPS, ALU.mult, ALU.add).then_inc(meaned, 1)
                dve.wait_ge(rooted, n + 1)
                step(dve.reciprocal(r, root))
                step(dve.scalar_tensor_tensor(out=t, in0=r, scalar=-0.5, in1=r, op0=ALU.mult, op1=ALU.mult))
                step(dve.tensor_tensor(t, t, v, ALU.mult))
                last = dve.scalar_tensor_tensor(out=r, in0=t, scalar=1.5, in1=r, op0=ALU.add, op1=ALU.mult)
                if n == 4:
                    last.then_inc(y_factors, 1)
                    dve.wait_ge(y_factors, 1)
                else:
                    step(last)
                if n < 4:
                    dve.tensor_tensor(diag[:, :, :],
                                      ident[:, :].rearrange("p (a c) -> p a c", a=1).to_broadcast([P, 3, P]),
                                      r.rearrange("p (a c) -> p a c", c=1).to_broadcast([P, 3, P]),
                                      ALU.mult).then_inc(diag_done, 1)

            dve.wait_ge(consts, 1)
            dve.tensor_copy(sel[:, :].rearrange("s (b t) -> s b t", b=NB),
                            ident[0:TB, 0:TB].rearrange("s (a t) -> s a t", a=1).to_broadcast([TB, NB, TB])
                            ).then_inc(sel_done, 1)
            dve.wait_ge(vecs_t, 1)
            dve.tensor_copy(vec[:, 0:KD], tb[0][:, 0:KD]).then_inc(vecs_done, 1)
            split_lo(0, 0)

            def copy_x(k4):
                for u in x_units(k4, 1):
                    dve.wait_ge(x_turned, u + 1)
                    dve.tensor_copy(*x_unit(u)).then_inc(x_copied[1], 1)

            copy_x(0)
            dve.wait_ge(vecs_done, 1)
            for k in range(KD):
                if k % 4 == 1:
                    copy_x(k // 4 + 1)
                if k % 4 == 0:
                    wait_x(dve, k // 4)
                dve.wait_ge(a_hi_done, k + 1)
                dve.scalar_tensor_tensor(out=tile(a_lo, k), in0=tile(xT, k), scalar=col(V_MIX_PRE + k),
                                         in1=tile(a_hi, k).bitcast(F32), op0=ALU.mult,
                                         op1=ALU.subtract).then_inc(a_lo_done, 1)
            split_lo(0, 1)
            dve.wait_ge(hists_t, 1)
            dve.tensor_copy(vec[:, KD:268], tb[0][:, KD:268])
            dve.tensor_copy(pool_hist[:, :, :, :].rearrange("p g b r -> p (g b r)"), tb[1][:, 0:480])
            dve.tensor_copy(conv_hist[:, :], tb[2][:, 0:96])
            dve.tensor_copy(ws[:, 0:4, :].rearrange("p j q -> p (j q)"), tb[3][:, :])
            dve.tensor_copy(ws[:, 4:6, :].rearrange("p j q -> p (j q)"), tb[4][:, 0:256])
            dve.tensor_copy(ffn_hist[:, 0:512], tb[5][:, :])
            dve.tensor_copy(ffn_hist[:, 512:704], tb[4][:, 256:448]).then_inc(hists_done, 1)
            for e in range(2):
                split_lo(1, e)
            with dve.Fori(1, NSGU // 2) as q:
                for e in range(2):
                    split_lo(q + 1, e)
            stats(0, D)
            dve.wait_ge(corner_mm, 1)
            dve.tensor_copy(bd[:, :, :, :],
                            tb[0][0:TS, 0:NSGU * TB].rearrange("s (j a q) -> s j a q", j=NSGU, a=1)
                            .to_broadcast([TS, NSGU, NB, TB])).then_inc(corner_done, 1)
            dve.wait_ge(r_done, 1)

            with dve.Fori(C_V // 2, C_POOL // 2) as q:
                for e in range(2):
                    dve.wait_ge(used, 2 * q + e + 1)
                    dve.tensor_tensor(tile(vT, 2 * q + e), mm[e][:, 0:T], r_x[:, :],
                                      ALU.mult).then_inc(drained[e], 1)
                    split_lo(q + 1, e)

            def fill_zz(g, c, e):
                dve.wait_ge(used, c + 1)
                if g:
                    dve.wait_ge(zz_free, g)
                dve.tensor_copy(samples(zz, LP, WP, 0, PH), pool_hist[:, g, :, :])
                dve.tensor_tensor(zz[:, PH:LP], mp[e], r_x[:, 0:SEQ], ALU.mult)
                dve.tensor_tensor(samples(zz, LP, WP, PH, WP), ms[e],
                                  r_x[:, SEQ:T].rearrange("p (b t) -> p b t", b=NB),
                                  ALU.mult).then_inc(drained[e], 1)
                dve.wait_ge(drained[e], c // 2 + 1)

            def pool_windows(g):
                w = WINDOWS[g]
                src, d, n = zz, 1, 0
                while d < w:
                    dst = win[n % 2]
                    o = 2 * d - 1
                    step(dve.tensor_tensor(dst[:, o:ZP], src[:, o:ZP], src[:, o - d:ZP - d], ALU.add))
                    src, d, n = dst, 2 * d, n + 1
                if g:
                    dve.wait_ge(pool_mm, g)
                dve.scalar_tensor_tensor(out=pooled[:, 0:SEQ], in0=src[:, PH:LP], scalar=1.0 / w,
                                         in1=zz[:, PH:LP], op0=ALU.mult, op1=ALU.subtract)
                step(dve.scalar_tensor_tensor(
                    out=pooled[:, SEQ:T].rearrange("p (b t) -> p b t", b=NB),
                    in0=samples(src, LP, WP, PH, WP), scalar=1.0 / w,
                    in1=samples(zz, LP, WP, PH, WP), op0=ALU.mult, op1=ALU.subtract))
                step(dve.tensor_tensor(pooled[:, 0:16], src[:, PH:PH + 16], icnt[:, g, :], ALU.mult))
                dve.tensor_tensor(pooled[:, 0:16], pooled[:, 0:16], zz[:, PH:PH + 16],
                                  ALU.subtract).then_inc(pooled_done, 1)
                dve.wait_ge(pooled_done, g + 1)

            def pool_lo(g):
                dve.wait_ge(m_hi_done, READY.index(g) + 1)
                dve.scalar_tensor_tensor(out=tile(m_lo, g), in0=tb[4][:, 0:T], scalar=col(V_POOL + g),
                                         in1=tile(m_hi, g).bitcast(F32), op0=ALU.mult,
                                         op1=ALU.subtract).then_inc(m_lo_done, 1)

            def gate(j):
                dve.wait_ge(sgu_mm, j + 1)
                out = tb[2 + j % 2]
                v0 = (NSGU + j) * T
                bias = sgu_bias[:, j:j + 1, :]
                dve.tensor_tensor(f[:, v0:v0 + SEQ].rearrange("p (n q) -> p n q", n=2),
                                  out[:, 0:SEQ].rearrange("p (n q) -> p n q", n=2),
                                  bias.to_broadcast([P, 2, P]), ALU.add)
                step(dve.tensor_tensor(f[:, v0 + SEQ:v0 + T].rearrange("p (b q) -> p b q", b=NB),
                                       out[:, SEQ:T].rearrange("p (b q) -> p b q", b=NB),
                                       bias[:, :, 0:TB].to_broadcast([P, NB, TB]), ALU.add))
                dve.wait_ge(u_scaled, j + 1)
                dve.tensor_tensor(tile(f, NSGU + j), tile(f, NSGU + j), tile(uT, j),
                                  ALU.mult).then_inc(mix_ready, 1)

            def gate_lo(j):
                dve.wait_ge(m_hi_done, READY.index(M_SGU + j) + 1)
                dve.tensor_tensor(tile(m_lo, M_SGU + j), tile(f, NSGU + j),
                                  tile(m_hi, M_SGU + j).bitcast(F32), ALU.subtract).then_inc(m_lo_done, 1)

            q0 = C_POOL // 2
            stats(1, NSGU * P)
            dve.wait_ge(pads_done, 1)
            dve.wait_ge(hists_done, 1)
            fill_zz(0, C_POOL, 0)
            split_lo(q0 + 1, 0)
            dve.wait_ge(r_done, 2)
            for j in range(NSGU):
                dve.scalar_tensor_tensor(out=tile(vT, NSGU + j), in0=tile(vT, NSGU + j),
                                         scalar=col(V_SGU + j), in1=r_v[:, :], op0=ALU.mult,
                                         op1=ALU.mult).then_inc(v_normed, 1)
            pool_windows(0)
            for g in range(1, NPOOL):
                fill_zz(g, C_POOL + g, g % 2)
                split_lo(q0 + 1 + g // 2, g % 2)
                pool_windows(g)
                pool_lo(g - 1)
                for part in (gate, gate_lo):
                    part(2 * g - 2)
                    part(2 * g - 1)
            split_lo(q0 + 3, 0)
            pool_lo(3)

            dve.wait_ge(zz_free, NPOOL)
            dve.memset(zc[:, 0:CH], 0.0).then_inc(zc_free, 1)
            head_base, PER_HEAD = steps[0], 4
            with dve.Fori(0, NCONV // 2) as i:
                q = C_CONV // 2 + 3 * i
                for h2 in range(2):
                    j = 2 * i + h2
                    made = [head_base + PER_HEAD * h2]

                    def head_step(ins):
                        made[0] += 1
                        ins.then_inc(dstep, 1)
                        dve.wait_ge(dstep, made[0] + 2 * PER_HEAD * i)

                    n = 3 * h2
                    e = n % 2
                    dve.wait_ge(used, 2 * q + n + 1)
                    dve.tensor_tensor(hs[:, :], mm[e][:, 0:T], r_x[:, :], ALU.mult).then_inc(drained[e], 1)
                    dve.wait_ge(drained[e], q + n // 2 + 1)
                    head_step(dve.tensor_tensor(hs[:, :], hs[:, :], r_x[:, :], ALU.mult))
                    split_lo(q + (n + 3) // 2, 1 - e)
                    n = 3 * h2 + 1
                    e = n % 2
                    dve.wait_ge(used, 2 * q + n + 1)
                    dve.wait_ge(zc_free, j + 1)
                    dve.tensor_copy(samples(zc, LC, WC, 0, CH),
                                    conv_hist[:, bass.ds(j * (NB * CH), NB * CH)]
                                    .rearrange("p (b r) -> p b r", b=NB))
                    dve.tensor_tensor(zc[:, CH:LC], mp[e], hs[:, 0:SEQ], ALU.mult)
                    dve.tensor_tensor(samples(zc, LC, WC, CH, WC), ms[e],
                                      hs[:, SEQ:T].rearrange("p (b t) -> p b t", b=NB),
                                      ALU.mult).then_inc(drained[e], 1)
                    dve.wait_ge(drained[e], q + n // 2 + 1)
                    head_step(dve.tensor_scalar(yc[:, 0:YC], zc[:, 0:YC], col(V_CONV + j), None, ALU.mult))
                    for t in range(1, 3):
                        head_step(dve.scalar_tensor_tensor(out=yc[:, 0:YC], in0=zc[:, t:t + YC],
                                                           scalar=col(V_CONV + t * NCONV + j),
                                                           in1=yc[:, 0:YC], op0=ALU.mult, op1=ALU.add))
                    split_lo(q + (n + 3) // 2, 1 - e)
                    n = 3 * h2 + 2
                    e = n % 2
                    dve.wait_ge(used, 2 * q + n + 1)
                    dve.tensor_tensor(hs[:, :], mm[e][:, 0:T], r_x[:, :], ALU.mult).then_inc(drained[e], 1)
                    dve.wait_ge(drained[e], q + n // 2 + 1)
                    dve.tensor_tensor(hs[:, 0:SEQ], hs[:, 0:SEQ], yc[:, 0:SEQ], ALU.mult)
                    hv = hs[:, SEQ:T].rearrange("p (b t) -> p b t", b=NB)
                    dve.tensor_tensor(hv, hv, samples(yc, LC, WC, 0, TB), ALU.mult).then_inc(mix_ready, 1)
                    dve.wait_ge(m_hi_done, NPOOL + NSGU + j + 1)
                    dve.wait_ge(v_stored, 16)
                    dve.tensor_tensor(tile(m_lo, M_CONV + j), hs[:, :],
                                      tile(m_hi, M_CONV + j).bitcast(F32),
                                      ALU.subtract).then_inc(m_lo_done, 1)
                    dve.wait_ge(m_lo_done, NPOOL + NSGU + j + 1)
                    split_lo(q + (n + 3) // 2, 1 - e)
            steps[0] += PER_HEAD * NCONV

            dve.wait_ge(spread, 2)
            step(dve.memset(acc[:, :], 0.0))

            def add_out_square(m):
                dve.wait_ge(squared, m + 1)
                dve.wait_ge(summed, SUMMED[1] + m)
                dve.tensor_tensor(acc[:, :], acc[:, :], sq[:, :], ALU.add).then_inc(summed, 1)

            add_out_square(0)
            add_out_square(1)
            split_lo(C_OUT // 2 + 1, 1)
            with dve.Fori(1, KD // 2 - 1) as i:
                for e in range(2):
                    add_out_square(2 * i + e)
                    split_lo(C_OUT // 2 + i + 1, e)
            add_out_square(KD - 2)
            split_lo(C_FFN // 2, 0)
            stats(2, D)
            split_lo(C_FFN // 2, 1)
            dve.memset(zf[:, 0:CH], 0.0).then_inc(zf_free, 1)

            dve.wait_ge(spread, 3)
            dve.wait_ge(drained[0], C_FFN // 2)
            dve.wait_ge(drained[1], C_FFN // 2)

            def scale_out(k):
                dve.tensor_tensor(tile(f, k), tile(f, k), tb[5][:, 64:64 + T],
                                  ALU.mult).then_inc(f_scaled, 1)

            def x1_lo(k):
                dve.wait_ge(a_hi_done, KD + k + 1)
                dve.scalar_tensor_tensor(out=tile(a_lo, k), in0=tile(xT, k), scalar=col(V_FFN_PRE + k),
                                         in1=tile(a_hi, k).bitcast(F32), op0=ALU.mult,
                                         op1=ALU.subtract).then_inc(a_lo_done, 1)

            AHEAD = 3
            for k in range(KD + AHEAD):
                if k < KD:
                    scale_out(k)
                if k >= AHEAD:
                    x1_lo(k - AHEAD)

            def sum_squares(dst, k0, n):
                dve.wait_ge(squared, KD + k0 + n)
                return dve.tensor_reduce(dst[:, :], tile(f, k0, n).rearrange("p (k t) -> p t k", k=n),
                                         mybir.AxisListType.X, ALU.add)

            q0 = C_FFN // 2
            dve.wait_ge(spread, 3)
            step(sum_squares(acc, 0, MERGED[0]))
            split_lo(q0 + 1, 0)
            dve.wait_ge(merged, 1)
            step(sum_squares(sq, MERGED[1], KD - MERGED[1]))
            dve.tensor_tensor(acc[:, :], acc[:, :], sq[:, :], ALU.add).then_inc(summed, 1)
            split_lo(q0 + 1, 1)
            stats(3, D)
            dve.wait_ge(r_done, 3)

            block_base, PER_BLOCK = steps[0], 2

            def up_step(g, i, n, early=False, blocks=KD):
                q = C_FFN // 2 + g * (PER_GROUP // 2) + i
                gate_mm, val_mm = tb[2 * i:2 * i + 2] if early else mm
                dve.wait_ge(used, 2 * q + 1)
                dve.wait_ge(zf_free, n + 1)
                dve.tensor_copy(samples(zf, LC, WC, 0, CH),
                                ffn_hist[:, bass.ds(n * (NB * CH), NB * CH)]
                                .rearrange("p (b r) -> p b r", b=NB))
                dve.tensor_tensor(zf[:, CH:LC], gate_mm[:, 0:SEQ], r_v[:, 0:SEQ], ALU.mult)
                dve.tensor_tensor(samples(zf, LC, WC, CH, WC),
                                  gate_mm[:, SEQ:T].rearrange("p (b t) -> p b t", b=NB),
                                  r_v[:, SEQ:T].rearrange("p (b t) -> p b t", b=NB),
                                  ALU.mult).then_inc(drained[0], 1)
                dve.wait_ge(drained[0], q + 1)
                dve.tensor_scalar(yf[:, 0:YC], zf[:, 0:YC], col(V_FCONV + n), None,
                                  ALU.mult).then_inc(dstep, 1)
                dve.wait_ge(dstep, block_base + PER_BLOCK * n + 1)
                dve.scalar_tensor_tensor(out=yf[:, 0:YC], in0=zf[:, 1:1 + YC], scalar=col(V_FCONV + NF + n),
                                         in1=yf[:, 0:YC], op0=ALU.mult, op1=ALU.add).then_inc(dstep, 1)
                dve.wait_ge(dstep, block_base + PER_BLOCK * n + 2)
                dve.scalar_tensor_tensor(out=yf[:, 0:YC], in0=zf[:, 2:2 + YC],
                                         scalar=col(V_FCONV + 2 * NF + n), in1=yf[:, 0:YC],
                                         op0=ALU.mult, op1=ALU.add).then_inc(conv_done, 1)
                split_lo(C_FFN // 2 + EARLY, i) if early else split_lo(q + 1, 0, blocks)
                dve.wait_ge(used, 2 * q + 2)
                dve.tensor_tensor(val[:, :], val_mm[:, 0:T], r_v[:, :], ALU.mult).then_inc(drained[1], 1)
                dve.wait_ge(drained[1], q + 1)
                dve.wait_ge(gelu_done, n + 1)
                dve.tensor_tensor(val[:, :], val[:, :], gel[:, :], ALU.mult).then_inc(h_ready, 1)
                dve.wait_ge(h_hi_done, n + 1)
                dve.tensor_tensor(tile(m_lo, i), val[:, :], tile(m_hi, i).bitcast(F32),
                                  ALU.subtract).then_inc(h_lo_done, 1)
                dve.wait_ge(h_lo_done, n + 1)
                if not early:
                    split_lo(q + 1, 1, blocks)

            def add_down(q, e, m):
                dve.wait_ge(used, 2 * q + e + 1)
                dve.tensor_tensor(tile(f, m), mm[e][:, 0:T], tile(f, m), ALU.add).then_inc(drained[e], 1)

            def up_steps(g, i0=0):
                with dve.Fori(i0, NG - 1) as i:
                    up_step(g, i, g * NG + i)
                up_step(g, NG - 1, g * NG + NG - 1, blocks=NG)

            def group(g, last):
                dve.wait_ge(f_zeroed, 1)
                qd = C_FFN // 2 + g * (PER_GROUP // 2) + NG
                if not last:
                    with dve.Fori(0, KD // 2 - 1) as i:
                        for e in range(2):
                            add_down(qd + i, e, 2 * i + e)
                            split_lo(qd + i + 1, e, NG)
                    for e in range(2):
                        add_down(qd + KD // 2 - 1, e, KD - 2 + e)
                        split_lo(qd + KD // 2, e)
                    return

                def add_square(m):
                    dve.wait_ge(squared, 2 * KD + m + 1)
                    dve.wait_ge(summed, SUMMED[3] + m)
                    dve.tensor_tensor(acc[:, :], acc[:, :], sq[:, :], ALU.add).then_inc(summed, 1)

                dve.wait_ge(spread, 4)
                step(dve.memset(acc[:, :], 0.0))
                for m in range(KD):
                    add_down(qd + m // 2, m % 2, m)
                    if m:
                        add_square(m - 1)
                    if m < KD - 2:
                        split_lo(qd + m // 2 + 1, m % 2, NG)

            for i in range(EARLY):
                up_step(0, i, i, early=True)
            up_steps(0, EARLY)
            group(0, 0)
            with dve.Fori(1, GROUPS - 1) as g:
                up_steps(g)
                group(g, 0)
            up_steps(GROUPS - 1)
            steps[0] += PER_BLOCK * NF
            group(GROUPS - 1, 1)

            stats(4, D)
            n_taken = sum(u[0] < KD for u in UNITS)
            dve.wait_ge(taken, n_taken)
            for k4, i in Y_ORDER:
                nt = TT[i][1]
                if k4 == QD - 1:
                    dve.wait_ge(turned, n_taken + i + 1)
                piece = y_tok[0:nt, i, k4 * 512:(k4 + 1) * 512]
                down = f_tok[3 * k4 + i] if k4 < QD - 1 else tb[(n_taken + i) % 5]
                dve.scalar_tensor_tensor(out=piece, in0=down[0:nt, :], scalar=cols[0:nt, 2, i:i + 1],
                                         in1=piece, op0=ALU.mult, op1=ALU.add).then_inc(y_done, 1)

        @block.gpsimd
        def _(pool):
            own = sem("own")
            steps = [0]

            def step(ins):
                steps[0] += 1
                ins.then_inc(own, 1)
                pool.wait_ge(own, steps[0])

            pool.dma_start(new_pool_sample[0, :, 0:PH - TB, :],
                           state_pool[0, :, TB:PH, :]).then_inc(hist_stored, 16)
            step(pool.memset(ident[:, :], 0.0))
            pool.memset(ones[:, :], 1.0)
            pool.affine_select(out=ident[:, :], in_=ident[:, :], compare_op=ALU.not_equal, fill=1.0,
                               base=0, pattern=[[-1, P]], channel_multiplier=1).then_inc(consts, 1)
            for g, w in enumerate(WINDOWS):
                pool.memset(icnt[:, g, w - 1:16], 1.0 / w)
                for t in range(w - 1):
                    pool.memset(icnt[:, g, t:t + 1], 1.0 / (t + 1))

            def add_square(src, first, last):
                dst = acc if first else sq
                ins = pool.tensor_tensor(dst[:, :], src, src, ALU.mult)
                step(ins)
                if not first:
                    ins = pool.tensor_tensor(acc[:, :], acc[:, :], sq[:, :], ALU.add)
                    if last:
                        ins.then_inc(summed, 1)
                    else:
                        step(ins)

            for k in range(KD):
                if k % 4 == 0:
                    wait_x(pool, k // 4)
                if k == KD // 2:
                    pool.wait_ge(hists_done, 1)
                    pool.affine_select(out=ws[:, :, :], in_=ws[:, :, :], compare_op=ALU.is_ge, fill=0.0,
                                       base=0, pattern=[[0, NSGU], [1, P]],
                                       channel_multiplier=-1).then_inc(tril_done, 1)
                add_square(tile(xT, k), k == 0, k == KD - 1)

            pool.wait_ge(x_turned, X_UNITS)
            pool.memset(zz[:, 0:PH], 0.0).then_inc(pads_done, 1)

            pool.wait_ge(corner_done, 1)
            step(pool.affine_select(out=bd[:, :, :, :], in_=bd[:, :, :, :], compare_op=ALU.is_ge, fill=0.0,
                                    base=0, pattern=[[0, NSGU], [-TB, NB], [0, TB]], channel_multiplier=1))
            pool.affine_select(out=bd[:, :, :, :], in_=bd[:, :, :, :], compare_op=ALU.is_ge, fill=0.0,
                               base=TB - 1, pattern=[[0, NSGU], [TB, NB], [0, TB]],
                               channel_multiplier=-1).then_inc(bd_done, 1)

            pool.wait_ge(r_done, 1)
            pool.wait_ge(drained[1], NSGU // 2)
            for j in range(NSGU):
                pool.tensor_tensor(tile(uT, j), tile(uT, j), r_x[:, :], ALU.mult).then_inc(u_scaled, 1)

            pool.wait_ge(spread, 1)
            for j in range(NSGU):
                c = C_V + j
                pool.wait_ge(drained[c % 2], c // 2 + 1)
                add_square(tile(vT, NSGU + j), j == 0, j == NSGU - 1)

            for g in range(NPOOL):
                c = C_POOL + g
                pool.wait_ge(drained[c % 2], c // 2 + 1)
                pool.tensor_copy(pool_tail_p[:, g * PH:(g + 1) * PH], zz[:, LP - PH:LP])
                pool.tensor_copy(pool_tail_s[:, g * TS:(g + 1) * TS].rearrange("p (b t) -> p b t", b=NB),
                                 samples(zz, LP, WP, PH, WP)).then_inc(zz_free, 1)
            pool.wait_ge(v_tok_done, NSGU)
            pool.dma_start(new_chunk_v[0].rearrange("b t c -> (b t) c"), vs_tok[:, :]).then_inc(v_stored, 16)

            with pool.Fori(0, NCONV // 2) as i:
                for h2 in range(2):
                    c = 3 * h2 + 1
                    j = 2 * i + h2
                    pool.wait_ge(drained[c % 2], C_CONV // 2 + 3 * i + c // 2 + 1)
                    pool.tensor_copy(conv_tail_p[:, bass.ds(j * CH, CH)], zc[:, LC - CH:LC])
                    pool.tensor_copy(conv_tail_s[:, bass.ds(j * (NB * CH), NB * CH)]
                                     .rearrange("p (b r) -> p b r", b=NB),
                                     samples(zc, LC, WC, WC - CH, WC)).then_inc(zc_free, 1)

            for k in range(KD):
                pool.wait_ge(f_scaled, k + 1)
                pool.tensor_tensor(tile(xT, k), tile(xT, k), tile(f, k), ALU.add).then_inc(x1_done, 1)
            pool.wait_ge(squared, KD + MERGED[1] + 1)
            total_block = tile(f, MERGED[1])
            for k in range(*MERGED):
                ins = pool.tensor_tensor(total_block, total_block, tile(f, k), ALU.add)
                if k < MERGED[1] - 1:
                    step(ins)
            ins.then_inc(merged, 1)
            pool.wait_ge(summed, SUMMED[3])
            pool.memset(f[:, :], 0.0).then_inc(f_zeroed, 1)

            def save_zf(g, i, n):
                pool.wait_ge(drained[0], C_FFN // 2 + g * (PER_GROUP // 2) + i + 1)
                pool.tensor_copy(ffn_tail_p[:, bass.ds(n * CH, CH)], zf[:, LC - CH:LC])
                pool.tensor_copy(ffn_tail_s[:, bass.ds(n * (NB * CH), NB * CH)]
                                 .rearrange("p (b r) -> p b r", b=NB),
                                 samples(zf, LC, WC, WC - CH, WC)).then_inc(zf_free, 1)

            with pool.Fori(0, GROUPS) as g:
                with pool.Fori(0, NG) as i:
                    save_zf(g, i, g * NG + i)

            pool.wait_ge(taken, sum(u[0] < KD for u in UNITS))
            for n, (k4, i) in enumerate(Y_POOL):
                nt = TT[i][1]
                piece = y_tok[0:nt, i, k4 * 512:(k4 + 1) * 512]
                pool.wait_ge(y_scaled, n + 1)
                pool.tensor_tensor(piece, piece, f_tok[3 * k4 + i][0:nt, :], ALU.add).then_inc(y_pool_done, 1)
            pool.wait_ge(hist_stored, 16)


_INS = ['x_prompt', 'x_sample', 'state_pool', 'state_conv', 'state_ffn', 'g_mix_pre', 'g_mix_post',
        'g_ffn_pre', 'g_ffn_post', 'w_in', 'pool_w', 'pool_scale', 'conv_w', 'sgu_norm', 'sgu_w',
        'sgu_b', 'w_out', 'ffn_up', 'ffn_conv_w', 'ffn_conv_b', 'ffn_down']


def kernel(**inputs):
    import numpy as _np
    import concourse.bacc as _bacc
    from concourse import mybir as _mybir
    from concourse.bass_utils import run_bass_kernel_spmd as _run

    nc = _bacc.Bacc("TRN2", target_bir_lowering=False, num_devices=1)
    arrays, args = {}, []
    for name in _INS:
        a = _np.ascontiguousarray(inputs[name])
        arrays[f"in_{name}_dram"] = a
        args.append(nc.dram_tensor(f"in_{name}_dram", a.shape, _mybir.dt.from_np(a.dtype),
                                   kind="ExternalInput").ap())
    n, b, t = (1,) + inputs["x_sample"].shape[:2]
    outs = [inputs["x_prompt"].shape, inputs["x_sample"].shape]
    for name in ("state_pool", "state_conv", "state_ffn"):
        s = inputs[name].shape
        outs += [(s[0], inputs["x_prompt"].shape[0]) + tuple(s[2:]), s]
    outs.append((inputs["sgu_norm"].shape[0], b, t, inputs["sgu_norm"].shape[1]))
    for i, shape in enumerate(outs):
        args.append(nc.dram_tensor(f"out_{i}_dram", tuple(shape), _mybir.dt.float32,
                                   kind="ExternalOutput").ap())
    hybrid_layer(nc, *args)
    r = _run(nc, [arrays], core_ids=[0])
    return tuple(r.results[0][f"out_{i}_dram"] for i in range(len(outs)))
```
